# Optimizing a Trainium2 kernel written in Bass

```python
import math
import jax, jax.numpy as jnp
from jax import lax
import numpy as np

D_MODEL = 1024
BATCH = 1
SEQ = 1024
DEPTH = 1
DEC_BATCH = 8
DEC_SEQ = 8
PAST_LEN = 256
PAGE_SIZE = 128

H_DIFF = 4
HD_DIFF = 64
W_DIFF = H_DIFF * 2 * HD_DIFF
H_SB = 8
HD_SB = 64
W_SB = H_SB * HD_SB
N_BUCKETS = 32
MAX_DISTANCE = 128
Q_BLOCK = 128
PEER_HEADS = 8
PEER_KEYS = 128
PEER_TOPK = 16
PEER_KD = 128
N_EXPERTS = PEER_KEYS * PEER_KEYS
PEER_BLOCK = 256
EPS = 1e-6

IN_WIDTHS = (W_DIFF, W_DIFF, W_DIFF, W_SB, W_SB, W_SB, D_MODEL, D_MODEL)
W_IN = sum(IN_WIDTHS)
SPLIT_POINTS = tuple(sum(IN_WIDTHS[:i + 1]) for i in range(len(IN_WIDTHS) - 1))

kernel_name = "hybrid_diffattn_stickbreak_peer_step"

def rms_norm(x, g):
    xf = x.astype(jnp.float32)
    y = xf * lax.rsqrt(jnp.mean(xf * xf, axis=-1, keepdims=True) + EPS)
    return (y * g.astype(jnp.float32)).astype(x.dtype)

def t5_bias(rel, table):
    n = jnp.maximum(rel, 0)
    max_exact = N_BUCKETS // 2
    log_ratio = jnp.log(jnp.maximum(n, 1).astype(jnp.float32) / max_exact) / math.log(MAX_DISTANCE / max_exact)
    large = jnp.minimum(max_exact + (log_ratio * (N_BUCKETS - max_exact)).astype(jnp.int32), N_BUCKETS - 1)
    bucket = jnp.where(n < max_exact, n, large)
    return jnp.transpose(table[bucket].astype(jnp.float32), (2, 0, 1))

def diff_attention(q, k, v, bias, mask, lam):
    scale = HD_DIFF ** -0.5

    def probs(qi, ki):
        s = jnp.einsum('bqhd,bkhd->bhqk', qi, ki).astype(jnp.float32) * scale + bias
        return jax.nn.softmax(jnp.where(mask, s, -jnp.inf), axis=-1)

    p = probs(q[..., :HD_DIFF], k[..., :HD_DIFF]) - lam * probs(q[..., HD_DIFF:], k[..., HD_DIFF:])
    return jnp.einsum('bhqk,bkhe->bqhe', p.astype(v.dtype), v)

def stick_breaking_attention(q, k, v, mask):
    z = jnp.einsum('bqhd,bkhd->bhqk', q, k).astype(jnp.float32) * (HD_SB ** -0.5)
    log_beta = jax.nn.log_sigmoid(z)
    log_1m = jnp.where(mask, jax.nn.log_sigmoid(-z), 0.0)
    shifted = jnp.pad(log_1m[..., 1:], ((0, 0), (0, 0), (0, 0), (0, 1)))
    tail = lax.cumsum(shifted, axis=3, reverse=True)
    a = jnp.where(mask, jnp.exp(log_beta + tail), 0.0)
    return jnp.einsum('bhqk,bkhd->bqhd', a.astype(v.dtype), v)

def project_mixer_inputs(xn, w_in_l):
    b, t = xn.shape[:2]
    qa, ka, va, qb, kb, vb, ga, gb = jnp.split(xn @ w_in_l, SPLIT_POINTS, axis=-1)
    qa = qa.reshape(b, t, H_DIFF, 2 * HD_DIFF)
    ka = ka.reshape(b, t, H_DIFF, 2 * HD_DIFF)
    va = va.reshape(b, t, H_DIFF, 2 * HD_DIFF)
    qb = qb.reshape(b, t, H_SB, HD_SB)
    kb = kb.reshape(b, t, H_SB, HD_SB)
    vb = vb.reshape(b, t, H_SB, HD_SB)
    return qa, ka, va, qb, kb, vb, ga, gb

def prompt_attention(qa, ka, va, qb, kb, vb, rel_bias, lam):
    b, s = qa.shape[:2]
    n_blk = s // Q_BLOCK
    k_pos = jnp.arange(s, dtype=jnp.int32)

    def to_blocks(t):
        return jnp.swapaxes(t.reshape(b, n_blk, Q_BLOCK, *t.shape[2:]), 0, 1)

    def from_blocks(t):
        return jnp.swapaxes(t, 0, 1).reshape(b, s, *t.shape[3:])

    def block(args):
        qa_blk, qb_blk, start = args
        q_pos = start + jnp.arange(Q_BLOCK, dtype=jnp.int32)
        rel = q_pos[:, None] - k_pos[None, :]
        o_a = diff_attention(qa_blk, ka, va, t5_bias(rel, rel_bias), rel >= 0, lam)
        o_b = stick_breaking_attention(qb_blk, kb, vb, rel > 0)
        return o_a, o_b

    starts = jnp.arange(n_blk, dtype=jnp.int32) * Q_BLOCK
    o_a, o_b = lax.map(block, (to_blocks(qa), to_blocks(qb), starts))
    return from_blocks(o_a), from_blocks(o_b)

def sample_attention(qa, ka, va, qb, kb, vb, ck_a, cv_a, ck_b, cv_b, page_table, rel_bias, lam):
    db, t = qa.shape[:2]
    past = page_table.shape[1] * ck_a.shape[1]

    def gather(pool, new):
        rows = pool[page_table].reshape(db, past, *pool.shape[2:])
        return jnp.concatenate([rows.astype(new.dtype), new], axis=1)

    q_pos = past + jnp.arange(t, dtype=jnp.int32)
    k_pos = jnp.arange(past + t, dtype=jnp.int32)
    rel = q_pos[:, None] - k_pos[None, :]
    o_a = diff_attention(qa, gather(ck_a, ka), gather(cv_a, va), t5_bias(rel, rel_bias), rel >= 0, lam)
    o_b = stick_breaking_attention(qb, gather(ck_b, kb), gather(cv_b, vb), rel > 0)
    return o_a, o_b

def merge_branches(o_a, o_b, ga, gb, subln_g, lam_init, w_pa, w_pb, w_o):
    b, t = o_a.shape[:2]
    o_a = rms_norm(o_a, subln_g) * (1.0 - lam_init)
    y_a = o_a.reshape(b, t, W_DIFF) @ w_pa
    y_b = o_b.reshape(b, t, W_SB) @ w_pb
    return (jax.nn.sigmoid(ga) * y_a + jax.nn.sigmoid(gb) * y_b) @ w_o

def peer_ffn(xn, w_q, sub_keys, u_tab, v_tab):
    lead = xn.shape[:-1]
    xt = xn.reshape(-1, D_MODEL)
    n_tok = xt.shape[0]
    xt = jnp.pad(xt, ((0, (-n_tok) % PEER_BLOCK), (0, 0)))

    def block(xb):
        q = (xb @ w_q).reshape(-1, PEER_HEADS, 2, PEER_KD // 2)
        s = jnp.einsum('thcd,hcnd->thcn', q, sub_keys).astype(jnp.float32)
        top_s, top_i = lax.top_k(s, PEER_TOPK)
        cand_s = top_s[:, :, 0, :, None] + top_s[:, :, 1, None, :]
        cand_i = top_i[:, :, 0, :, None] * PEER_KEYS + top_i[:, :, 1, None, :]
        best_s, best_j = lax.top_k(cand_s.reshape(*cand_s.shape[:2], -1), PEER_TOPK)
        idx = jnp.take_along_axis(cand_i.reshape(*cand_i.shape[:2], -1), best_j, axis=-1)
        g = jax.nn.softmax(best_s, axis=-1)
        act = jax.nn.gelu(jnp.einsum('td,thkd->thk', xb, u_tab[idx]).astype(jnp.float32), approximate=False)
        return jnp.einsum('thk,thkd->td', (g * act).astype(xb.dtype), v_tab[idx])

    out = lax.map(block, xt.reshape(-1, PEER_BLOCK, D_MODEL))
    return out.reshape(-1, D_MODEL)[:n_tok].reshape(*lead, D_MODEL)

def setup_inputs(seed: int = 0) -> dict:
    key = jax.random.key(seed)
    ks = jax.random.split(key, 24)
    f32 = jnp.float32

    def nrm(k, shape, scale):
        return jax.random.normal(k, shape, f32) * scale

    n_pages = PAST_LEN // PAGE_SIZE
    n_used = DEC_BATCH * n_pages
    n_pool = n_used + (n_used + 3) // 4
    page_table = jax.random.permutation(ks[0], n_pool)[:n_used].reshape(DEC_BATCH, n_pages).astype(jnp.int32)

    return {
        "x_prompt": nrm(ks[1], (BATCH, SEQ, D_MODEL), 1.0),
        "x_sample": nrm(ks[2], (DEC_BATCH, DEC_SEQ, D_MODEL), 1.0),
        "cache_k_diff": nrm(ks[3], (DEPTH, n_pool, PAGE_SIZE, H_DIFF, 2 * HD_DIFF), 1.0),
        "cache_v_diff": nrm(ks[4], (DEPTH, n_pool, PAGE_SIZE, H_DIFF, 2 * HD_DIFF), 1.0),
        "cache_k_sb": nrm(ks[5], (DEPTH, n_pool, PAGE_SIZE, H_SB, HD_SB), 1.0),
        "cache_v_sb": nrm(ks[6], (DEPTH, n_pool, PAGE_SIZE, H_SB, HD_SB), 1.0),
        "page_table": page_table,
        "rel_bias": nrm(ks[7], (N_BUCKETS, H_DIFF), 0.5),
        "norm_mix": 1.0 + nrm(ks[8], (DEPTH, D_MODEL), 0.01),
        "w_in": nrm(ks[9], (DEPTH, D_MODEL, W_IN), D_MODEL ** -0.5),
        "lambda_q1": nrm(ks[10], (DEPTH, HD_DIFF), 0.1),
        "lambda_k1": nrm(ks[11], (DEPTH, HD_DIFF), 0.1),
        "lambda_q2": nrm(ks[12], (DEPTH, HD_DIFF), 0.1),
        "lambda_k2": nrm(ks[13], (DEPTH, HD_DIFF), 0.1),
        "subln_gain": 1.0 + nrm(ks[14], (DEPTH, 2 * HD_DIFF), 0.01),
        "w_proj_diff": nrm(ks[15], (DEPTH, W_DIFF, D_MODEL), W_DIFF ** -0.5),
        "w_proj_sb": nrm(ks[16], (DEPTH, W_SB, D_MODEL), W_SB ** -0.5),
        "w_out": nrm(ks[17], (DEPTH, D_MODEL, D_MODEL), D_MODEL ** -0.5),
        "norm_ffn": 1.0 + nrm(ks[18], (DEPTH, D_MODEL), 0.01),
        "peer_w_query": nrm(ks[19], (DEPTH, D_MODEL, PEER_HEADS * PEER_KD), D_MODEL ** -0.5),
        "peer_sub_keys": nrm(ks[20], (DEPTH, PEER_HEADS, 2, PEER_KEYS, PEER_KD // 2), (PEER_KD // 2) ** -0.5),
        "peer_u": nrm(ks[21], (DEPTH, N_EXPERTS, D_MODEL), D_MODEL ** -0.5),
        "peer_v": nrm(ks[22], (DEPTH, N_EXPERTS, D_MODEL), PEER_HEADS ** -0.5),
        "norm_final": 1.0 + nrm(ks[23], (D_MODEL,), 0.01),
    }

def reference(x_prompt, x_sample, cache_k_diff, cache_v_diff, cache_k_sb, cache_v_sb, page_table,
              rel_bias, norm_mix, w_in, lambda_q1, lambda_k1, lambda_q2, lambda_k2, subln_gain,
              w_proj_diff, w_proj_sb, w_out, norm_ffn, peer_w_query, peer_sub_keys, peer_u, peer_v,
              norm_final):
    f32 = jnp.float32
    h_p, h_s = x_prompt, x_sample
    kdp, vdp, ksp, vsp, kds, vds, kss, vss = [], [], [], [], [], [], [], []
    for l in range(DEPTH):
        lam_init = 0.8 - 0.6 * math.exp(-0.3 * l)
        lam = (jnp.exp(jnp.sum(lambda_q1[l].astype(f32) * lambda_k1[l].astype(f32)))
               - jnp.exp(jnp.sum(lambda_q2[l].astype(f32) * lambda_k2[l].astype(f32))) + lam_init)

        def layer(h, attend):
            xn = rms_norm(h, norm_mix[l])
            qa, ka, va, qb, kb, vb, ga, gb = project_mixer_inputs(xn, w_in[l])
            o_a, o_b = attend(qa, ka, va, qb, kb, vb)
            h = h + merge_branches(o_a, o_b, ga, gb, subln_gain[l], lam_init,
                                   w_proj_diff[l], w_proj_sb[l], w_out[l])
            h = h + peer_ffn(rms_norm(h, norm_ffn[l]), peer_w_query[l], peer_sub_keys[l], peer_u[l], peer_v[l])
            return h, ka, va, kb, vb

        h_p, ka, va, kb, vb = layer(
            h_p, lambda qa, ka, va, qb, kb, vb: prompt_attention(qa, ka, va, qb, kb, vb, rel_bias, lam))
        kdp.append(ka); vdp.append(va); ksp.append(kb); vsp.append(vb)

        h_s, ka, va, kb, vb = layer(
            h_s, lambda qa, ka, va, qb, kb, vb: sample_attention(
                qa, ka, va, qb, kb, vb, cache_k_diff[l], cache_v_diff[l], cache_k_sb[l], cache_v_sb[l],
                page_table, rel_bias, lam))
        kds.append(ka); vds.append(va); kss.append(kb); vss.append(vb)

    y_prompt = rms_norm(h_p, norm_final)
    y_sample = rms_norm(h_s, norm_final)
    return (y_prompt, y_sample,
            jnp.stack(kdp), jnp.stack(vdp), jnp.stack(ksp), jnp.stack(vsp),
            jnp.stack(kds), jnp.stack(vds), jnp.stack(kss), jnp.stack(vss))


_drawn_inputs = setup_inputs


def setup_inputs(seed=0):
    import zlib

    import numpy as np

    out = dict(_drawn_inputs(seed))
    spreads = {}
    factors = {'norm_mix': 3.284,
     'lambda_q1': 6.052,
     'subln_gain': 21.727,
     'norm_ffn': 16.04,
     'norm_final': 33.849}
    for name, (base, spread) in spreads.items():
        noise = np.random.default_rng([zlib.crc32(name.encode()), seed]).standard_normal(out[name].shape)
        drawn = base * np.exp(spread * noise) if base else spread * noise
        out[name] = __import__('jax').numpy.asarray(drawn.astype(out[name].dtype))
    for name, factor in factors.items():
        out[name] = (out[name] * factor).astype(out[name].dtype)
    return out
```

```python
from contextlib import ExitStack

import numpy as np

import concourse.bass as bass
from concourse import mybir

F32 = mybir.dt.float32
U32 = mybir.dt.uint32
I32 = mybir.dt.int32
ALU = mybir.AluOpType
ACT = mybir.ActivationFunctionType
AX = mybir.AxisListType.X
ds = bass.ds

P = 128
D = 1024
KD = D // P
NPT = 8
NS = 64
SEQ = NPT * P
T = SEQ + NS
W_IN = 5120
CH = 512
NCH = W_IN // CH
HA = 4
HB = 8
NB_DEC = 8
TD = 8
SLABW = 2 * SEQ - P
PAGES = 2
PAST = PAGES * P
KS = PAST + TD
PH = 8
TK = 16
NSLOT = PH * TK
R = 8
NDG = 4
VSUM = (1, 3, 5, 7)
TSUM = tuple(r for r in range(R) if r not in VSUM)
BUCKETS = 32
MAXD = 128
EPS = 1e-6
QA, KA, VA, QB, KB, VB, GA, GB = 0, 512, 1024, 1536, 2048, 2560, 3072, 4096
NEG = -1e30
LOWEST = -3.0e38
LAM_INIT = 0.2
RELW = 2 * SEQ


def distance_onehot():
    rel = (SEQ - 1) - np.arange(RELW)
    n = np.maximum(rel, 0)
    exact = BUCKETS // 2
    ratio = np.log(np.maximum(n, 1).astype(np.float32) / np.float32(exact)) / np.float32(np.log(MAXD / exact))
    large = np.minimum(exact + (ratio * (BUCKETS - exact)).astype(np.int32), BUCKETS - 1)
    bucket = np.where(n < exact, n, large)
    hot = np.zeros((BUCKETS + 2, RELW), np.float32)
    hot[bucket, np.arange(RELW)] = 1.0
    hot[BUCKETS, rel < 0] = 1.0
    hot[BUCKETS + 1, rel == 0] = 1.0
    return hot


def mask_rows():
    rows = np.zeros((BUCKETS + 2, HA + 1), np.float32)
    rows[BUCKETS, :] = NEG
    rows[BUCKETS + 1, HA] = NEG
    return rows


def build(nc, a, o):
    ctx = ExitStack()
    nc.disable_value_cache = True

    def dram(name, shape):
        return nc.dram_tensor(name, shape, F32, kind="Internal").ap()

    def semaphore(name):
        return ctx.enter_context(nc.semaphore(name))

    proj_d = dram("proj_d", (T, W_IN))
    attn_d = dram("attn_d", (NS, D))
    h_d = dram("h_d", (T, D))
    dist_d = dram("dist_d", (HA + 1, RELW))
    slab_d = dram("slab_d", (HA + 1, P, SLABW))

    x_all = [a["x_prompt"].rearrange("b s d -> (b s) d"), a["x_sample"].rearrange("b s d -> (b s) d")]
    w_in = a["w_in"][0].rearrange("(k p) n -> p k n", p=P)
    y_out = [o[0].rearrange("b s d -> (b s) d"), o[1].rearrange("b s d -> (b s) d")]
    kv_out = [[o[n].rearrange("l b s h e -> (l b s) (h e)") for n in group] for group in ((2, 3, 4, 5), (6, 7, 8, 9))]

    with ctx:
        ps = ctx.enter_context(nc.psum_tensor("ps", [P, 8, CH], F32))

        def both(b):
            return ps[:, b:b + 2, :].rearrange("p b c -> p (b c)")

        def keep(name, shape, dt=F32):
            return ctx.enter_context(nc.sbuf_tensor(name, shape, dt))

        ident = keep("ident", [P, P])
        gain_mix = keep("gain_mix", [P, D])
        gain_ffn = keep("gain_ffn", [P, D])
        gain_fin = keep("gain_fin", [P, D])
        gain_sub = keep("gain_sub", [P, P])
        neg_lam = keep("neg_lam", [P, 1])
        eps_t = keep("eps_t", [P, 1])
        one_t = keep("one_t", [P, 1])
        subkT = keep("subkT", [P, PH, 2 * P])
        iota16 = keep("iota16", [P, TK])
        half_scale = keep("half_scale", [P, 2])

        with ExitStack() as stage:
            def sb(name, shape, dt=F32):
                return stage.enter_context(nc.sbuf_tensor(name, shape, dt))

            hot = sb("hot", [BUCKETS + 2, RELW])
            table = sb("table", [BUCKETS + 2, HA + 1])
            dist = sb("dist", [HA + 1, RELW])
            lams = sb("lams", [P, 4, 64])
            prod = sb("prod", [P, 2, 64])
            dots = sb("dots", [P, 2])
            expd = sb("expd", [P, 2])
            diff = sb("diff", [P, 1])
            subk = sb("subk", [P, PH, 2, 64])
            s_mask = semaphore("c_mask")
            s_gain = semaphore("c_gain")
            s_lam = semaphore("c_lam")
            s_subk = semaphore("c_subk")
            s_tab = semaphore("c_tab")
            s_ident = semaphore("c_ident")
            s_zero = semaphore("c_zero")
            s_dot = semaphore("c_dot")
            s_exp = semaphore("c_exp")
            s_link = semaphore("c_link")
            s_dist = semaphore("c_dist")
            s_dcopy = semaphore("c_dcopy")
            s_skT = semaphore("c_skT")
            s_skc = semaphore("c_skc")
            s_store = semaphore("c_store")

            with nc.Block() as block:
                @block.sync
                def _(sp):
                    sp.dma_start(table[:], a["mask_rows"]).then_inc(s_mask, 16)
                    sp.dma_start(hot[:], a["distance_onehot"]).then_inc(s_tab, 16)
                    sp.wait_ge(s_mask, 16)
                    sp.dma_start(table[0:BUCKETS, 0:HA], a["rel_bias"], allow_slow_non_contiguous=True).then_inc(s_tab, 16)
                    sp.dma_start(subk[:], a["peer_sub_keys"][0].rearrange("h c n e -> n h c e")).then_inc(s_subk, 16)
                    for n, name in enumerate(("lambda_q1", "lambda_k1", "lambda_q2", "lambda_k2")):
                        sp.dma_start(lams[:, n, :], a[name][0:1, :].broadcast_to([P, 64])).then_inc(s_lam, 16)
                    sp.dma_start(gain_mix[:], a["norm_mix"][0:1, :].broadcast_to([P, D])).then_inc(s_gain, 16)
                    sp.dma_start(gain_ffn[:], a["norm_ffn"][0:1, :].broadcast_to([P, D])).then_inc(s_gain, 16)
                    sp.dma_start(gain_fin[:], a["norm_final"].rearrange("(o d) -> o d", o=1).broadcast_to([P, D])).then_inc(s_gain, 16)
                    sp.dma_start(gain_sub[:], a["subln_gain"][0:1, :].broadcast_to([P, P])).then_inc(s_gain, 16)
                    sp.wait_ge(s_dcopy, 4)
                    sp.dma_start(dist_d[:, :], dist[:]).then_inc(s_store, 16)
                    sp.wait_ge(s_store, 16)
                    sp.wait_ge(s_gain, 64)

                @block.gpsimd
                def _(pool):
                    pool.memset(ident[:], 0.0).then_inc(s_zero, 1)
                    pool.memset(subkT[:], 0.0).then_inc(s_zero, 1)
                    pool.memset(eps_t[:], EPS).then_inc(s_zero, 1)
                    pool.memset(one_t[:], 1.0).then_inc(s_zero, 1)
                    pool.iota(iota16[:], pattern=[[1, TK]], base=0, channel_multiplier=0,
                              allow_small_or_imprecise_dtypes=True).then_inc(s_zero, 1)
                    pool.wait_ge(s_zero, 1)
                    pool.affine_select(out=ident[:], in_=ident[:], compare_op=ALU.not_equal, fill=1.0,
                                       base=0, pattern=[[-1, P]], channel_multiplier=1).then_inc(s_ident, 1)

                @block.tensor
                def _(pe):
                    pe.wait_ge(s_tab, 32)
                    for c in range(4):
                        nc.tensor.matmul(ps[0:HA + 1, c, :], table[:], hot[:, c * CH:(c + 1) * CH],
                                         start=True, stop=True).then_inc(s_dist, 1)
                    pe.wait_ge(s_ident, 1)
                    pe.wait_ge(s_subk, 16)
                    for h in range(PH):
                        nc.tensor.transpose(ps[:, 4 + h // 4, (h % 4) * P:(h % 4 + 1) * P],
                                            subk[:, h].rearrange("n c e -> n (c e)"), ident[:]).then_inc(s_skT, 1)

                @block.vector
                def _(dve):
                    for m in range(2):
                        nc.vector.memset(half_scale[64 * m:64 * m + 64, m:m + 1], 0.125)
                        nc.vector.memset(half_scale[64 * m:64 * m + 64, 1 - m:2 - m], 0.0)
                    for c in range(4):
                        dve.wait_ge(s_dist, c + 1)
                        nc.vector.tensor_copy(dist[:, c * CH:(c + 1) * CH], ps[0:HA + 1, c, :]).then_inc(s_dcopy, 1)
                    dve.wait_ge(s_lam, 64)
                    for n in range(2):
                        nc.vector.tensor_tensor_reduce(out=prod[:, n, :], in0=lams[:, 2 * n, :], in1=lams[:, 2 * n + 1, :],
                                                       scale=1.0, scalar=0.0, op0=ALU.mult, op1=ALU.add,
                                                       accum_out=dots[:, n:n + 1]).then_inc(s_dot, 1)
                    dve.wait_ge(s_exp, 1)
                    nc.vector.tensor_tensor(diff[:], expd[:, 1:2], expd[:, 0:1], ALU.subtract).then_inc(s_link, 1)
                    dve.wait_ge(s_link, 1)
                    nc.vector.tensor_scalar_add(neg_lam[:], diff[:], -LAM_INIT).then_inc(s_link, 1)
                    dve.wait_ge(s_gain, 64)
                    nc.vector.tensor_scalar_mul(gain_sub[:], gain_sub[:], 1.0 - LAM_INIT).then_inc(s_link, 1)
                    dve.wait_ge(s_skT, PH)
                    dve.wait_ge(s_zero, 2)
                    for half in range(2):
                        rows = slice(64 * half, 64 * half + 64)
                        nc.vector.tensor_copy(subkT[rows, :, half * P:(half + 1) * P],
                                              both(4)[rows, :].rearrange("p (h n) -> p h n", n=P)).then_inc(s_skc, 1)

                @block.scalar
                def _(act):
                    act.wait_ge(s_dot, 2)
                    nc.scalar.activation(expd[:], dots[:], ACT.Exp).then_inc(s_exp, 1)

        with ExitStack() as stage:
            def sb(name, shape, dt=F32):
                return stage.enter_context(nc.sbuf_tensor(name, shape, dt))

            xnT = sb("xnT", [P, KD, T])
            wbuf = sb("wbuf", [P, 2, KD, CH])
            xin = sb("xin", [P, 2, D])
            xn = sb("xn", [P, 2, D])
            sq = sb("sq", [P, D])
            ssum = sb("ssum", [P, 2])
            rms = sb("rms", [P, 2])
            rstd = sb("rstd", [P, 2])
            pout = sb("pout", [P, 3, CH])
            s_x = [semaphore(f"p_x{n}") for n in range(2)]
            s_w = [semaphore(f"p_w{n}") for n in range(2)]
            s_sum = semaphore("p_sum")
            s_rms = semaphore("p_rms")
            s_rstd = semaphore("p_rstd")
            s_xn = semaphore("p_xn")
            s_xT = semaphore("p_xT")
            s_xTc = semaphore("p_xTc")
            s_mm = semaphore("p_mm")
            s_ev = semaphore("p_ev")
            s_st = [semaphore(f"p_st{n}") for n in range(3)]
            s_turn_pool = semaphore("p_turn_pool")
            s_turn_act = semaphore("p_turn_act")

            tiles = [(t, P) for t in range(NPT)] + [(NPT, NS)]
            NT = len(tiles)

            with nc.Block() as block:
                def load_x(sp, t):
                    src = x_all[0][t * P:(t + 1) * P, :] if t < NPT else x_all[1]
                    sp.dma_start(xin[0:tiles[t][1], t % 2, :], src).then_inc(s_x[t % 2], 16)

                @block.sync
                def _(sp):
                    load_x(sp, 0)
                    load_x(sp, 1)
                    for n in range(2):
                        sp.dma_start(wbuf[:, n], w_in[:, :, n * CH:(n + 1) * CH]).then_inc(s_w[n], 16)
                    for t in range(2, NT):
                        sp.wait_ge(s_xn, t - 1)
                        load_x(sp, t)
                    with sp.Fori(0, NCH // 2 - 1) as i:
                        for n in range(2):
                            src = sp.snap(i * (2 * CH) + (2 + n) * CH)
                            sp.wait_ge(s_mm, i * (2 * NT) + (n + 1) * NT)
                            sp.dma_start(wbuf[:, n], w_in[:, :, ds(src, CH)]).then_inc(s_w[n], 16)

                @block.gpsimd
                def _(pool):
                    with pool.Fori(0, NCH // 2) as i:
                        for c in range(2):
                            for t, rows in tiles:
                                k = c * NT + t
                                col = pool.snap(i * (2 * CH) + c * CH)
                                pool.wait_ge(s_ev, i * (2 * NT) + k + 1)
                                pool.sem_inc(s_turn_pool, 1)
                                pool.dma_start(proj_d[t * P:t * P + rows, ds(col, CH)],
                                               pout[0:rows, k % 3, :]).then_inc(s_st[k % 3], 16)
                    for n in range(3):
                        pool.wait_ge(s_st[n], 16 * NCH * NT // 3)

                @block.vector
                def _(dve):
                    for t, rows in tiles:
                        b = t % 2
                        dve.wait_ge(s_x[b], 16 * (t // 2 + 1))
                        if t:
                            dve.wait_ge(s_sum, t)
                        nc.vector.tensor_tensor_reduce(out=sq[0:rows, :], in0=xin[0:rows, b, :], in1=xin[0:rows, b, :],
                                                       scale=1.0, scalar=0.0, op0=ALU.mult, op1=ALU.add,
                                                       accum_out=ssum[0:rows, b:b + 1]).then_inc(s_sum, 1)
                        dve.wait_ge(s_rms, t + 1)
                        nc.vector.reciprocal(rstd[0:rows, b:b + 1], rms[0:rows, b:b + 1]).then_inc(s_rstd, 1)
                        dve.wait_ge(s_rstd, t + 1)
                        if t >= 2:
                            dve.wait_ge(s_xT, 2 * (t - 1))
                        nc.vector.scalar_tensor_tensor(out=xn[0:rows, b, :], in0=xin[0:rows, b, :],
                                                       scalar=rstd[0:rows, b:b + 1], in1=gain_mix[0:rows, :],
                                                       op0=ALU.mult, op1=ALU.mult).then_inc(s_xn, 1)

                @block.scalar
                def _(act):
                    for t, rows in tiles:
                        b = t % 2
                        act.wait_ge(s_sum, t + 1)
                        nc.scalar.activation(rms[0:rows, b:b + 1], ssum[0:rows, b:b + 1], ACT.Sqrt,
                                             bias=eps_t[0:rows, :], scale=1.0 / D).then_inc(s_rms, 1)
                        for g in range(2):
                            act.wait_ge(s_xT, 2 * t + g + 1)
                            nc.scalar.copy(xnT[:, 4 * g:4 * g + 4, t * P:t * P + rows],
                                           ps[:, g, :].rearrange("p (k r) -> p k r", r=P)[:, :, 0:rows]).then_inc(s_xTc, 1)

                    def take(c, i):
                        for t, rows in tiles:
                            k = c * NT + t
                            act.wait_ge(s_mm, i * (2 * NT) + k + 1)
                            act.sem_inc(s_turn_act, 1)
                            if k >= 3 or not isinstance(i, int):
                                act.wait_ge(s_st[k % 3], i * (16 * 2 * NT // 3) + 16 * (k // 3))
                            nc.scalar.copy(pout[0:rows, k % 3, :], ps[0:rows, k % 6 + 2, :]).then_inc(s_ev, 1)

                    for c in range(2):
                        take(c, 0)
                    with act.Fori(1, NCH // 2) as i:
                        for c in range(2):
                            take(c, i)

                @block.tensor
                def _(pe):
                    for t, rows in tiles:
                        pe.wait_ge(s_xn, t + 1)
                        for g in range(2):
                            if t:
                                pe.wait_ge(s_xTc, 2 * (t - 1) + g + 1)
                            for k in range(4):
                                kt = 4 * g + k
                                m = nc.tensor.transpose(ps[:, g, k * P:k * P + rows],
                                                        xn[0:rows, t % 2, kt * P:(kt + 1) * P], ident[0:rows, 0:rows])
                            m.then_inc(s_xT, 1)
                    pe.wait_ge(s_xTc, 2 * NT)

                    def chunk(c, i, after):
                        pe.wait_ge(s_w[c], i * 16 + 16)
                        for t, rows in tiles:
                            k = c * NT + t
                            if after is not None:
                                pe.wait_ge(s_ev, after + k - 5)
                            elif k >= 6:
                                pe.wait_ge(s_ev, k - 5)
                            for kt in range(KD):
                                m = nc.tensor.matmul(ps[0:rows, k % 6 + 2, :], xnT[:, kt, t * P:t * P + rows],
                                                     wbuf[:, c, kt, :], start=(kt == 0), stop=(kt == KD - 1))
                            m.then_inc(s_mm, 1)

                    for c in range(2):
                        chunk(c, 0, None)
                    with pe.Fori(1, NCH // 2) as i:
                        for c in range(2):
                            chunk(c, i, i * (2 * NT))

        keyT = keep("keyT", [P, KD, SEQ])
        val = keep("val", [P, NPT, D])
        with ExitStack() as stage:
            kst = stage.enter_context(nc.sbuf_tensor("kst", [P, 2, D], F32))
            flip = stage.enter_context(nc.sbuf_tensor("flip", [P, P], F32))
            climb = stage.enter_context(nc.sbuf_tensor("climb", [P, HA + 1, SLABW], F32))
            slab = stage.enter_context(nc.sbuf_tensor("slab", [P, HA + 1, SLABW], F32))
            QW = SLABW // 4
            s_climb = semaphore("k_climb")
            s_flip = semaphore("k_flip")
            s_mm = semaphore("k_mm")
            s_slab = semaphore("k_slab")
            s_slab_out = semaphore("k_slab_out")
            s_v = semaphore("k_v")
            s_k = [semaphore(f"k_k{n}") for n in range(2)]
            s_kT = semaphore("k_kT")
            s_kTc = semaphore("k_kTc")
            s_out = semaphore("k_out")

            with nc.Block() as block:
                @block.sync
                def _(sp):
                    for r in range(HA + 1):
                        sp.dma_start(climb[:, r, :], bass.AP(tensor=dist_d.tensor, offset=r * RELW,
                                                             ap=[[1, P], [1, SLABW]])).then_inc(s_climb, 16)
                    for t in range(NPT):
                        b = t % 2
                        if t >= 2:
                            sp.wait_ge(s_kT, 2 * (t - 1))
                        for n, col in enumerate((KA, KB)):
                            sp.dma_start(kst[:, b, n * CH:(n + 1) * CH],
                                         proj_d[t * P:(t + 1) * P, col:col + CH]).then_inc(s_k[b], 16)
                    sp.wait_ge(s_slab, 4 * (HA + 1))
                    sp.dma_start(slab_d.rearrange("r p c -> p r c"), slab[:]).then_inc(s_slab_out, 16)
                    sp.wait_ge(s_slab_out, 16)

                @block.gpsimd
                def _(pool):
                    pool.memset(flip[:], 0.0).then_inc(s_flip, 1)
                    pool.wait_ge(s_flip, 1)
                    pool.affine_select(out=flip[:], in_=flip[:], compare_op=ALU.not_equal, fill=1.0,
                                       base=1 - P, pattern=[[1, P]], channel_multiplier=1).then_inc(s_flip, 1)
                    for n, col in enumerate((VA, VB)):
                        pool.dma_start(val[:, :, n * CH:(n + 1) * CH],
                                       proj_d[0:SEQ, col:col + CH].rearrange("(t p) c -> p t c", p=P)).then_inc(s_v, 16)
                    for group, (r0, r1) in zip(kv_out, ((0, SEQ), (SEQ, T))):
                        for dst, col in zip(group, (KA, VA, KB, VB)):
                            pool.dma_start(dst, proj_d[r0:r1, col:col + CH]).then_inc(s_out, 16)
                    pool.wait_ge(s_v, 32)
                    pool.wait_ge(s_out, 16 * 8)

                @block.tensor
                def _(pe):
                    for t in range(NPT):
                        pe.wait_ge(s_k[t % 2], 32 * (t // 2 + 1))
                        for g in range(2):
                            if t:
                                pe.wait_ge(s_kTc, 2 * (t - 1) + g + 1)
                            for k in range(4):
                                u = 4 * g + k
                                m = nc.tensor.transpose(ps[:, g, k * P:(k + 1) * P],
                                                        kst[:, t % 2, u * P:(u + 1) * P], ident[:])
                            m.then_inc(s_kT, 1)
                    pe.wait_ge(s_flip, 2)
                    pe.wait_ge(s_climb, 16 * (HA + 1))
                    for n in range(4 * (HA + 1)):
                        if n >= 4:
                            pe.wait_ge(s_slab, n - 3)
                        c = (n % 4) * QW
                        nc.tensor.matmul(ps[:, 2 + n % 4, 0:QW], flip[:], climb[:, n // 4, c:c + QW],
                                         start=True, stop=True).then_inc(s_mm, 1)

                @block.vector
                def _(dve):
                    for n in range(4 * (HA + 1)):
                        dve.wait_ge(s_mm, n + 1)
                        c = (n % 4) * QW
                        nc.vector.tensor_copy(slab[:, n // 4, c:c + QW], ps[:, 2 + n % 4, 0:QW]).then_inc(s_slab, 1)

                @block.scalar
                def _(act):
                    for t in range(NPT):
                        for g in range(2):
                            act.wait_ge(s_kT, 2 * t + g + 1)
                            nc.scalar.copy(keyT[:, 4 * g:4 * g + 4, t * P:(t + 1) * P],
                                           ps[:, g, :].rearrange("p (u r) -> p u r", r=P)).then_inc(s_kTc, 1)

        with ExitStack() as stage:
            def sb(name, shape, dt=F32):
                return stage.enter_context(nc.sbuf_tensor(name, shape, dt))

            qk = sb("s_qk", [NS, 2, D])
            qT = sb("s_qT", [P, KD, NS])
            knT = sb("s_knT", [P, KD, NS])
            qblk = sb("s_qblk", [P, KD * (P + TK)])
            kpage = sb("s_kpage", [P, PAGES, D])
            vpage = sb("s_vpage", [P, 2, PAGES, D])
            vnew = sb("s_vnew", [TD, 2, D])
            kT = sb("s_kT", [P, KD, KS])
            add = sb("s_add", [P, KS])
            s = sb("s_s", [P, KS])
            e = sb("s_e", [P, KS])
            w = sb("s_w", [P, KS])
            mx = sb("s_mx", [P, 1])
            nm = sb("s_nm", [P, 1])
            l = sb("s_l", [P, 1])
            rl = sb("s_rl", [P, 1])
            pT = sb("s_pT", [P, 3, P])
            pd = sb("s_pd", [P, 3, HA * TD])
            oa = sb("s_oa", [HA * TD, CH])
            ob = sb("s_ob", [HB * TD, CH])
            pages = sb("s_pages", [1, NB_DEC * PAGES], I32)
            s_qk = semaphore("s_qk")
            s_pt = semaphore("s_pt")
            s_add = semaphore("s_add")
            s_page = semaphore("s_page")
            s_val = [semaphore(f"s_val{n}") for n in range(2)]
            s_z = semaphore("s_z")
            s_qT = semaphore("s_qT")
            s_qTc = semaphore("s_qTc")
            s_blk = semaphore("s_blk")
            s_kT = semaphore("s_kT")
            s_kTc = semaphore("s_kTc")
            s_S = semaphore("s_S")
            s_sa = semaphore("s_sa")
            s_act = semaphore("s_act")
            s_dve = semaphore("s_dve")
            s_prob = semaphore("s_prob")
            s_T = semaphore("s_T")
            s_Tc = semaphore("s_Tc")
            s_pd = semaphore("s_pd")
            s_O = semaphore("s_O")
            s_Oc = semaphore("s_Oc")
            s_store = semaphore("s_store")
            s_link2 = semaphore("s_pTnew")
            A, B = slice(0, HA * 2 * TD), slice(HA * 2 * TD, P)
            KC = (P, P, TD)
            pools = [a[n][0].rearrange("n p h e -> n p (h e)") for n in
                     ("cache_k_diff", "cache_k_sb", "cache_v_diff", "cache_v_sb")]
            last_page = pools[0].shape[0] - 1

            with nc.Block() as block:
                @block.sync
                def _(sp):
                    sp.dma_start(pages[:], a["page_table"].rearrange("(o b) g -> o (b g)", o=1)).then_inc(s_pt, 16)
                    for n, (c0, c1) in enumerate(((QA, QB), (KA, KB))):
                        sp.dma_start(qk[:, n, 0:CH], proj_d[SEQ:T, c0:c0 + CH]).then_inc(s_qk, 16)
                        sp.dma_start(qk[:, n, CH:D], proj_d[SEQ:T, c1:c1 + CH]).then_inc(s_qk, 16)
                    for m in range(2 * HA + HB):
                        row = min(m // 2, HA)
                        sp.dma_start(add[m * TD:(m + 1) * TD, :],
                                     slab_d[row, 0:TD, SLABW - SEQ - PAST:SLABW - SEQ - PAST + KS]).then_inc(s_add, 16)
                    sp.wait_ge(s_pt, 16)
                    for b in range(NB_DEC):
                        for g in range(PAGES):
                            page = sp.value_load(pages[0:1, b * PAGES + g:b * PAGES + g + 1], min_val=0, max_val=last_page)
                            if g == 0 and b:
                                sp.wait_ge(s_kT, 4 * b)
                            for n in range(2):
                                sp.dma_start(kpage[:, g, n * CH:(n + 1) * CH],
                                             pools[n][ds(page, 1)].rearrange("o p c -> (o p) c")).then_inc(s_page, 16)
                            if g == 0 and b >= 2:
                                sp.wait_ge(s_O, b - 1)
                            for n in range(2):
                                sp.dma_start(vpage[:, b % 2, g, n * CH:(n + 1) * CH],
                                             pools[2 + n][ds(page, 1)].rearrange("o p c -> (o p) c")).then_inc(s_val[b % 2], 16)
                        for n, col in enumerate((VA, VB)):
                            sp.dma_start(vnew[:, b % 2, n * CH:(n + 1) * CH],
                                         proj_d[SEQ + b * TD:SEQ + (b + 1) * TD, col:col + CH]).then_inc(s_val[b % 2], 16)

                @block.gpsimd
                def _(pool):
                    pool.memset(qblk[:], 0.0).then_inc(s_z, 1)
                    for b in range(NB_DEC):
                        rows = slice(b * TD, (b + 1) * TD)
                        pool.wait_ge(s_Oc, 2 * b + 2)
                        for h in range(HA):
                            pool.dma_start(attn_d[rows, h * P:(h + 1) * P],
                                           oa[h * TD:(h + 1) * TD, h * P:(h + 1) * P]).then_inc(s_store, 16)
                        for h in range(HB):
                            pool.dma_start(attn_d[rows, CH + h * 64:CH + (h + 1) * 64],
                                           ob[h * TD:(h + 1) * TD, h * 64:(h + 1) * 64]).then_inc(s_store, 16)
                    pool.wait_ge(s_store, 16 * NB_DEC * (HA + HB))

                @block.tensor
                def _(pe):
                    pe.wait_ge(s_qk, 64)
                    for n in range(2):
                        for u in range(KD):
                            m = nc.tensor.transpose(ps[:, n, u * NS:(u + 1) * NS], qk[:, n, u * P:(u + 1) * P], ident[0:NS, 0:NS])
                        m.then_inc(s_qT, 1)
                    pe.wait_ge(s_qTc, 2)

                    def transpose_keys(b):
                        pe.wait_ge(s_page, 64 * (b + 1))
                        for g in range(PAGES):
                            for j in range(2):
                                bank = 2 * g + j
                                if b:
                                    pe.wait_ge(s_kTc, 5 * (b - 1) + bank + 1)
                                for k in range(4):
                                    u = 4 * j + k
                                    m = nc.tensor.transpose(ps[:, bank, k * P:(k + 1) * P],
                                                            kpage[:, g, u * P:(u + 1) * P], ident[:])
                                m.then_inc(s_kT, 1)

                    transpose_keys(0)
                    for b in range(NB_DEC):
                        pe.wait_ge(s_kTc, 5 * (b + 1))
                        pe.wait_ge(s_blk, 2 * (b + 1))
                        if b:
                            pe.wait_ge(s_sa, b)
                        for u in range(KD):
                            m = nc.tensor.matmul(ps[:, 4, 0:KS], qblk[:, u * P:(u + 1) * P], kT[:, u, :],
                                                 start=(u == 0), stop=(u == KD - 1))
                        m.then_inc(s_S, 1)
                        if b + 1 < NB_DEC:
                            transpose_keys(b + 1)
                        pe.wait_ge(s_prob, 2 * (b + 1))
                        if b:
                            pe.wait_ge(s_Tc, b)
                        for c, kc in enumerate(KC):
                            m = nc.tensor.transpose(ps[0:kc, 5, c * P:(c + 1) * P], w[:, c * P:c * P + kc], ident[:])
                        m.then_inc(s_T, 1)
                        pe.wait_ge(s_pd, b + 1)
                        pe.wait_ge(s_val[b % 2], 96 * (b // 2 + 1))
                        if b:
                            pe.wait_ge(s_Oc, 2 * b)
                        for c, kc in enumerate(KC):
                            v = vpage[:, b % 2, c, :] if c < PAGES else vnew[:, b % 2, :]
                            nc.tensor.matmul(ps[0:HA * TD, 6, :], pd[0:kc, c, :], v[0:kc, 0:CH], start=(c == 0), stop=(c == 2))
                        for c, kc in enumerate(KC):
                            v = vpage[:, b % 2, c, :] if c < PAGES else vnew[:, b % 2, :]
                            m = nc.tensor.matmul(ps[0:HB * TD, 7, :], pT[0:kc, c, 64:P], v[0:kc, CH:D], start=(c == 0), stop=(c == 2))
                        m.then_inc(s_O, 1)

                @block.scalar
                def _(act):
                    n = 0
                    act.wait_ge(s_qT, 1)
                    nc.scalar.activation(qT[:], ps[:, 0, :].rearrange("p (u r) -> p u r", r=NS), ACT.Copy, scale=0.125).then_inc(s_qTc, 1)
                    act.wait_ge(s_qT, 2)
                    nc.scalar.copy(knT[:], ps[:, 1, :].rearrange("p (u r) -> p u r", r=NS)).then_inc(s_qTc, 1)
                    act.wait_ge(s_qTc, 2)

                    def take_keys(b):
                        if b:
                            act.wait_ge(s_S, b)
                        for g in range(PAGES):
                            for j in range(2):
                                act.wait_ge(s_kT, 4 * b + 2 * g + j + 1)
                                nc.scalar.copy(kT[:, 4 * j:4 * j + 4, g * P:(g + 1) * P],
                                               ps[:, 2 * g + j, :].rearrange("p (u r) -> p u r", r=P)).then_inc(s_kTc, 1)
                        nc.scalar.copy(kT[:, :, PAST:KS], knT[:, :, b * TD:(b + 1) * TD]).then_inc(s_kTc, 1)

                    take_keys(0)
                    for b in range(NB_DEC):
                        act.wait_ge(s_sa, b + 1)
                        nc.scalar.activation(e[B], s[B], ACT.Abs).then_inc(s_act, 1)
                        act.wait_ge(s_act, 4 * b + 1)
                        nc.scalar.activation(e[B], e[B], ACT.Exp, scale=-1.0).then_inc(s_act, 1)
                        act.wait_ge(s_dve, 7 * b + 2)
                        nc.scalar.activation(e[A], s[A], ACT.Exp, bias=nm[A, :], accum_out=l[A, :]).then_inc(s_act, 1)
                        act.wait_ge(s_act, 4 * b + 3)
                        nc.scalar.activation(e[B], e[B], ACT.Ln, bias=one_t[B, :]).then_inc(s_act, 1)
                        if b + 1 < NB_DEC:
                            take_keys(b + 1)
                        act.wait_ge(s_dve, 7 * b + 7)
                        nc.scalar.activation(w[B], s[B], ACT.Exp).then_inc(s_prob, 1)
                        act.wait_ge(s_T, b + 1)
                        nc.scalar.copy(pT[:, 0:2, :], ps[:, 5, 0:2 * P].rearrange("p (c r) -> p c r", r=P)).then_inc(s_Tc, 0 + 1)

                @block.vector
                def _(dve):
                    dve.wait_ge(s_z, 1)
                    dve.wait_ge(s_qTc, 1)
                    dve.wait_ge(s_add, 16 * 16)
                    blk = qblk[:].rearrange("p (u c) -> p u c", c=P + TK)
                    for b in range(NB_DEC):
                        if b:
                            dve.wait_ge(s_S, b)
                        for half in range(2):
                            rows = slice(64 * half, 64 * half + 64)
                            nc.vector.tensor_copy(blk[rows, :, half * TD:(half + 1) * TD],
                                                  qT[rows, :, b * TD:(b + 1) * TD]).then_inc(s_blk, 1)
                        dve.wait_ge(s_S, b + 1)
                        if b:
                            dve.wait_ge(s_prob, 2 * b)
                        nc.vector.tensor_tensor(s[:], ps[:, 4, 0:KS], add[:], ALU.add).then_inc(s_sa, 1)
                        dve.wait_ge(s_sa, b + 1)
                        nc.vector.reduce_max(mx[A, :], s[A], AX).then_inc(s_dve, 1)
                        dve.wait_ge(s_dve, 7 * b + 1)
                        nc.vector.tensor_scalar_mul(nm[A, :], mx[A, :], -1.0).then_inc(s_dve, 1)
                        dve.wait_ge(s_act, 4 * b + 4)
                        nc.vector.reciprocal(rl[A, :], l[A, :]).then_inc(s_dve, 1)
                        nc.vector.scalar_tensor_tensor(out=e[B], in0=s[B], scalar=0.0, in1=e[B], op0=ALU.max, op1=ALU.add).then_inc(s_dve, 1)
                        dve.wait_ge(s_dve, 7 * b + 4)
                        if b:
                            dve.wait_ge(s_T, b)
                        nc.vector.tensor_scalar_mul(w[A], e[A], rl[A, :]).then_inc(s_prob, 1)
                        nc.vector.tensor_tensor_scan(out=w[B, ::-1], data0=e[B, ::-1], data1=e[B, ::-1], initial=0.0,
                                                     op0=ALU.add, op1=ALU.bypass).then_inc(s_dve, 1)
                        dve.wait_ge(s_dve, 7 * b + 5)
                        nc.vector.tensor_tensor(s[B], s[B], w[B], ALU.subtract).then_inc(s_dve, 2)
                        dve.wait_ge(s_Tc, b + 1)
                        nc.vector.tensor_copy(pT[0:TD, 2, :], ps[0:TD, 5, 2 * P:3 * P]).then_inc(s_link2, 1)
                        dve.wait_ge(s_link2, b + 1)
                        for c, kc in enumerate(KC):
                            two = pT[0:kc, c, 0:64].rearrange("p (h m q) -> p h m q", m=2, q=TD)
                            m = nc.vector.scalar_tensor_tensor(out=pd[0:kc, c, :].rearrange("p (h q) -> p h q", q=TD),
                                                               in0=two[:, :, 1, :], scalar=neg_lam[0:kc, :],
                                                               in1=two[:, :, 0, :], op0=ALU.mult, op1=ALU.add)
                        m.then_inc(s_pd, 1)
                        dve.wait_ge(s_O, b + 1)
                        if b:
                            dve.wait_ge(s_store, 16 * b * (HA + HB))
                        nc.vector.tensor_copy(oa[:], ps[0:HA * TD, 6, :]).then_inc(s_Oc, 1)
                        nc.vector.tensor_copy(ob[:], ps[0:HB * TD, 7, :]).then_inc(s_Oc, 1)

        with ExitStack() as stage:
            def sb(name, shape, dt=F32):
                return stage.enter_context(nc.sbuf_tensor(name, shape, dt))

            ring = sb("t_ring", [P, R, D])
            big = sb("t_big", [P, 11, D])
            pTr = sb("t_pTr", [P, KD, P])
            o_sb = sb("t_o_sb", [P, D])
            h_sb = sb("t_h_sb", [P, D])
            xn_sb = sb("t_xn_sb", [P, D])
            y_sb = sb("t_y_sb", [P, D])

            def slots(n, m):
                return big[:, n:m, :].rearrange("p a c -> p (a c)")

            bias = big[:, 0:2, :]
            bmask = big[:, 2, :]
            z = big[:, 3:5, :]
            soft = big[:, 5:7, :]
            prob = big[:, 7:9, :]
            qz = slots(9, 11).rearrange("p (u m r) -> p u m r", m=2, r=P)
            x_sb = big[:, 0, :]
            sq = big[:, 1, :]
            wring = big[:, 3:7, :]
            mixed = big[:, 7, :]
            gates = slots(9, 11)
            q_sb = big[:, 8, :]
            left = slots(9, 11)
            cand = slots(7, 9)
            pick = slots(0, 2)
            ysq = big[:, 8, :]
            mx = sb("t_mx", [P, 2])
            nm = sb("t_nm", [P, 2])
            l = sb("t_l", [P, 2])
            rl = sb("t_rl", [P, 2])
            rl2 = sb("t_rl2", [P, 1])
            ssh, rmsh, rsh = (sb("t_" + n, [P, HA]) for n in ("ssh", "rmsh", "rsh"))
            ssx, rmsx, rsx = (sb("t_" + n, [P, 1]) for n in ("ssx", "rmsx", "rsx"))
            ssy, rmsy, rsy = (sb("t_" + n, [P, 1]) for n in ("ssy", "rmsy", "rsy"))
            top = sb("t_top", [P, 2 * PH, TK])
            topi = sb("t_topi", [P, 2 * PH, TK], U32)
            topf = sb("t_topf", [P, 2 * PH, TK])
            best = sb("t_best", [P, PH, TK])
            bestj = sb("t_bestj", [P, NSLOT], U32)
            ja = sb("t_ja", [P, 2, NSLOT], U32)
            jf = sb("t_jf", [P, 2, NSLOT])
            sel = sb("t_sel", [P, 2, NSLOT])
            idx_u = sb("t_idx_u", [P, NSLOT], U32)
            idx_v = sb("t_idx_v", [P, NSLOT], U32)
            gexp = sb("t_gexp", [P, PH, TK])
            gsum = sb("t_gsum", [P, PH])
            grec = sb("t_grec", [P, PH])
            gate = sb("t_gate", [P, PH, TK])
            dots = sb("t_dots", [P, NSLOT])
            act_u = sb("t_act_u", [P, NSLOT])
            wgt = sb("t_wgt", [P, NSLOT])
            diag = sb("t_diag", [P, NDG, P])

            s_qin = semaphore("a_qin")
            s_bias = [semaphore(f"a_bias{n}") for n in range(2)]
            s_bmask = semaphore("a_bmask")
            s_S = [semaphore(f"a_S{n}") for n in range(2)]
            s_Sr = [semaphore(f"a_Sr{n}") for n in range(2)]
            s_nm = semaphore("a_nm")
            s_exp = semaphore("a_exp")
            s_softc = semaphore("a_softc")
            s_soft = semaphore("a_soft")
            s_w = semaphore("a_w")
            s_pA = semaphore("a_pA")
            s_pB = semaphore("a_pB")
            s_T = semaphore("t_full")
            s_Tc = semaphore("t_taken")
            s_PV = semaphore("a_PV")
            s_Oc = semaphore("a_Oc")
            s_oin = semaphore("m_oin")
            s_adve = semaphore("a_dve")
            s_gin = semaphore("m_gin")
            s_xin = semaphore("m_xin")
            s_wr = [semaphore(f"m_wr{n}") for n in range(4)]
            s_wu = semaphore("m_wu")
            s_sig = semaphore("m_sig")
            s_ssh = semaphore("m_ssh")
            s_rmsh = semaphore("m_rmsh")
            s_mdve = semaphore("m_dve")
            s_On = semaphore("m_On")
            s_m = semaphore("m_m")
            s_h = semaphore("m_h")
            s_ssx = semaphore("r_ssx")
            s_rmsx = semaphore("r_rmsx")
            s_rdve = semaphore("r_dve")
            s_xn = semaphore("r_xn")
            s_qc = semaphore("r_qc")
            s_sc = semaphore("r_sc")
            s_scr = semaphore("r_scr")
            s_route = semaphore("r_route")
            s_shift = semaphore("r_shift")
            s_gexp = semaphore("r_gexp")
            s_idx = semaphore("r_idx")
            s_ring = [semaphore(f"e_ring{n}") for n in range(R)]
            s_dot = semaphore("e_dot")
            s_sum = semaphore("e_sum")
            s_vsum = semaphore("e_vsum")
            s_idxv = semaphore("e_idxv")
            s_gelu = semaphore("e_gelu")
            s_wgt = semaphore("e_wgt")
            s_diag = semaphore("e_diag")
            s_res = semaphore("e_res")
            s_yc = semaphore("f_yc")
            s_ssy = semaphore("f_ssy")
            s_rmsy = semaphore("f_rmsy")
            s_fdve = semaphore("f_dve")
            s_y_out = semaphore("f_y")
            s_yst = semaphore("f_yst")
            turn = {n: semaphore(f"turn_{n}") for n in ("sync", "pool", "act", "dve")}

            NTB = 34
            NW = 24

            class Steps:

                def __init__(self, sem, per):
                    self.sem, self.per, self.k, self.t = sem, per, 0, 0

                def begin(self, t):
                    self.t, self.k = t, 0

                def raised_by(self, instruction):
                    instruction.then_inc(self.sem, 1)
                    self.k += 1

                @property
                def value(self):
                    return self.t * self.per + self.k

            def tile(t):
                return slice(t * P, t * P + P) if isinstance(t, int) else ds(t * P, P)

            def rows_of(t):
                return NS if isinstance(t, int) and t == NPT else P

            def window(row, t, kw):
                first = SLABW - SEQ - t * P
                return slab_d[row, :, first:first + kw] if isinstance(t, int) else slab_d[row, :, ds(first, kw)]

            def sync_attend(sp, t, kw):
                rows = tile(t)
                if not (isinstance(t, int) and t == 0):
                    sp.wait_ge(s_T, (t - 1) * NTB + (28))
                    sp.sem_inc(turn["sync"], 1)
                for n, col in enumerate((QA, QB)):
                    sp.dma_start(o_sb[:, n * CH:(n + 1) * CH], proj_d[rows, col:col + CH]).then_inc(s_qin, 16)
                wins = [window(u, t, kw) for u in range(HA + 1)]
                sp.wait_ge(s_route, t)
                sp.sem_inc(turn["sync"], 1)
                for u in range(HA):
                    if u >= 2:
                        sp.wait_ge(s_Sr[1], t * 8 + u - 1)
                        sp.sem_inc(turn["sync"], 1)
                    sp.dma_start(bias[:, u % 2, 0:kw], wins[u]).then_inc(s_bias[u % 2], 16)
                    if u == 1:
                        sp.dma_start(bmask[:, 0:kw], wins[HA]).then_inc(s_bmask, 16)

            def sync_merge(sp, t):
                n_rows = rows_of(t)
                if n_rows == P:
                    x_src, g_src = x_all[0][tile(t), :], proj_d[tile(t), GA:W_IN]
                    sp.wait_ge(s_S[1], t * 8 + 8)
                    sp.sem_inc(turn["sync"], 1)
                    sp.dma_start(gates[:], g_src).then_inc(s_gin, 16)
                    sp.wait_ge(s_Sr[1], t * 8 + 3)
                    sp.sem_inc(turn["sync"], 1)
                    sp.dma_start(x_sb, x_src).then_inc(s_xin, 16)
                    sp.wait_ge(s_pB, t * 8 + 8)
                    sp.sem_inc(turn["sync"], 1)
                else:
                    sp.wait_ge(s_T, (t - 1) * NTB + 28)
                    sp.sem_inc(turn["sync"], 1)
                    sp.dma_start(o_sb[0:NS, :], attn_d[:, :]).then_inc(s_oin, 16)
                    sp.wait_ge(s_route, t)
                    sp.sem_inc(turn["sync"], 1)
                    sp.dma_start(gates[0:NS, :], proj_d[SEQ:T, GA:W_IN]).then_inc(s_gin, 16)
                    sp.dma_start(x_sb[0:NS, :], x_all[1]).then_inc(s_xin, 16)
                for n in range(NW):
                    for name, first, last in (("w_proj_diff", 0, 4), ("w_proj_sb", 4, 8), ("w_out", 8, 16),
                                              ("peer_w_query", 16, 24)):
                        if first <= n < last:
                            src = a[name][0][(n - first) * P:(n - first + 1) * P, :]
                    if n >= 4:
                        sp.wait_ge(s_wu, t * NW + n - 3)
                        sp.sem_inc(turn["sync"], 1)
                    sp.dma_start(wring[:, n % 4, :], src).then_inc(s_wr[n % 4], 16)

            def sync_finish(sp, e):
                dst = y_out[0][tile(e), :] if rows_of(e) == P else y_out[1]
                sp.wait_ge(s_y_out, e + 1)
                sp.sem_inc(turn["sync"], 1)
                sp.dma_start(dst, y_sb[0:rows_of(e), :]).then_inc(s_yst, 16)

            def gather(pool, e, table, idx, phase):
                n = rows_of(e)
                for s in range(NSLOT):
                    if phase == 0:
                        free = summed(e, s, -1) if s < R else (s_dot, e * NSLOT + s - R + 1)
                    else:
                        free = (s_dot, e * NSLOT + NSLOT - R + s + 1) if s < R else summed(e, s, -1)
                    pool.wait_ge(*free)
                    pool.sem_inc(turn["pool"], 1)
                    pool.indirect_dma_start(ring[0:n, s % R, :], None, table,
                                            bass.IndirectOffsetOnAxis(ap=idx[0:n, s:s + 1], axis=0)).then_inc(s_ring[s % R], 16)

            def summed(e, s, rounds=0):
                mine, sem = (VSUM, s_vsum) if s % R in VSUM else (TSUM, s_sum)
                return sem, (e * (NSLOT // R) + s // R + 1 + rounds) * len(mine) + mine.index(s % R) + 1

            def arrived(e, phase, s):
                return s_ring[s % R], (e * (2 * NSLOT // R) + phase * (NSLOT // R) + s // R + 1) * 16

            def pool_experts(pool, e):
                pool.wait_ge(s_route, e + 1)
                pool.sem_inc(turn["pool"], 1)
                gather(pool, e, a["peer_u"][0], idx_u, 0)
                pool.wait_ge(s_idxv, e + 1)
                pool.sem_inc(turn["pool"], 1)
                gather(pool, e, a["peer_v"][0], idx_v, 1)

            pe_T = Steps(s_T, NTB)

            def pe_transposes(pe, blocks, n):
                pe.wait_ge(s_Tc, pe_T.value)
                for k, blk in enumerate(blocks):
                    m = nc.tensor.transpose(ps[:, 6, k * P:k * P + n], blk, ident[0:n, 0:n])
                pe_T.raised_by(m)

            def pe_scores(pe, t, u, kw):
                for hf in range(2):
                    pe.wait_ge(s_Sr[hf], t * 8 + u)
                    for c in range(kw // CH):
                        m = nc.tensor.matmul(ps[:, 2 + 2 * hf + c, :], qz[:, u, hf, :], keyT[:, u, c * CH:(c + 1) * CH],
                                             start=True, stop=True)
                    m.then_inc(s_S[hf], 1)

            def pe_attend(pe, t, kw):
                nb = kw // P // 2
                pe_T.begin(t)
                pe.wait_ge(s_qin, t * 32 + 32)
                for g in range(2):
                    pe_transposes(pe, [o_sb[:, u * P:(u + 1) * P] for u in range(4 * g, 4 * g + 4)], P)
                pe.wait_ge(s_Tc, pe_T.value)
                pe.wait_ge(s_scr, t)
                pe_scores(pe, t, 0, kw)
                for u in range(8):
                    if u < 7:
                        pe_scores(pe, t, u + 1, kw)
                    if u % 4 == 0:
                        pe.wait_ge(s_Oc, t * 2 + u // 4)
                    for hf in range(1 if u < HA else 2):
                        n = u if u < HA else 4 + 2 * (u - HA) + hf
                        pe.wait_ge(*((s_pA, t * 4 + u + 1) if u < HA else (s_pB, t * 8 + n - 3)))
                        for j in range(2):
                            pe_transposes(pe, [prob[:, n % 2, (j * nb + k) * P:(j * nb + k + 1) * P] for k in range(nb)], P)
                        pe.wait_ge(s_Tc, pe_T.value)
                        wide = P if u < HA else 64
                        col = (u % 4) * P + hf * 64
                        for kb in range(2 * nb):
                            m = nc.tensor.matmul(ps[:, 7, col:col + wide], pTr[:, kb, :],
                                                 val[:, kb, u * P + hf * 64:u * P + hf * 64 + wide],
                                                 start=(kb == 0), stop=(kb == 2 * nb - 1))
                        m.then_inc(s_PV, 1)

            def pe_product(pe, t, n, bank, first, blocks, k0, k1):
                for k in range(k0, k1):
                    w = first + k - blocks[0]
                    pe.wait_ge(s_wr[w % 4], t * (16 * NW // 4) + 16 * (w // 4) + 16)
                    for c in range(2):
                        m = nc.tensor.matmul(ps[0:n, bank + c, :], pTr[:, k, 0:n], wring[:, w % 4, c * CH:(c + 1) * CH],
                                             start=(k == blocks[0]), stop=(k == blocks[1] - 1))
                    m.then_inc(s_wu, 1)

            def pe_merge(pe, t, piece):
                n = rows_of(t)

                def turn_rows(src):
                    for g in range(2):
                        pe_transposes(pe, [src[0:n, k * P:(k + 1) * P] for k in range(4 * g, 4 * g + 4)], n)

                if piece == "turn_o":
                    if n < P:
                        pe_T.begin(t)
                    pe.wait_ge(s_On, t + 1)
                    turn_rows(o_sb)
                elif piece == "branch_a":
                    pe.wait_ge(s_Tc, pe_T.value)
                    pe_product(pe, t, n, 2, 0, (0, 4), 0, 4)
                elif piece == "branch_b":
                    pe_product(pe, t, n, 4, 4, (4, 8), 4, 8)
                elif piece == "turn_m":
                    pe.wait_ge(s_m, t + 1)
                    turn_rows(mixed)
                elif piece == "out_1":
                    pe.wait_ge(s_Tc, pe_T.value)
                    pe_product(pe, t, n, 2, 8, (0, 8), 0, 4)
                elif piece == "out_2":
                    pe_product(pe, t, n, 2, 8, (0, 8), 4, 8)
                elif piece == "turn_x":
                    pe.wait_ge(s_xn, t + 1)
                    turn_rows(xn_sb)
                elif piece == "query_1":
                    pe.wait_ge(s_Tc, pe_T.value)
                    pe_product(pe, t, n, 4, 16, (0, 8), 0, 4)
                elif piece == "query_2":
                    pe_product(pe, t, n, 4, 16, (0, 8), 4, 8)
                elif piece == "turn_q":
                    pe.wait_ge(s_qc, t + 1)
                    turn_rows(q_sb)
                elif piece == "score":
                    pe.wait_ge(s_Tc, pe_T.value)
                    for h in range(PH):
                        m = nc.tensor.matmul(ps[0:n, 2 + h // 2, (h % 2) * 2 * P:(h % 2 + 1) * 2 * P], pTr[:, h, 0:n],
                                             subkT[:, h, :], start=True, stop=True)
                    m.then_inc(s_sc, 1)

            def turn_of(e, s):
                return e * (NSLOT // R * len(TSUM)) + s // R * len(TSUM) + TSUM.index(s % R)

            def pe_experts(pe, e, k):
                if k == 0:
                    pe.wait_ge(s_yc, e + 1)
                    pe.wait_ge(s_h, e + 1)
                    for c in range(2):
                        m = nc.tensor.matmul(ps[:, c, :], ident[:], h_sb[:, c * CH:(c + 1) * CH], start=True, stop=False)
                    m.then_inc(s_res, 1)
                for s in range(4 * k, 4 * k + 4):
                    if s % R in TSUM:
                        pe.wait_ge(*arrived(e, 1, s))
                        pe.wait_ge(s_diag, turn_of(e, s) + 1)
                        for c in range(2):
                            m = nc.tensor.matmul(ps[:, c, :], diag[:, turn_of(0, s) % NDG, :], ring[:, s % R, c * CH:(c + 1) * CH],
                                                 start=False, stop=(s // R == NSLOT // R - 1 and s % R == TSUM[-1]))
                        m.then_inc(s_sum, 1)

            act_T = Steps(s_Tc, NTB)

            def act_take(act, dst, n):
                act.wait_ge(s_T, act_T.value + 1)
                src = ps[:, 6, 0:dst.shape[1] * P].rearrange("p (k r) -> p k r", r=P)[:, :, 0:n]
                act_T.raised_by(nc.scalar.copy(dst[:, :, 0:n], src))

            def act_attend(act, t, kw):
                nb = kw // P // 2
                act_T.begin(t)
                act.wait_ge(s_route, t)
                act.sem_inc(turn["act"], 1)
                for g in range(2):
                    act.wait_ge(s_T, act_T.value + 1)
                    src = ps[:, 6, :].rearrange("p (u r) -> p u r", r=P)
                    nc.scalar.activation(qz[:, 4 * g:4 * g + 4, 0, :], src, ACT.Copy, scale=half_scale[:, 0:1])
                    act_T.raised_by(nc.scalar.activation(qz[:, 4 * g:4 * g + 4, 1, :], src, ACT.Copy, scale=half_scale[:, 1:2]))
                for u in range(8):
                    if u < HA:
                        for hf in range(2):
                            act.wait_ge(s_nm, t * 8 + 2 * u + hf + 1)
                            nc.scalar.activation(z[:, hf, 0:kw], z[:, hf, 0:kw], ACT.Exp, bias=nm[:, hf:hf + 1],
                                                 accum_out=l[:, hf:hf + 1]).then_inc(s_exp, 1)
                        for j in range(2):
                            act_take(act, pTr[:, j * nb:(j + 1) * nb, :], P)
                    else:
                        v = 4 * (u - HA)
                        for hf in range(2):
                            act.wait_ge(s_Sr[hf], t * 8 + u + 1)
                            nc.scalar.activation(soft[:, hf, 0:kw], z[:, hf, 0:kw], ACT.Abs).then_inc(s_softc, 1)
                        for hf in range(2):
                            act.wait_ge(s_softc, t * 16 + v + hf + 1)
                            nc.scalar.activation(soft[:, hf, 0:kw], soft[:, hf, 0:kw], ACT.Exp, scale=-1.0).then_inc(s_softc, 1)
                        for hf in range(2):
                            act.wait_ge(s_softc, t * 16 + v + hf + 3)
                            nc.scalar.activation(soft[:, hf, 0:kw], soft[:, hf, 0:kw], ACT.Ln, bias=one_t[:]).then_inc(s_soft, 1)
                        for hf in range(2):
                            act.wait_ge(s_w, t * 8 + 2 * (u - HA) + hf + 1)
                            nc.scalar.activation(prob[:, hf, 0:kw], z[:, hf, 0:kw], ACT.Exp).then_inc(s_pB, 1)
                        for j in range(4):
                            act_take(act, pTr[:, (j % 2) * nb:(j % 2 + 1) * nb, :], P)
                    if u % 4 == 3:
                        act.wait_ge(s_PV, t * 12 + (4 if u == 3 else 12))
                        nc.scalar.copy(o_sb[:, (u // 4) * CH:(u // 4 + 1) * CH], ps[:, 7, :]).then_inc(s_Oc, 1)

            def act_merge(act, t, piece):
                n = rows_of(t)

                def take_two():
                    for g in range(2):
                        act_take(act, pTr[:, 4 * g:4 * g + 4, :], n)

                if piece == "norm_o":
                    if n < P:
                        act_T.begin(t)
                    act.wait_ge(s_gin, t * 16 + 16)
                    nc.scalar.activation(gates[0:n, :], gates[0:n, :], ACT.Sigmoid).then_inc(s_sig, 1)
                    act.wait_ge(s_ssh, t + 1)
                    nc.scalar.activation(rmsh[0:n, :], ssh[0:n, :], ACT.Sqrt, bias=eps_t[0:n, :], scale=1.0 / P).then_inc(s_rmsh, 1)
                elif piece in ("turn_o", "turn_m", "turn_x", "turn_q"):
                    take_two()
                elif piece == "residual":
                    act.wait_ge(s_ssx, t + 1)
                    nc.scalar.activation(rmsx[0:n, :], ssx[0:n, :], ACT.Sqrt, bias=eps_t[0:n, :], scale=1.0 / D).then_inc(s_rmsx, 1)
                elif piece == "query_2":
                    act.wait_ge(s_wu, t * NW + 24)
                    nc.scalar.copy(q_sb[0:n, :], both(4)[0:n, :]).then_inc(s_qc, 1)
                elif piece == "gate":
                    act.wait_ge(s_shift, t + 1)
                    nc.scalar.activation(gexp[0:n], gexp[0:n], ACT.Exp).then_inc(s_gexp, 1)

            def act_gelu(act, e):
                n = rows_of(e)
                act.wait_ge(s_dot, e * NSLOT + NSLOT)
                nc.scalar.activation(act_u[0:n, :], dots[0:n, :], ACT.Gelu).then_inc(s_gelu, 1)

            def act_experts(act, e, k):
                if k == 0:
                    act.wait_ge(s_wgt, e + 1)
                    act.sem_inc(turn["act"], 1)
                for s in range(4 * k, 4 * k + 4):
                    if s % R in TSUM:
                        act.wait_ge(s_sum, turn_of(e, s) + 1 - NDG + len(TSUM))
                        nc.scalar.activation(diag[:, turn_of(0, s) % NDG, :], ident[:], ACT.Copy,
                                             scale=wgt[:, s:s + 1]).then_inc(s_diag, 1)

            def act_finish(act, e):
                n = rows_of(e)
                act.wait_ge(s_ssy, e + 1)
                nc.scalar.activation(rmsy[0:n, :], ssy[0:n, :], ACT.Sqrt, bias=eps_t[0:n, :], scale=1.0 / D).then_inc(s_rmsy, 1)

            lk = {"a": Steps(s_adve, 4 * 3 + 4 * 4), "m": Steps(s_mdve, 3), "r": Steps(s_rdve, 21), "f": Steps(s_fdve, 1)}

            def chain(name, instruction):
                lk[name].raised_by(instruction)

            def linked(dve, name):
                dve.wait_ge(lk[name].sem, lk[name].value)
                dve.sem_inc(turn["dve"], 1)

            def dve_attend(dve, t, u, part, kw):
                if u == 0 and part == 0:
                    lk["a"].begin(t)
                    dve.wait_ge(s_wu, t * NW)
                if part == 0:
                    if u < HA:
                        dve.wait_ge(s_bias[u % 2], t * 32 + 16 * (u // 2) + 16)
                    elif u == HA:
                        dve.wait_ge(s_bmask, t * 16 + 16)
                    if u <= HA:
                        dve.wait_ge(s_pA, t * 4 + u)
                        dve.sem_inc(turn["dve"], 1)
                    for hf in range(2):
                        if u == 0 or u > HA:
                            dve.wait_ge(s_pB, t * 8 + (0 if u == 0 else 2 * (u - HA) - 1 + hf))
                            dve.sem_inc(turn["dve"], 1)
                        dve.wait_ge(s_S[hf], t * 8 + u + 1)
                        dve.sem_inc(turn["dve"], 1)
                        src = both(2 + 2 * hf)[:, 0:kw]
                        if u < HA:
                            nc.vector.tensor_tensor_reduce(out=z[:, hf, 0:kw], in0=src, in1=bias[:, u % 2, 0:kw], scale=1.0,
                                                           scalar=LOWEST, op0=ALU.add, op1=ALU.max,
                                                           accum_out=mx[:, hf:hf + 1]).then_inc(s_Sr[hf], 1)
                        else:
                            nc.vector.tensor_tensor(z[:, hf, 0:kw], src, bmask[:, 0:kw], ALU.add).then_inc(s_Sr[hf], 1)
                    if u < HA:
                        for hf in range(2):
                            dve.wait_ge(s_Sr[hf], t * 8 + u + 1)
                            nc.vector.tensor_scalar_mul(nm[:, hf:hf + 1], mx[:, hf:hf + 1], -1.0).then_inc(s_nm, 1)
                elif u < HA:
                    dve.wait_ge(s_exp, t * 8 + 2 * u + 2)
                    chain("a", nc.vector.reciprocal(rl[:], l[:]))
                    linked(dve, "a")
                    chain("a", nc.vector.tensor_scalar_mul(rl2[:], rl[:, 1:2], neg_lam[:]))
                    dve.wait_ge(s_T, t * NTB + 2 * u)
                    chain("a", nc.vector.tensor_scalar_mul(prob[:, u % 2, 0:kw], z[:, 0, 0:kw], rl[:, 0:1]))
                    linked(dve, "a")
                    nc.vector.scalar_tensor_tensor(out=prob[:, u % 2, 0:kw], in0=z[:, 1, 0:kw], scalar=rl2[:],
                                                   in1=prob[:, u % 2, 0:kw], op0=ALU.mult, op1=ALU.add).then_inc(s_pA, 1)
                else:
                    for hf in range(2):
                        dve.wait_ge(s_soft, t * 8 + 2 * (u - HA) + hf + 1)
                        chain("a", nc.vector.scalar_tensor_tensor(out=soft[:, hf, 0:kw], in0=z[:, hf, 0:kw], scalar=0.0,
                                                                  in1=soft[:, hf, 0:kw], op0=ALU.max, op1=ALU.add))
                    for hf in range(2):
                        dve.wait_ge(s_T, t * NTB + 2 * (4 + 2 * (u - HA) + hf))
                        dve.sem_inc(turn["dve"], 1)
                        dve.wait_ge(s_adve, lk["a"].value - 1)
                        m = nc.vector.tensor_tensor_scan(out=prob[:, hf, kw - 1::-1],
                                                         data0=soft[:, hf, kw - 1::-1], data1=soft[:, hf, kw - 1::-1],
                                                         initial=0.0, op0=ALU.add, op1=ALU.bypass)
                        chain("a", m)
                    for hf in range(2):
                        dve.wait_ge(s_adve, lk["a"].value - 1 + hf)
                        nc.vector.tensor_tensor(z[:, hf, 0:kw], z[:, hf, 0:kw], prob[:, hf, 0:kw], ALU.subtract).then_inc(s_w, 1)

            def dve_merge(dve, t, piece):
                n = rows_of(t)
                if piece == "norm_o":
                    lk["m"].begin(t)
                    lk["r"].begin(t)
                    if n == P:
                        dve.wait_ge(s_Oc, t * 2 + 2)
                    else:
                        dve.wait_ge(s_oin, 16)
                    for h in range(HA):
                        cols = slice(h * P, (h + 1) * P)
                        m = nc.vector.tensor_tensor_reduce(out=sq[0:n, cols], in0=o_sb[0:n, cols], in1=o_sb[0:n, cols],
                                                           scale=1.0, scalar=0.0, op0=ALU.mult, op1=ALU.add,
                                                           accum_out=ssh[0:n, h:h + 1])
                    m.then_inc(s_ssh, 1)
                elif piece == "scale_o":
                    dve.wait_ge(s_rmsh, t + 1)
                    chain("m", nc.vector.reciprocal(rsh[0:n, :], rmsh[0:n, :]))
                    linked(dve, "m")
                    for h in range(HA):
                        cols = slice(h * P, (h + 1) * P)
                        m = nc.vector.scalar_tensor_tensor(out=o_sb[0:n, cols], in0=o_sb[0:n, cols], scalar=rsh[0:n, h:h + 1],
                                                           in1=gain_sub[0:n, :], op0=ALU.mult, op1=ALU.mult)
                    m.then_inc(s_On, 1)
                elif piece == "mix":
                    dve.wait_ge(s_sig, t + 1)
                    dve.sem_inc(turn["dve"], 1)
                    dve.wait_ge(s_wu, t * NW + 8)
                    chain("m", nc.vector.tensor_tensor(mixed[0:n, :], both(2)[0:n, :], gates[0:n, 0:D], ALU.mult))
                    chain("m", nc.vector.tensor_tensor(gates[0:n, D:2 * D], both(4)[0:n, :], gates[0:n, D:2 * D], ALU.mult))
                    linked(dve, "m")
                    nc.vector.tensor_tensor(mixed[0:n, :], mixed[0:n, :], gates[0:n, D:2 * D], ALU.add).then_inc(s_m, 1)
                elif piece == "residual":
                    dve.wait_ge(s_wu, t * NW + 16)
                    dve.sem_inc(turn["dve"], 1)
                    dve.wait_ge(s_res, t)
                    dve.sem_inc(turn["dve"], 1)
                    dve.wait_ge(s_xin, t * 16 + 16)
                    nc.vector.tensor_tensor(h_sb[0:n, :], both(2)[0:n, :], x_sb[0:n, :], ALU.add).then_inc(s_h, 1)
                    dve.wait_ge(s_h, t + 1)
                    nc.vector.tensor_tensor_reduce(out=sq[0:n, :], in0=h_sb[0:n, :], in1=h_sb[0:n, :], scale=1.0, scalar=0.0,
                                                   op0=ALU.mult, op1=ALU.add, accum_out=ssx[0:n, :]).then_inc(s_ssx, 1)
                elif piece == "norm_x":
                    dve.wait_ge(s_rmsx, t + 1)
                    chain("r", nc.vector.reciprocal(rsx[0:n, :], rmsx[0:n, :]))
                    linked(dve, "r")
                    nc.vector.scalar_tensor_tensor(out=xn_sb[0:n, :], in0=h_sb[0:n, :], scalar=rsx[0:n, :],
                                                   in1=gain_ffn[0:n, :], op0=ALU.mult, op1=ALU.mult).then_inc(s_xn, 1)
                sc = [ps[0:n, 2 + i // 4, (i % 4) * P:(i % 4 + 1) * P] for i in range(2 * PH)]
                lf = [left[0:n, i * P:(i + 1) * P] for i in range(2 * PH)]
                cd = [cand[0:n, i * 2 * P:(i + 1) * 2 * P] for i in range(PH)]
                lc = [left[0:n, i * 2 * P:(i + 1) * 2 * P] for i in range(PH)]
                if piece == "key_1":
                    dve.wait_ge(s_sc, t + 1)
                    dve.sem_inc(turn["dve"], 1)
                    for i in range(2 * PH):
                        m = nc.vector.max(top[0:n, i, 0:8], sc[i])
                    chain("r", m)
                elif piece == "key_2":
                    linked(dve, "r")
                    for i in range(2 * PH):
                        m = nc.vector.match_replace(lf[i], top[0:n, i, 0:8], sc[i], LOWEST)
                    chain("r", m)
                elif piece == "key_3":
                    for i in range(2 * PH):
                        m = nc.vector.max_index(topi[0:n, i, 0:8], top[0:n, i, 0:8], sc[i])
                    m.then_inc(s_scr, 1)
                elif piece == "key_4":
                    linked(dve, "r")
                    for i in range(2 * PH):
                        m = nc.vector.max(top[0:n, i, 8:16], lf[i])
                    chain("r", m)
                elif piece == "key_5":
                    linked(dve, "r")
                    for i in range(2 * PH):
                        m = nc.vector.max_index(topi[0:n, i, 8:16], top[0:n, i, 8:16], lf[i])
                    chain("r", m)
                elif piece == "pair_1":
                    linked(dve, "r")
                    chain("r", nc.vector.tensor_copy(topf[0:n], topi[0:n]))
                    halves = top[0:n].rearrange("p (h c) a -> p h c a", c=2)
                    chain("r", nc.vector.tensor_tensor(cand[0:n, :].rearrange("p (h k a) -> p h k a", h=PH, k=TK),
                                                       halves[:, :, 0, :].unsqueeze(3).broadcast_to([n, PH, TK, TK]),
                                                       halves[:, :, 1, :].unsqueeze(2).broadcast_to([n, PH, TK, TK]), ALU.add))
                elif piece == "pair_2":
                    linked(dve, "r")
                    for i in range(PH):
                        m = nc.vector.max(best[0:n, i, 0:8], cd[i])
                    chain("r", m)
                elif piece == "pair_3":
                    linked(dve, "r")
                    for i in range(PH):
                        m = nc.vector.match_replace(lc[i], best[0:n, i, 0:8], cd[i], LOWEST)
                    chain("r", m)
                elif piece == "pair_4":
                    for i in range(PH):
                        nc.vector.max_index(bestj[0:n, i * TK:i * TK + 8], best[0:n, i, 0:8], cd[i])
                elif piece == "pair_5":
                    linked(dve, "r")
                    for i in range(PH):
                        m = nc.vector.max(best[0:n, i, 8:16], lc[i])
                    chain("r", m)
                elif piece == "pair_6":
                    linked(dve, "r")
                    for i in range(PH):
                        m = nc.vector.max_index(bestj[0:n, i * TK + 8:(i + 1) * TK], best[0:n, i, 8:16], lc[i])
                    chain("r", m)
                elif piece == "gate":
                    linked(dve, "r")
                    nc.vector.tensor_tensor(gexp[0:n], best[0:n], best[0:n, :, 0:1].broadcast_to([n, PH, TK]),
                                            ALU.subtract).then_inc(s_shift, 1)
                    nc.vector.tensor_scalar(ja[0:n, 0, :], bestj[0:n, :], 4, None, ALU.logical_shift_right)
                    chain("r", nc.vector.tensor_scalar(ja[0:n, 1, :], bestj[0:n, :], 15, None, ALU.bitwise_and))
                    linked(dve, "r")
                    chain("r", nc.vector.tensor_copy(jf[0:n], ja[0:n]))
                elif piece in ("pick_1", "pick_2"):
                    c = int(piece == "pick_2")
                    linked(dve, "r")
                    hot4 = pick[0:n, :].rearrange("p (h k a) -> p h k a", h=PH, k=TK)
                    hot3 = pick[0:n, :].rearrange("p (s a) -> p s a", a=TK)
                    ids = topf[0:n].rearrange("p (h c) a -> p h c a", c=2)[:, :, c, :].unsqueeze(2).broadcast_to([n, PH, TK, TK])
                    chain("r", nc.vector.tensor_tensor(hot3, jf[0:n, c, :].unsqueeze(2).broadcast_to([n, NSLOT, TK]),
                                                       iota16[0:n, :].unsqueeze(1).broadcast_to([n, NSLOT, TK]), ALU.is_equal))
                    linked(dve, "r")
                    chain("r", nc.vector.tensor_tensor(hot4, hot4, ids, ALU.mult))
                    linked(dve, "r")
                    chain("r", nc.vector.tensor_reduce(sel[0:n, c, :], hot3, AX, ALU.add))
                elif piece == "choose":
                    linked(dve, "r")
                    nc.vector.scalar_tensor_tensor(out=idx_u[0:n, :], in0=sel[0:n, 0, :], scalar=float(P), in1=sel[0:n, 1, :],
                                                   op0=ALU.mult, op1=ALU.add)
                    dve.wait_ge(s_gexp, t + 1)
                    chain("r", nc.vector.tensor_reduce(gsum[0:n, :], gexp[0:n], AX, ALU.add))
                    linked(dve, "r")
                    chain("r", nc.vector.reciprocal(grec[0:n, :], gsum[0:n, :]))
                    linked(dve, "r")
                    nc.vector.tensor_tensor(gate[0:n], gexp[0:n], grec[0:n, :].unsqueeze(2).broadcast_to([n, PH, TK]),
                                            ALU.mult).then_inc(s_route, 1)

            def dve_dots(dve, e, g):
                n = rows_of(e)
                for s in range(8 * g, 8 * g + 8):
                    dve.wait_ge(*arrived(e, 0, s))
                    nc.vector.tensor_tensor_reduce(out=ring[0:n, s % R, :], in0=ring[0:n, s % R, :], in1=xn_sb[0:n, :],
                                                   scale=1.0, scalar=0.0, op0=ALU.mult, op1=ALU.add,
                                                   accum_out=dots[0:n, s:s + 1]).then_inc(s_dot, 1)

            def dve_keep_idx(dve, e):
                dve.wait_ge(*summed(e, NSLOT - 1, -(NSLOT // R)))
                dve.wait_ge(*summed(e, NSLOT - 2, -(NSLOT // R)))
                nc.vector.tensor_copy(idx_v[0:rows_of(e), :], idx_u[0:rows_of(e), :]).then_inc(s_idxv, 1)

            def dve_weights(dve, e):
                n = rows_of(e)
                dve.wait_ge(s_gelu, e + 1)
                nc.vector.tensor_tensor(wgt[0:n, :], act_u[0:n, :], gate[0:n].rearrange("p h k -> p (h k)"), ALU.mult).then_inc(s_wgt, 1)

            def dve_experts(dve, e, k):
                n = rows_of(e)
                if k == 0:
                    dve.wait_ge(s_wgt, e + 1)
                    dve.wait_ge(s_yst, e * 16 + 16)
                for s in range(4 * k, 4 * k + 4):
                    if s % R in VSUM:
                        row, w = ring[0:n, s % R, :], wgt[0:n, s:s + 1]
                        dve.wait_ge(*arrived(e, 1, s))
                        if s == VSUM[0]:
                            m = nc.vector.tensor_scalar_mul(y_sb[0:n, :], row, w)
                        else:
                            before_this = s_vsum, summed(e, s)[1] - 1
                            dve.wait_ge(*before_this)
                            m = nc.vector.scalar_tensor_tensor(out=y_sb[0:n, :], in0=row, scalar=w, in1=y_sb[0:n, :],
                                                               op0=ALU.mult, op1=ALU.add)
                        m.then_inc(s_vsum, 1)

            def dve_finish(dve, e, part):
                n = rows_of(e)
                if part == 0:
                    lk["f"].begin(e)
                    dve.wait_ge(*summed(e, NSLOT - R + TSUM[-1]))
                    dve.sem_inc(turn["dve"], 1)
                    dve.wait_ge(*summed(e, NSLOT - R + VSUM[-1]))
                    nc.vector.tensor_tensor(y_sb[0:n, :], both(0)[0:n, :], y_sb[0:n, :], ALU.add).then_inc(s_yc, 1)
                    dve.wait_ge(s_yc, e + 2)
                    nc.vector.tensor_tensor_reduce(out=ysq[0:n, :], in0=y_sb[0:n, :], in1=y_sb[0:n, :], scale=1.0, scalar=0.0,
                                                   op0=ALU.mult, op1=ALU.add, accum_out=ssy[0:n, :]).then_inc(s_ssy, 1)
                else:
                    dve.wait_ge(s_rmsy, e + 1)
                    chain("f", nc.vector.reciprocal(rsy[0:n, :], rmsy[0:n, :]))
                    linked(dve, "f")
                    nc.vector.scalar_tensor_tensor(out=y_sb[0:n, :], in0=y_sb[0:n, :], scalar=rsy[0:n, :], in1=gain_fin[0:n, :],
                                                   op0=ALU.mult, op1=ALU.mult).then_inc(s_y_out, 1)

            PIECES = ("norm_o", "scale_o", "turn_o", "branch_a", "branch_b", "mix", "turn_m", "out_1", "out_2", "residual",
                      "norm_x", "turn_x", "query_1", "query_2", "turn_q", "score", "key_1", "key_2", "key_3", "key_4", "key_5",
                      "pair_1", "pair_2", "pair_3", "pair_4", "pair_5", "pair_6", "gate", "pick_1", "pick_2", "choose", "")

            def tiles_of(eng, step):
                step(0, CH)
                with eng.Fori(1, NPT // 2) as t:
                    step(t, CH)
                with eng.Fori(NPT // 2, NPT) as t:
                    step(t, SEQ)
                step(NPT, None)
                step(NPT + 1, None)

            def before(t):
                return None if isinstance(t, int) and t == 0 else t - 1

            def mixes(t):
                return not (isinstance(t, int) and t > NPT)

            with nc.Block() as block:
                @block.sync
                def _(sp):
                    def step(t, kw):
                        if kw:
                            sync_attend(sp, t, kw)
                        if mixes(t):
                            sync_merge(sp, t)
                        if before(t) is not None:
                            sync_finish(sp, before(t))

                    sp.sem_inc(s_yst, 16)
                    tiles_of(sp, step)
                    sp.wait_ge(s_yst, 16 * (NPT + 2))

                @block.gpsimd
                def _(pool):
                    with pool.Fori(0, NPT) as e:
                        pool_experts(pool, e)
                    pool_experts(pool, NPT)

                @block.tensor
                def _(pe):
                    pe.sem_inc(s_sum, len(TSUM))
                    pe.sem_inc(s_vsum, len(VSUM))
                    pe.sem_inc(s_yc, 1)

                    def step(t, kw):
                        if kw:
                            pe_attend(pe, t, kw)
                        for k, piece in enumerate(PIECES):
                            if mixes(t):
                                pe_merge(pe, t, piece)
                            if before(t) is not None:
                                pe_experts(pe, before(t), k)

                    tiles_of(pe, step)

                @block.scalar
                def _(act):
                    def step(t, kw):
                        if kw:
                            act_attend(act, t, kw)
                        if before(t) is not None:
                            act_gelu(act, before(t))
                        for k, piece in enumerate(PIECES):
                            if before(t) is not None:
                                act_experts(act, before(t), k)
                            if mixes(t):
                                act_merge(act, t, piece)
                        if before(t) is not None:
                            act_finish(act, before(t))

                    tiles_of(act, step)

                @block.vector
                def _(dve):
                    def step(t, kw):
                        for g in range(NSLOT // 8):
                            if before(t) is not None:
                                dve_dots(dve, before(t), g)
                                if g == 8:
                                    dve_keep_idx(dve, before(t))
                            if kw:
                                dve_attend(dve, t, g // 2, g % 2, kw)
                        if before(t) is not None:
                            dve_weights(dve, before(t))
                        for k, piece in enumerate(PIECES):
                            if mixes(t):
                                dve_merge(dve, t, piece)
                            if before(t) is not None:
                                dve_experts(dve, before(t), k)
                        if before(t) is not None:
                            dve_finish(dve, before(t), 0)
                            dve_finish(dve, before(t), 1)

                    tiles_of(dve, step)



OUTS = [(1, SEQ, D), (NB_DEC, TD, D),
        (1, 1, SEQ, HA, 128), (1, 1, SEQ, HA, 128), (1, 1, SEQ, HB, 64), (1, 1, SEQ, HB, 64),
        (1, NB_DEC, TD, HA, 128), (1, NB_DEC, TD, HA, 128), (1, NB_DEC, TD, HB, 64), (1, NB_DEC, TD, HB, 64)]


def kernel(**inputs):
    import concourse.bacc as bacc
    from concourse.bass_utils import run_bass_kernel_spmd

    nc = bacc.Bacc("TRN2", target_bir_lowering=False, num_devices=1)
    arrays, args = {}, {}
    given = {name: np.ascontiguousarray(v) for name, v in inputs.items()}
    given["distance_onehot"] = distance_onehot()
    given["mask_rows"] = mask_rows()
    for name, v in given.items():
        arrays[f"in_{name}"] = v
        args[name] = nc.dram_tensor(f"in_{name}", v.shape, mybir.dt.from_np(v.dtype), kind="ExternalInput").ap()
    outs = [nc.dram_tensor(f"out_{n}", shape, F32, kind="ExternalOutput").ap() for n, shape in enumerate(OUTS)]
    build(nc, args, outs)
    r = run_bass_kernel_spmd(nc, [arrays], core_ids=[0])
    return tuple(r.results[0][f"out_{n}"] for n in range(len(OUTS)))
```

```python
from contextlib import ExitStack

import numpy as np

import concourse.bass as bass
from concourse import mybir

F32 = mybir.dt.float32
U32 = mybir.dt.uint32
I32 = mybir.dt.int32
ALU = mybir.AluOpType
ACT = mybir.ActivationFunctionType
AX = mybir.AxisListType.X
ds = bass.ds

P = 128
D = 1024
KD = D // P
NPT = 8
NS = 64
SEQ = NPT * P
T = SEQ + NS
W_IN = 5120
CH = 512
NCH = W_IN // CH
HA = 4
HB = 8
NB_DEC = 8
TD = 8
SLABW = 2 * SEQ - P
PAGES = 2
PAST = PAGES * P
KS = PAST + TD
PH = 8
TK = 16
NSLOT = PH * TK
R = 8
NDG = 4
VSUM = (1, 3, 5, 7)
TSUM = tuple(r for r in range(R) if r not in VSUM)
BUCKETS = 32
MAXD = 128
EPS = 1e-6
QA, KA, VA, QB, KB, VB, GA, GB = 0, 512, 1024, 1536, 2048, 2560, 3072, 4096
NEG = -1e30
LOWEST = -3.0e38
LAM_INIT = 0.2
RELW = 2 * SEQ


def distance_onehot():
    rel = (SEQ - 1) - np.arange(RELW)
    n = np.maximum(rel, 0)
    exact = BUCKETS // 2
    ratio = np.log(np.maximum(n, 1).astype(np.float32) / np.float32(exact)) / np.float32(np.log(MAXD / exact))
    large = np.minimum(exact + (ratio * (BUCKETS - exact)).astype(np.int32), BUCKETS - 1)
    bucket = np.where(n < exact, n, large)
    hot = np.zeros((BUCKETS + 2, RELW), np.float32)
    hot[bucket, np.arange(RELW)] = 1.0
    hot[BUCKETS, rel < 0] = 1.0
    hot[BUCKETS + 1, rel == 0] = 1.0
    return hot


def mask_rows():
    rows = np.zeros((BUCKETS + 2, HA + 1), np.float32)
    rows[BUCKETS, :] = NEG
    rows[BUCKETS + 1, HA] = NEG
    return rows


def build(nc, a, o):
    ctx = ExitStack()
    nc.disable_value_cache = True

    def dram(name, shape):
        return nc.dram_tensor(name, shape, F32, kind="Internal").ap()

    def semaphore(name):
        return ctx.enter_context(nc.semaphore(name))

    proj_d = dram("proj_d", (T, W_IN))
    attn_d = dram("attn_d", (NS, D))
    h_d = dram("h_d", (T, D))
    dist_d = dram("dist_d", (HA + 1, RELW))
    slab_d = dram("slab_d", (HA + 1, P, SLABW))

    x_all = [a["x_prompt"].rearrange("b s d -> (b s) d"), a["x_sample"].rearrange("b s d -> (b s) d")]
    w_in = a["w_in"][0].rearrange("(k p) n -> p k n", p=P)
    y_out = [o[0].rearrange("b s d -> (b s) d"), o[1].rearrange("b s d -> (b s) d")]
    kv_out = [[o[n].rearrange("l b s h e -> (l b s) (h e)") for n in group] for group in ((2, 3, 4, 5), (6, 7, 8, 9))]

    with ctx:
        ps = ctx.enter_context(nc.psum_tensor("ps", [P, 8, CH], F32))

        def both(b):
            return ps[:, b:b + 2, :].rearrange("p b c -> p (b c)")

        def keep(name, shape, dt=F32):
            return ctx.enter_context(nc.sbuf_tensor(name, shape, dt))

        ident = keep("ident", [P, P])
        gain_mix = keep("gain_mix", [P, D])
        gain_ffn = keep("gain_ffn", [P, D])
        gain_fin = keep("gain_fin", [P, D])
        gain_sub = keep("gain_sub", [P, P])
        neg_lam = keep("neg_lam", [P, 1])
        eps_t = keep("eps_t", [P, 1])
        one_t = keep("one_t", [P, 1])
        subkT = keep("subkT", [P, PH, 2 * P])
        iota16 = keep("iota16", [P, TK])
        half_scale = keep("half_scale", [P, 2])

        with ExitStack() as stage:
            def sb(name, shape, dt=F32):
                return stage.enter_context(nc.sbuf_tensor(name, shape, dt))

            hot = sb("hot", [BUCKETS + 2, RELW])
            table = sb("table", [BUCKETS + 2, HA + 1])
            dist = sb("dist", [HA + 1, RELW])
            lams = sb("lams", [P, 4, 64])
            prod = sb("prod", [P, 2, 64])
            dots = sb("dots", [P, 2])
            expd = sb("expd", [P, 2])
            diff = sb("diff", [P, 1])
            subk = sb("subk", [P, PH, 2, 64])
            s_mask = semaphore("c_mask")
            s_gain = semaphore("c_gain")
            s_lam = semaphore("c_lam")
            s_subk = semaphore("c_subk")
            s_tab = semaphore("c_tab")
            s_ident = semaphore("c_ident")
            s_zero = semaphore("c_zero")
            s_dot = semaphore("c_dot")
            s_exp = semaphore("c_exp")
            s_link = semaphore("c_link")
            s_dist = semaphore("c_dist")
            s_dcopy = semaphore("c_dcopy")
            s_skT = semaphore("c_skT")
            s_skc = semaphore("c_skc")
            s_store = semaphore("c_store")

            with nc.Block() as block:
                @block.sync
                def _(sp):
                    sp.dma_start(table[:], a["mask_rows"]).then_inc(s_mask, 16)
                    sp.dma_start(hot[:], a["distance_onehot"]).then_inc(s_tab, 16)
                    sp.wait_ge(s_mask, 16)
                    sp.dma_start(table[0:BUCKETS, 0:HA], a["rel_bias"], allow_slow_non_contiguous=True).then_inc(s_tab, 16)
                    sp.dma_start(subk[:], a["peer_sub_keys"][0].rearrange("h c n e -> n h c e")).then_inc(s_subk, 16)
                    for n, name in enumerate(("lambda_q1", "lambda_k1", "lambda_q2", "lambda_k2")):
                        sp.dma_start(lams[:, n, :], a[name][0:1, :].broadcast_to([P, 64])).then_inc(s_lam, 16)
                    sp.dma_start(gain_mix[:], a["norm_mix"][0:1, :].broadcast_to([P, D])).then_inc(s_gain, 16)
                    sp.dma_start(gain_ffn[:], a["norm_ffn"][0:1, :].broadcast_to([P, D])).then_inc(s_gain, 16)
                    sp.dma_start(gain_fin[:], a["norm_final"].rearrange("(o d) -> o d", o=1).broadcast_to([P, D])).then_inc(s_gain, 16)
                    sp.dma_start(gain_sub[:], a["subln_gain"][0:1, :].broadcast_to([P, P])).then_inc(s_gain, 16)
                    sp.wait_ge(s_dcopy, 4)
                    sp.dma_start(dist_d[:, :], dist[:]).then_inc(s_store, 16)
                    sp.wait_ge(s_store, 16)
                    sp.wait_ge(s_gain, 64)

                @block.gpsimd
                def _(pool):
                    pool.memset(ident[:], 0.0).then_inc(s_zero, 1)
                    pool.memset(subkT[:], 0.0).then_inc(s_zero, 1)
                    pool.memset(eps_t[:], EPS).then_inc(s_zero, 1)
                    pool.memset(one_t[:], 1.0).then_inc(s_zero, 1)
                    pool.iota(iota16[:], pattern=[[1, TK]], base=0, channel_multiplier=0,
                              allow_small_or_imprecise_dtypes=True).then_inc(s_zero, 1)
                    pool.wait_ge(s_zero, 1)
                    pool.affine_select(out=ident[:], in_=ident[:], compare_op=ALU.not_equal, fill=1.0,
                                       base=0, pattern=[[-1, P]], channel_multiplier=1).then_inc(s_ident, 1)

                @block.tensor
                def _(pe):
                    pe.wait_ge(s_tab, 32)
                    for c in range(4):
                        nc.tensor.matmul(ps[0:HA + 1, c, :], table[:], hot[:, c * CH:(c + 1) * CH],
                                         start=True, stop=True).then_inc(s_dist, 1)
                    pe.wait_ge(s_ident, 1)
                    pe.wait_ge(s_subk, 16)
                    for h in range(PH):
                        nc.tensor.transpose(ps[:, 4 + h // 4, (h % 4) * P:(h % 4 + 1) * P],
                                            subk[:, h].rearrange("n c e -> n (c e)"), ident[:]).then_inc(s_skT, 1)

                @block.vector
                def _(dve):
                    for m in range(2):
                        nc.vector.memset(half_scale[64 * m:64 * m + 64, m:m + 1], 0.125)
                        nc.vector.memset(half_scale[64 * m:64 * m + 64, 1 - m:2 - m], 0.0)
                    for c in range(4):
                        dve.wait_ge(s_dist, c + 1)
                        nc.vector.tensor_copy(dist[:, c * CH:(c + 1) * CH], ps[0:HA + 1, c, :]).then_inc(s_dcopy, 1)
                    dve.wait_ge(s_lam, 64)
                    for n in range(2):
                        nc.vector.tensor_tensor_reduce(out=prod[:, n, :], in0=lams[:, 2 * n, :], in1=lams[:, 2 * n + 1, :],
                                                       scale=1.0, scalar=0.0, op0=ALU.mult, op1=ALU.add,
                                                       accum_out=dots[:, n:n + 1]).then_inc(s_dot, 1)
                    dve.wait_ge(s_exp, 1)
                    nc.vector.tensor_tensor(diff[:], expd[:, 1:2], expd[:, 0:1], ALU.subtract).then_inc(s_link, 1)
                    dve.wait_ge(s_link, 1)
                    nc.vector.tensor_scalar_add(neg_lam[:], diff[:], -LAM_INIT).then_inc(s_link, 1)
                    dve.wait_ge(s_gain, 64)
                    nc.vector.tensor_scalar_mul(gain_sub[:], gain_sub[:], 1.0 - LAM_INIT).then_inc(s_link, 1)
                    dve.wait_ge(s_skT, PH)
                    dve.wait_ge(s_zero, 2)
                    for half in range(2):
                        rows = slice(64 * half, 64 * half + 64)
                        nc.vector.tensor_copy(subkT[rows, :, half * P:(half + 1) * P],
                                              both(4)[rows, :].rearrange("p (h n) -> p h n", n=P)).then_inc(s_skc, 1)

                @block.scalar
                def _(act):
                    act.wait_ge(s_dot, 2)
                    nc.scalar.activation(expd[:], dots[:], ACT.Exp).then_inc(s_exp, 1)

        with ExitStack() as stage:
            def sb(name, shape, dt=F32):
                return stage.enter_context(nc.sbuf_tensor(name, shape, dt))

            xnT = sb("xnT", [P, KD, T])
            wbuf = sb("wbuf", [P, 2, KD, CH])
            xin = sb("xin", [P, 2, D])
            xn = sb("xn", [P, 2, D])
            sq = sb("sq", [P, D])
            ssum = sb("ssum", [P, 2])
            rms = sb("rms", [P, 2])
            rstd = sb("rstd", [P, 2])
            pout = sb("pout", [P, 3, CH])
            s_x = [semaphore(f"p_x{n}") for n in range(2)]
            s_w = [semaphore(f"p_w{n}") for n in range(2)]
            s_sum = semaphore("p_sum")
            s_rms = semaphore("p_rms")
            s_rstd = semaphore("p_rstd")
            s_xn = semaphore("p_xn")
            s_xT = semaphore("p_xT")
            s_xTc = semaphore("p_xTc")
            s_mm = semaphore("p_mm")
            s_ev = semaphore("p_ev")
            s_st = [semaphore(f"p_st{n}") for n in range(3)]
            s_turn_pool = semaphore("p_turn_pool")
            s_turn_act = semaphore("p_turn_act")

            tiles = [(t, P) for t in range(NPT)] + [(NPT, NS)]
            NT = len(tiles)

            with nc.Block() as block:
                def load_x(sp, t):
                    src = x_all[0][t * P:(t + 1) * P, :] if t < NPT else x_all[1]
                    sp.dma_start(xin[0:tiles[t][1], t % 2, :], src).then_inc(s_x[t % 2], 16)

                @block.sync
                def _(sp):
                    load_x(sp, 0)
                    load_x(sp, 1)
                    for n in range(2):
                        sp.dma_start(wbuf[:, n], w_in[:, :, n * CH:(n + 1) * CH]).then_inc(s_w[n], 16)
                    for t in range(2, NT):
                        sp.wait_ge(s_xn, t - 1)
                        load_x(sp, t)
                    with sp.Fori(0, NCH // 2 - 1) as i:
                        for n in range(2):
                            src = sp.snap(i * (2 * CH) + (2 + n) * CH)
                            sp.wait_ge(s_mm, i * (2 * NT) + (n + 1) * NT)
                            sp.dma_start(wbuf[:, n], w_in[:, :, ds(src, CH)]).then_inc(s_w[n], 16)

                @block.gpsimd
                def _(pool):
                    with pool.Fori(0, NCH // 2) as i:
                        for c in range(2):
                            for t, rows in tiles:
                                k = c * NT + t
                                col = pool.snap(i * (2 * CH) + c * CH)
                                pool.wait_ge(s_ev, i * (2 * NT) + k + 1)
                                pool.sem_inc(s_turn_pool, 1)
                                pool.dma_start(proj_d[t * P:t * P + rows, ds(col, CH)],
                                               pout[0:rows, k % 3, :]).then_inc(s_st[k % 3], 16)
                    for n in range(3):
                        pool.wait_ge(s_st[n], 16 * NCH * NT // 3)

                @block.vector
                def _(dve):
                    for t, rows in tiles:
                        b = t % 2
                        dve.wait_ge(s_x[b], 16 * (t // 2 + 1))
                        if t:
                            dve.wait_ge(s_sum, t)
                        nc.vector.tensor_tensor_reduce(out=sq[0:rows, :], in0=xin[0:rows, b, :], in1=xin[0:rows, b, :],
                                                       scale=1.0, scalar=0.0, op0=ALU.mult, op1=ALU.add,
                                                       accum_out=ssum[0:rows, b:b + 1]).then_inc(s_sum, 1)
                        dve.wait_ge(s_rms, t + 1)
                        nc.vector.reciprocal(rstd[0:rows, b:b + 1], rms[0:rows, b:b + 1]).then_inc(s_rstd, 1)
                        dve.wait_ge(s_rstd, t + 1)
                        if t >= 2:
                            dve.wait_ge(s_xT, 2 * (t - 1))
                        nc.vector.scalar_tensor_tensor(out=xn[0:rows, b, :], in0=xin[0:rows, b, :],
                                                       scalar=rstd[0:rows, b:b + 1], in1=gain_mix[0:rows, :],
                                                       op0=ALU.mult, op1=ALU.mult).then_inc(s_xn, 1)

                @block.scalar
                def _(act):
                    for t, rows in tiles:
                        b = t % 2
                        act.wait_ge(s_sum, t + 1)
                        nc.scalar.activation(rms[0:rows, b:b + 1], ssum[0:rows, b:b + 1], ACT.Sqrt,
                                             bias=eps_t[0:rows, :], scale=1.0 / D).then_inc(s_rms, 1)
                        for g in range(2):
                            act.wait_ge(s_xT, 2 * t + g + 1)
                            nc.scalar.copy(xnT[:, 4 * g:4 * g + 4, t * P:t * P + rows],
                                           ps[:, g, :].rearrange("p (k r) -> p k r", r=P)[:, :, 0:rows]).then_inc(s_xTc, 1)

                    def take(c, i):
                        for t, rows in tiles:
                            k = c * NT + t
                            act.wait_ge(s_mm, i * (2 * NT) + k + 1)
                            act.sem_inc(s_turn_act, 1)
                            if k >= 3 or not isinstance(i, int):
                                act.wait_ge(s_st[k % 3], i * (16 * 2 * NT // 3) + 16 * (k // 3))
                            nc.scalar.copy(pout[0:rows, k % 3, :], ps[0:rows, k % 6 + 2, :]).then_inc(s_ev, 1)

                    for c in range(2):
                        take(c, 0)
                    with act.Fori(1, NCH // 2) as i:
                        for c in range(2):
                            take(c, i)

                @block.tensor
                def _(pe):
                    for t, rows in tiles:
                        pe.wait_ge(s_xn, t + 1)
                        for g in range(2):
                            if t:
                                pe.wait_ge(s_xTc, 2 * (t - 1) + g + 1)
                            for k in range(4):
                                kt = 4 * g + k
                                m = nc.tensor.transpose(ps[:, g, k * P:k * P + rows],
                                                        xn[0:rows, t % 2, kt * P:(kt + 1) * P], ident[0:rows, 0:rows])
                            m.then_inc(s_xT, 1)
                    pe.wait_ge(s_xTc, 2 * NT)

                    def chunk(c, i, after):
                        pe.wait_ge(s_w[c], i * 16 + 16)
                        for t, rows in tiles:
                            k = c * NT + t
                            if after is not None:
                                pe.wait_ge(s_ev, after + k - 5)
                            elif k >= 6:
                                pe.wait_ge(s_ev, k - 5)
                            for kt in range(KD):
                                m = nc.tensor.matmul(ps[0:rows, k % 6 + 2, :], xnT[:, kt, t * P:t * P + rows],
                                                     wbuf[:, c, kt, :], start=(kt == 0), stop=(kt == KD - 1))
                            m.then_inc(s_mm, 1)

                    for c in range(2):
                        chunk(c, 0, None)
                    with pe.Fori(1, NCH // 2) as i:
                        for c in range(2):
                            chunk(c, i, i * (2 * NT))

        keyT = keep("keyT", [P, KD, SEQ])
        val = keep("val", [P, NPT, D])
        with ExitStack() as stage:
            kst = stage.enter_context(nc.sbuf_tensor("kst", [P, 2, D], F32))
            flip = stage.enter_context(nc.sbuf_tensor("flip", [P, P], F32))
            climb = stage.enter_context(nc.sbuf_tensor("climb", [P, HA + 1, SLABW], F32))
            slab = stage.enter_context(nc.sbuf_tensor("slab", [P, HA + 1, SLABW], F32))
            QW = SLABW // 4
            s_climb = semaphore("k_climb")
            s_flip = semaphore("k_flip")
            s_mm = semaphore("k_mm")
            s_slab = semaphore("k_slab")
            s_slab_out = semaphore("k_slab_out")
            s_v = semaphore("k_v")
            s_k = [semaphore(f"k_k{n}") for n in range(2)]
            s_kT = semaphore("k_kT")
            s_kTc = semaphore("k_kTc")
            s_out = semaphore("k_out")

            with nc.Block() as block:
                @block.sync
                def _(sp):
                    for r in range(HA + 1):
                        sp.dma_start(climb[:, r, :], bass.AP(tensor=dist_d.tensor, offset=r * RELW,
                                                             ap=[[1, P], [1, SLABW]])).then_inc(s_climb, 16)
                    for t in range(NPT):
                        b = t % 2
                        if t >= 2:
                            sp.wait_ge(s_kT, 2 * (t - 1))
                        for n, col in enumerate((KA, KB)):
                            sp.dma_start(kst[:, b, n * CH:(n + 1) * CH],
                                         proj_d[t * P:(t + 1) * P, col:col + CH]).then_inc(s_k[b], 16)
                    sp.wait_ge(s_slab, 4 * (HA + 1))
                    sp.dma_start(slab_d.rearrange("r p c -> p r c"), slab[:]).then_inc(s_slab_out, 16)
                    sp.wait_ge(s_slab_out, 16)

                @block.gpsimd
                def _(pool):
                    pool.memset(flip[:], 0.0).then_inc(s_flip, 1)
                    pool.wait_ge(s_flip, 1)
                    pool.affine_select(out=flip[:], in_=flip[:], compare_op=ALU.not_equal, fill=1.0,
                                       base=1 - P, pattern=[[1, P]], channel_multiplier=1).then_inc(s_flip, 1)
                    for n, col in enumerate((VA, VB)):
                        pool.dma_start(val[:, :, n * CH:(n + 1) * CH],
                                       proj_d[0:SEQ, col:col + CH].rearrange("(t p) c -> p t c", p=P)).then_inc(s_v, 16)
                    for group, (r0, r1) in zip(kv_out, ((0, SEQ), (SEQ, T))):
                        for dst, col in zip(group, (KA, VA, KB, VB)):
                            pool.dma_start(dst, proj_d[r0:r1, col:col + CH]).then_inc(s_out, 16)
                    pool.wait_ge(s_v, 32)
                    pool.wait_ge(s_out, 16 * 8)

                @block.tensor
                def _(pe):
                    for t in range(NPT):
                        pe.wait_ge(s_k[t % 2], 32 * (t // 2 + 1))
                        for g in range(2):
                            if t:
                                pe.wait_ge(s_kTc, 2 * (t - 1) + g + 1)
                            for k in range(4):
                                u = 4 * g + k
                                m = nc.tensor.transpose(ps[:, g, k * P:(k + 1) * P],
                                                        kst[:, t % 2, u * P:(u + 1) * P], ident[:])
                            m.then_inc(s_kT, 1)
                    pe.wait_ge(s_flip, 2)
                    pe.wait_ge(s_climb, 16 * (HA + 1))
                    for n in range(4 * (HA + 1)):
                        if n >= 4:
                            pe.wait_ge(s_slab, n - 3)
                        c = (n % 4) * QW
                        nc.tensor.matmul(ps[:, 2 + n % 4, 0:QW], flip[:], climb[:, n // 4, c:c + QW],
                                         start=True, stop=True).then_inc(s_mm, 1)

                @block.vector
                def _(dve):
                    for n in range(4 * (HA + 1)):
                        dve.wait_ge(s_mm, n + 1)
                        c = (n % 4) * QW
                        nc.vector.tensor_copy(slab[:, n // 4, c:c + QW], ps[:, 2 + n % 4, 0:QW]).then_inc(s_slab, 1)

                @block.scalar
                def _(act):
                    for t in range(NPT):
                        for g in range(2):
                            act.wait_ge(s_kT, 2 * t + g + 1)
                            nc.scalar.copy(keyT[:, 4 * g:4 * g + 4, t * P:(t + 1) * P],
                                           ps[:, g, :].rearrange("p (u r) -> p u r", r=P)).then_inc(s_kTc, 1)

        with ExitStack() as stage:
            def sb(name, shape, dt=F32):
                return stage.enter_context(nc.sbuf_tensor(name, shape, dt))

            ring = sb("t_ring", [P, R, D])
            big = sb("t_big", [P, 11, D])
            pTr = sb("t_pTr", [P, KD, P])
            o_sb = sb("t_o_sb", [P, D])
            h_sb = sb("t_h_sb", [P, D])
            xn_sb = sb("t_xn_sb", [P, D])
            y_sb = sb("t_y_sb", [P, D])

            def slots(n, m):
                return big[:, n:m, :].rearrange("p a c -> p (a c)")

            bias = big[:, 0:2, :]
            bmask = big[:, 2, :]
            z = big[:, 3:5, :]
            soft = big[:, 5:7, :]
            prob = big[:, 7:9, :]
            qz = slots(9, 11).rearrange("p (u m r) -> p u m r", m=2, r=P)
            x_sb = big[:, 0, :]
            sq = big[:, 1, :]
            wring = big[:, 3:7, :]
            mixed = big[:, 7, :]
            gates = slots(9, 11)
            q_sb = big[:, 8, :]
            left = slots(9, 11)
            cand = slots(7, 9)
            pick = slots(0, 2)
            ysq = big[:, 8, :]
            mx = sb("t_mx", [P, 2])
            nm = sb("t_nm", [P, 2])
            l = sb("t_l", [P, 2])
            rl = sb("t_rl", [P, 2])
            rl2 = sb("t_rl2", [P, 1])
            ssh, rmsh, rsh = (sb("t_" + n, [P, HA]) for n in ("ssh", "rmsh", "rsh"))
            ssx, rmsx, rsx = (sb("t_" + n, [P, 1]) for n in ("ssx", "rmsx", "rsx"))
            ssy, rmsy, rsy = (sb("t_" + n, [P, 1]) for n in ("ssy", "rmsy", "rsy"))
            top = sb("t_top", [P, 2 * PH, TK])
            topi = sb("t_topi", [P, 2 * PH, TK], U32)
            topf = sb("t_topf", [P, 2 * PH, TK])
            best = sb("t_best", [P, PH, TK])
            bestj = sb("t_bestj", [P, NSLOT], U32)
            ja = sb("t_ja", [P, 2, NSLOT], U32)
            jf = sb("t_jf", [P, 2, NSLOT])
            sel = sb("t_sel", [P, 2, NSLOT])
            idx_u = sb("t_idx_u", [P, NSLOT], U32)
            idx_v = sb("t_idx_v", [P, NSLOT], U32)
            gexp = sb("t_gexp", [P, PH, TK])
            gsum = sb("t_gsum", [P, PH])
            grec = sb("t_grec", [P, PH])
            gate = sb("t_gate", [P, PH, TK])
            dots = sb("t_dots", [P, NSLOT])
            act_u = sb("t_act_u", [P, NSLOT])
            wgt = sb("t_wgt", [P, NSLOT])
            diag = sb("t_diag", [P, NDG, P])

            s_qin = semaphore("a_qin")
            s_bias = [semaphore(f"a_bias{n}") for n in range(2)]
            s_bmask = semaphore("a_bmask")
            s_S = [semaphore(f"a_S{n}") for n in range(2)]
            s_Sr = [semaphore(f"a_Sr{n}") for n in range(2)]
            s_nm = semaphore("a_nm")
            s_exp = semaphore("a_exp")
            s_softc = semaphore("a_softc")
            s_soft = semaphore("a_soft")
            s_w = semaphore("a_w")
            s_pA = semaphore("a_pA")
            s_pB = semaphore("a_pB")
            s_T = semaphore("t_full")
            s_Tc = semaphore("t_taken")
            s_PV = semaphore("a_PV")
            s_Oc = semaphore("a_Oc")
            s_oin = semaphore("m_oin")
            s_adve = semaphore("a_dve")
            s_gin = semaphore("m_gin")
            s_xin = semaphore("m_xin")
            s_wr = [semaphore(f"m_wr{n}") for n in range(4)]
            s_wu = semaphore("m_wu")
            s_sig = semaphore("m_sig")
            s_ssh = semaphore("m_ssh")
            s_rmsh = semaphore("m_rmsh")
            s_mdve = semaphore("m_dve")
            s_On = semaphore("m_On")
            s_m = semaphore("m_m")
            s_h = semaphore("m_h")
            s_ssx = semaphore("r_ssx")
            s_rmsx = semaphore("r_rmsx")
            s_rdve = semaphore("r_dve")
            s_xn = semaphore("r_xn")
            s_qc = semaphore("r_qc")
            s_sc = semaphore("r_sc")
            s_scr = semaphore("r_scr")
            s_route = semaphore("r_route")
            s_shift = semaphore("r_shift")
            s_gexp = semaphore("r_gexp")
            s_idx = semaphore("r_idx")
            s_ring = [semaphore(f"e_ring{n}") for n in range(R)]
            s_dot = semaphore("e_dot")
            s_sum = semaphore("e_sum")
            s_vsum = semaphore("e_vsum")
            s_idxv = semaphore("e_idxv")
            s_gelu = semaphore("e_gelu")
            s_wgt = semaphore("e_wgt")
            s_diag = semaphore("e_diag")
            s_res = semaphore("e_res")
            s_yc = semaphore("f_yc")
            s_ssy = semaphore("f_ssy")
            s_rmsy = semaphore("f_rmsy")
            s_fdve = semaphore("f_dve")
            s_y_out = semaphore("f_y")
            s_yst = semaphore("f_yst")
            turn = {n: semaphore(f"turn_{n}") for n in ("sync", "pool", "act", "dve")}

            room_k = keyT[:].rearrange("p u k -> p (u k)")
            room_v = val[:].rearrange("p t c -> p (t c)")
            taken_cols = {}

            def part(room, name, shape):
                cols = int(np.prod(shape[1:]))
                first = taken_cols.get(name, 0)
                taken_cols[name] = first + cols
                assert taken_cols[name] <= KD * SEQ
                flat = room[0:shape[0], first:first + cols]
                if len(shape) == 3:
                    return flat.rearrange("p (a b) -> p a b", b=shape[2])
                if len(shape) == 4:
                    return flat.rearrange("p (a b c) -> p a b c", b=shape[2], c=shape[3])
                return flat

            kpage = part(room_k, "k", (P, PAGES, D))
            vpage = part(room_k, "k", (P, 2, PAGES, D))
            qk = part(room_k, "k", (NS, 2, D))
            oa, ob = qk[0:HA * TD, 0, 0:CH], qk[0:HB * TD, 0, CH:D]
            vnew = part(room_v, "v", (TD, 2, D))
            kT = part(room_v, "v", (P, KD, KS))
            qblk = part(room_v, "v", (P, KD, P + TK))
            qblk_flat = qblk.rearrange("p u c -> p (u c)")
            qT = part(room_v, "v", (P, KD, NS))
            knT = part(room_v, "v", (P, KD, NS))
            smask = part(room_v, "v", (P, KS))
            ss_ = part(room_v, "v", (P, KS))
            se_ = part(room_v, "v", (P, KS))
            sw_ = part(room_v, "v", (P, KS))
            pT = part(room_v, "v", (P, 3, P))
            pd = part(room_v, "v", (P, 3, HA * TD))
            smx, snm, sl_, srl = mx[:, 0:1], nm[:, 0:1], l[:, 0:1], rl[:, 0:1]
            pages = sb("t_pages", [1, NB_DEC * PAGES], I32)
            d_qk = semaphore("d_qk")
            d_pt = semaphore("d_pt")
            d_mask = semaphore("d_mask")
            d_page = semaphore("d_page")
            d_val = [semaphore(f"d_val{n}") for n in range(2)]
            d_zero = semaphore("d_zero")
            d_qT = semaphore("d_qT")
            d_qTc = semaphore("d_qTc")
            d_blk = semaphore("d_blk")
            d_kT = semaphore("d_kT")
            d_kTc = semaphore("d_kTc")
            d_S = semaphore("d_S")
            d_Sr = semaphore("d_Sr")
            d_act = semaphore("d_act")
            d_dve = semaphore("d_dve")
            d_prob = semaphore("d_prob")
            d_T = semaphore("d_T")
            d_Tc = semaphore("d_Tc")
            d_new = semaphore("d_new")
            d_pd = semaphore("d_pd")
            d_O = semaphore("d_O")
            d_Oc = semaphore("d_Oc")
            d_store = semaphore("d_store")
            A, B = slice(0, HA * 2 * TD), slice(HA * 2 * TD, P)
            KC = (P, P, TD)
            pools = [a[n][0].rearrange("n p h e -> n p (h e)") for n in
                     ("cache_k_diff", "cache_k_sb", "cache_v_diff", "cache_v_sb")]
            last_page = pools[0].shape[0] - 1


            NTB = 34
            NW = 24

            class Steps:

                def __init__(self, sem, per):
                    self.sem, self.per, self.k, self.t = sem, per, 0, 0

                def begin(self, t):
                    self.t, self.k = t, 0

                def raised_by(self, instruction):
                    instruction.then_inc(self.sem, 1)
                    self.k += 1

                @property
                def value(self):
                    return self.t * self.per + self.k

            def tile(t):
                return slice(t * P, t * P + P) if isinstance(t, int) else ds(t * P, P)

            def rows_of(t):
                return NS if isinstance(t, int) and t == NPT else P

            def window(row, t, kw):
                first = SLABW - SEQ - t * P
                return slab_d[row, :, first:first + kw] if isinstance(t, int) else slab_d[row, :, ds(first, kw)]

            def sync_attend(sp, t, kw):
                rows = tile(t)
                if not (isinstance(t, int) and t == 0):
                    sp.wait_ge(s_T, (t - 1) * NTB + (28))
                    sp.sem_inc(turn["sync"], 1)
                for n, col in enumerate((QA, QB)):
                    sp.dma_start(o_sb[:, n * CH:(n + 1) * CH], proj_d[rows, col:col + CH]).then_inc(s_qin, 16)
                wins = [window(u, t, kw) for u in range(HA + 1)]
                sp.wait_ge(s_route, t)
                sp.sem_inc(turn["sync"], 1)
                for u in range(HA):
                    if u >= 2:
                        sp.wait_ge(s_Sr[1], t * 8 + u - 1)
                        sp.sem_inc(turn["sync"], 1)
                    sp.dma_start(bias[:, u % 2, 0:kw], wins[u]).then_inc(s_bias[u % 2], 16)
                    if u == 1:
                        sp.dma_start(bmask[:, 0:kw], wins[HA]).then_inc(s_bmask, 16)

            def sync_merge(sp, t):
                n_rows = rows_of(t)
                if n_rows == P:
                    x_src, g_src = x_all[0][tile(t), :], proj_d[tile(t), GA:W_IN]
                    sp.wait_ge(s_S[1], t * 8 + 8)
                    sp.sem_inc(turn["sync"], 1)
                    sp.dma_start(gates[:], g_src).then_inc(s_gin, 16)
                    sp.wait_ge(s_Sr[1], t * 8 + 3)
                    sp.sem_inc(turn["sync"], 1)
                    sp.dma_start(x_sb, x_src).then_inc(s_xin, 16)
                    sp.wait_ge(s_pB, t * 8 + 8)
                    sp.sem_inc(turn["sync"], 1)
                else:
                    sp.wait_ge(s_T, (t - 1) * NTB + 28)
                    sp.sem_inc(turn["sync"], 1)
                    sp.dma_start(o_sb[0:NS, :], attn_d[:, :]).then_inc(s_oin, 16)
                    sp.wait_ge(s_route, t)
                    sp.sem_inc(turn["sync"], 1)
                    sp.dma_start(gates[0:NS, :], proj_d[SEQ:T, GA:W_IN]).then_inc(s_gin, 16)
                    sp.dma_start(x_sb[0:NS, :], x_all[1]).then_inc(s_xin, 16)
                for n in range(NW):
                    for name, first, last in (("w_proj_diff", 0, 4), ("w_proj_sb", 4, 8), ("w_out", 8, 16),
                                              ("peer_w_query", 16, 24)):
                        if first <= n < last:
                            src = a[name][0][(n - first) * P:(n - first + 1) * P, :]
                    if n >= 4:
                        sp.wait_ge(s_wu, t * NW + n - 3)
                        sp.sem_inc(turn["sync"], 1)
                    sp.dma_start(wring[:, n % 4, :], src).then_inc(s_wr[n % 4], 16)

            def sync_finish(sp, e):
                dst = y_out[0][tile(e), :] if rows_of(e) == P else y_out[1]
                sp.wait_ge(s_y_out, e + 1)
                sp.sem_inc(turn["sync"], 1)
                sp.dma_start(dst, y_sb[0:rows_of(e), :]).then_inc(s_yst, 16)

            def gather(pool, e, table, idx, phase):
                n = rows_of(e)
                for s in range(NSLOT):
                    if phase == 0:
                        free = summed(e, s, -1) if s < R else (s_dot, e * NSLOT + s - R + 1)
                    else:
                        free = (s_dot, e * NSLOT + NSLOT - R + s + 1) if s < R else summed(e, s, -1)
                    pool.wait_ge(*free)
                    pool.sem_inc(turn["pool"], 1)
                    pool.indirect_dma_start(ring[0:n, s % R, :], None, table,
                                            bass.IndirectOffsetOnAxis(ap=idx[0:n, s:s + 1], axis=0)).then_inc(s_ring[s % R], 16)

            def summed(e, s, rounds=0):
                mine, sem = (VSUM, s_vsum) if s % R in VSUM else (TSUM, s_sum)
                return sem, (e * (NSLOT // R) + s // R + 1 + rounds) * len(mine) + mine.index(s % R) + 1

            def arrived(e, phase, s):
                return s_ring[s % R], (e * (2 * NSLOT // R) + phase * (NSLOT // R) + s // R + 1) * 16

            def pool_experts(pool, e):
                pool.wait_ge(s_route, e + 1)
                pool.sem_inc(turn["pool"], 1)
                gather(pool, e, a["peer_u"][0], idx_u, 0)
                pool.wait_ge(s_idxv, e + 1)
                pool.sem_inc(turn["pool"], 1)
                gather(pool, e, a["peer_v"][0], idx_v, 1)

            pe_T = Steps(s_T, NTB)

            def pe_transposes(pe, blocks, n):
                pe.wait_ge(s_Tc, pe_T.value)
                for k, blk in enumerate(blocks):
                    m = nc.tensor.transpose(ps[:, 6, k * P:k * P + n], blk, ident[0:n, 0:n])
                pe_T.raised_by(m)

            def pe_scores(pe, t, u, kw):
                for hf in range(2):
                    pe.wait_ge(s_Sr[hf], t * 8 + u)
                    for c in range(kw // CH):
                        m = nc.tensor.matmul(ps[:, 2 + 2 * hf + c, :], qz[:, u, hf, :], keyT[:, u, c * CH:(c + 1) * CH],
                                             start=True, stop=True)
                    m.then_inc(s_S[hf], 1)

            def pe_attend(pe, t, kw):
                nb = kw // P // 2
                pe_T.begin(t)
                pe.wait_ge(s_qin, t * 32 + 32)
                for g in range(2):
                    pe_transposes(pe, [o_sb[:, u * P:(u + 1) * P] for u in range(4 * g, 4 * g + 4)], P)
                pe.wait_ge(s_Tc, pe_T.value)
                pe.wait_ge(s_scr, t)
                pe_scores(pe, t, 0, kw)
                for u in range(8):
                    if u < 7:
                        pe_scores(pe, t, u + 1, kw)
                    if u % 4 == 0:
                        pe.wait_ge(s_Oc, t * 2 + u // 4)
                    for hf in range(1 if u < HA else 2):
                        n = u if u < HA else 4 + 2 * (u - HA) + hf
                        pe.wait_ge(*((s_pA, t * 4 + u + 1) if u < HA else (s_pB, t * 8 + n - 3)))
                        for j in range(2):
                            pe_transposes(pe, [prob[:, n % 2, (j * nb + k) * P:(j * nb + k + 1) * P] for k in range(nb)], P)
                        pe.wait_ge(s_Tc, pe_T.value)
                        wide = P if u < HA else 64
                        col = (u % 4) * P + hf * 64
                        for kb in range(2 * nb):
                            m = nc.tensor.matmul(ps[:, 7, col:col + wide], pTr[:, kb, :],
                                                 val[:, kb, u * P + hf * 64:u * P + hf * 64 + wide],
                                                 start=(kb == 0), stop=(kb == 2 * nb - 1))
                        m.then_inc(s_PV, 1)

            def pe_product(pe, t, n, bank, first, blocks, k0, k1):
                for k in range(k0, k1):
                    w = first + k - blocks[0]
                    pe.wait_ge(s_wr[w % 4], t * (16 * NW // 4) + 16 * (w // 4) + 16)
                    for c in range(2):
                        m = nc.tensor.matmul(ps[0:n, bank + c, :], pTr[:, k, 0:n], wring[:, w % 4, c * CH:(c + 1) * CH],
                                             start=(k == blocks[0]), stop=(k == blocks[1] - 1))
                    m.then_inc(s_wu, 1)

            def pe_merge(pe, t, piece):
                n = rows_of(t)

                def turn_rows(src):
                    for g in range(2):
                        pe_transposes(pe, [src[0:n, k * P:(k + 1) * P] for k in range(4 * g, 4 * g + 4)], n)

                if piece == "turn_o":
                    if n < P:
                        pe_T.begin(t)
                    pe.wait_ge(s_On, t + 1)
                    turn_rows(o_sb)
                elif piece == "branch_a":
                    pe.wait_ge(s_Tc, pe_T.value)
                    pe_product(pe, t, n, 2, 0, (0, 4), 0, 4)
                elif piece == "branch_b":
                    pe_product(pe, t, n, 4, 4, (4, 8), 4, 8)
                elif piece == "turn_m":
                    pe.wait_ge(s_m, t + 1)
                    turn_rows(mixed)
                elif piece == "out_1":
                    pe.wait_ge(s_Tc, pe_T.value)
                    pe_product(pe, t, n, 2, 8, (0, 8), 0, 4)
                elif piece == "out_2":
                    pe_product(pe, t, n, 2, 8, (0, 8), 4, 8)
                elif piece == "turn_x":
                    pe.wait_ge(s_xn, t + 1)
                    turn_rows(xn_sb)
                elif piece == "query_1":
                    pe.wait_ge(s_Tc, pe_T.value)
                    pe_product(pe, t, n, 4, 16, (0, 8), 0, 4)
                elif piece == "query_2":
                    pe_product(pe, t, n, 4, 16, (0, 8), 4, 8)
                elif piece == "turn_q":
                    pe.wait_ge(s_qc, t + 1)
                    turn_rows(q_sb)
                elif piece == "score":
                    pe.wait_ge(s_Tc, pe_T.value)
                    for h in range(PH):
                        m = nc.tensor.matmul(ps[0:n, 2 + h // 2, (h % 2) * 2 * P:(h % 2 + 1) * 2 * P], pTr[:, h, 0:n],
                                             subkT[:, h, :], start=True, stop=True)
                    m.then_inc(s_sc, 1)

            def turn_of(e, s):
                return e * (NSLOT // R * len(TSUM)) + s // R * len(TSUM) + TSUM.index(s % R)

            def pe_experts(pe, e, k):
                if k == 0:
                    pe.wait_ge(s_yc, e + 1)
                    pe.wait_ge(s_h, e + 1)
                    for c in range(2):
                        m = nc.tensor.matmul(ps[:, c, :], ident[:], h_sb[:, c * CH:(c + 1) * CH], start=True, stop=False)
                    m.then_inc(s_res, 1)
                for s in range(4 * k, 4 * k + 4):
                    if s % R in TSUM:
                        pe.wait_ge(*arrived(e, 1, s))
                        pe.wait_ge(s_diag, turn_of(e, s) + 1)
                        for c in range(2):
                            m = nc.tensor.matmul(ps[:, c, :], diag[:, turn_of(0, s) % NDG, :], ring[:, s % R, c * CH:(c + 1) * CH],
                                                 start=False, stop=(s // R == NSLOT // R - 1 and s % R == TSUM[-1]))
                        m.then_inc(s_sum, 1)

            act_T = Steps(s_Tc, NTB)

            def act_take(act, dst, n):
                act.wait_ge(s_T, act_T.value + 1)
                src = ps[:, 6, 0:dst.shape[1] * P].rearrange("p (k r) -> p k r", r=P)[:, :, 0:n]
                act_T.raised_by(nc.scalar.copy(dst[:, :, 0:n], src))

            def act_attend(act, t, kw):
                nb = kw // P // 2
                act_T.begin(t)
                act.wait_ge(s_route, t)
                act.sem_inc(turn["act"], 1)
                for g in range(2):
                    act.wait_ge(s_T, act_T.value + 1)
                    src = ps[:, 6, :].rearrange("p (u r) -> p u r", r=P)
                    nc.scalar.activation(qz[:, 4 * g:4 * g + 4, 0, :], src, ACT.Copy, scale=half_scale[:, 0:1])
                    act_T.raised_by(nc.scalar.activation(qz[:, 4 * g:4 * g + 4, 1, :], src, ACT.Copy, scale=half_scale[:, 1:2]))
                for u in range(8):
                    if u < HA:
                        for hf in range(2):
                            act.wait_ge(s_nm, t * 8 + 2 * u + hf + 1)
                            nc.scalar.activation(z[:, hf, 0:kw], z[:, hf, 0:kw], ACT.Exp, bias=nm[:, hf:hf + 1],
                                                 accum_out=l[:, hf:hf + 1]).then_inc(s_exp, 1)
                        for j in range(2):
                            act_take(act, pTr[:, j * nb:(j + 1) * nb, :], P)
                    else:
                        v = 4 * (u - HA)
                        for hf in range(2):
                            act.wait_ge(s_Sr[hf], t * 8 + u + 1)
                            nc.scalar.activation(soft[:, hf, 0:kw], z[:, hf, 0:kw], ACT.Abs).then_inc(s_softc, 1)
                        for hf in range(2):
                            act.wait_ge(s_softc, t * 16 + v + hf + 1)
                            nc.scalar.activation(soft[:, hf, 0:kw], soft[:, hf, 0:kw], ACT.Exp, scale=-1.0).then_inc(s_softc, 1)
                        for hf in range(2):
                            act.wait_ge(s_softc, t * 16 + v + hf + 3)
                            nc.scalar.activation(soft[:, hf, 0:kw], soft[:, hf, 0:kw], ACT.Ln, bias=one_t[:]).then_inc(s_soft, 1)
                        for hf in range(2):
                            act.wait_ge(s_w, t * 8 + 2 * (u - HA) + hf + 1)
                            nc.scalar.activation(prob[:, hf, 0:kw], z[:, hf, 0:kw], ACT.Exp).then_inc(s_pB, 1)
                        for j in range(4):
                            act_take(act, pTr[:, (j % 2) * nb:(j % 2 + 1) * nb, :], P)
                    if u % 4 == 3:
                        act.wait_ge(s_PV, t * 12 + (4 if u == 3 else 12))
                        nc.scalar.copy(o_sb[:, (u // 4) * CH:(u // 4 + 1) * CH], ps[:, 7, :]).then_inc(s_Oc, 1)

            def act_merge(act, t, piece):
                n = rows_of(t)

                def take_two():
                    for g in range(2):
                        act_take(act, pTr[:, 4 * g:4 * g + 4, :], n)

                if piece == "norm_o":
                    if n < P:
                        act_T.begin(t)
                    act.wait_ge(s_gin, t * 16 + 16)
                    nc.scalar.activation(gates[0:n, :], gates[0:n, :], ACT.Sigmoid).then_inc(s_sig, 1)
                    act.wait_ge(s_ssh, t + 1)
                    nc.scalar.activation(rmsh[0:n, :], ssh[0:n, :], ACT.Sqrt, bias=eps_t[0:n, :], scale=1.0 / P).then_inc(s_rmsh, 1)
                elif piece in ("turn_o", "turn_m", "turn_x", "turn_q"):
                    take_two()
                elif piece == "residual":
                    act.wait_ge(s_ssx, t + 1)
                    nc.scalar.activation(rmsx[0:n, :], ssx[0:n, :], ACT.Sqrt, bias=eps_t[0:n, :], scale=1.0 / D).then_inc(s_rmsx, 1)
                elif piece == "query_2":
                    act.wait_ge(s_wu, t * NW + 24)
                    nc.scalar.copy(q_sb[0:n, :], both(4)[0:n, :]).then_inc(s_qc, 1)
                elif piece == "gate":
                    act.wait_ge(s_shift, t + 1)
                    nc.scalar.activation(gexp[0:n], gexp[0:n], ACT.Exp).then_inc(s_gexp, 1)

            def act_gelu(act, e):
                n = rows_of(e)
                act.wait_ge(s_dot, e * NSLOT + NSLOT)
                nc.scalar.activation(act_u[0:n, :], dots[0:n, :], ACT.Gelu).then_inc(s_gelu, 1)

            def act_experts(act, e, k):
                if k == 0:
                    act.wait_ge(s_wgt, e + 1)
                    act.sem_inc(turn["act"], 1)
                for s in range(4 * k, 4 * k + 4):
                    if s % R in TSUM:
                        act.wait_ge(s_sum, turn_of(e, s) + 1 - NDG + len(TSUM))
                        nc.scalar.activation(diag[:, turn_of(0, s) % NDG, :], ident[:], ACT.Copy,
                                             scale=wgt[:, s:s + 1]).then_inc(s_diag, 1)

            def act_finish(act, e):
                n = rows_of(e)
                act.wait_ge(s_ssy, e + 1)
                nc.scalar.activation(rmsy[0:n, :], ssy[0:n, :], ACT.Sqrt, bias=eps_t[0:n, :], scale=1.0 / D).then_inc(s_rmsy, 1)

            lk = {"a": Steps(s_adve, 4 * 3 + 4 * 4), "m": Steps(s_mdve, 3), "r": Steps(s_rdve, 21), "f": Steps(s_fdve, 1)}

            def chain(name, instruction):
                lk[name].raised_by(instruction)

            def linked(dve, name):
                dve.wait_ge(lk[name].sem, lk[name].value)
                dve.sem_inc(turn["dve"], 1)

            def dve_attend(dve, t, u, part, kw):
                if u == 0 and part == 0:
                    lk["a"].begin(t)
                    dve.wait_ge(s_wu, t * NW)
                if part == 0:
                    if u < HA:
                        dve.wait_ge(s_bias[u % 2], t * 32 + 16 * (u // 2) + 16)
                    elif u == HA:
                        dve.wait_ge(s_bmask, t * 16 + 16)
                    if u <= HA:
                        dve.wait_ge(s_pA, t * 4 + u)
                        dve.sem_inc(turn["dve"], 1)
                    for hf in range(2):
                        if u == 0 or u > HA:
                            dve.wait_ge(s_pB, t * 8 + (0 if u == 0 else 2 * (u - HA) - 1 + hf))
                            dve.sem_inc(turn["dve"], 1)
                        dve.wait_ge(s_S[hf], t * 8 + u + 1)
                        dve.sem_inc(turn["dve"], 1)
                        src = both(2 + 2 * hf)[:, 0:kw]
                        if u < HA:
                            nc.vector.tensor_tensor_reduce(out=z[:, hf, 0:kw], in0=src, in1=bias[:, u % 2, 0:kw], scale=1.0,
                                                           scalar=LOWEST, op0=ALU.add, op1=ALU.max,
                                                           accum_out=mx[:, hf:hf + 1]).then_inc(s_Sr[hf], 1)
                        else:
                            nc.vector.tensor_tensor(z[:, hf, 0:kw], src, bmask[:, 0:kw], ALU.add).then_inc(s_Sr[hf], 1)
                    if u < HA:
                        for hf in range(2):
                            dve.wait_ge(s_Sr[hf], t * 8 + u + 1)
                            nc.vector.tensor_scalar_mul(nm[:, hf:hf + 1], mx[:, hf:hf + 1], -1.0).then_inc(s_nm, 1)
                elif u < HA:
                    dve.wait_ge(s_exp, t * 8 + 2 * u + 2)
                    chain("a", nc.vector.reciprocal(rl[:], l[:]))
                    linked(dve, "a")
                    chain("a", nc.vector.tensor_scalar_mul(rl2[:], rl[:, 1:2], neg_lam[:]))
                    dve.wait_ge(s_T, t * NTB + 2 * u)
                    chain("a", nc.vector.tensor_scalar_mul(prob[:, u % 2, 0:kw], z[:, 0, 0:kw], rl[:, 0:1]))
                    linked(dve, "a")
                    nc.vector.scalar_tensor_tensor(out=prob[:, u % 2, 0:kw], in0=z[:, 1, 0:kw], scalar=rl2[:],
                                                   in1=prob[:, u % 2, 0:kw], op0=ALU.mult, op1=ALU.add).then_inc(s_pA, 1)
                else:
                    for hf in range(2):
                        dve.wait_ge(s_soft, t * 8 + 2 * (u - HA) + hf + 1)
                        chain("a", nc.vector.scalar_tensor_tensor(out=soft[:, hf, 0:kw], in0=z[:, hf, 0:kw], scalar=0.0,
                                                                  in1=soft[:, hf, 0:kw], op0=ALU.max, op1=ALU.add))
                    for hf in range(2):
                        dve.wait_ge(s_T, t * NTB + 2 * (4 + 2 * (u - HA) + hf))
                        dve.sem_inc(turn["dve"], 1)
                        dve.wait_ge(s_adve, lk["a"].value - 1)
                        m = nc.vector.tensor_tensor_scan(out=prob[:, hf, kw - 1::-1],
                                                         data0=soft[:, hf, kw - 1::-1], data1=soft[:, hf, kw - 1::-1],
                                                         initial=0.0, op0=ALU.add, op1=ALU.bypass)
                        chain("a", m)
                    for hf in range(2):
                        dve.wait_ge(s_adve, lk["a"].value - 1 + hf)
                        nc.vector.tensor_tensor(z[:, hf, 0:kw], z[:, hf, 0:kw], prob[:, hf, 0:kw], ALU.subtract).then_inc(s_w, 1)

            def dve_merge(dve, t, piece):
                n = rows_of(t)
                if piece == "norm_o":
                    lk["m"].begin(t)
                    lk["r"].begin(t)
                    if n == P:
                        dve.wait_ge(s_Oc, t * 2 + 2)
                    else:
                        dve.wait_ge(s_oin, 16)
                    for h in range(HA):
                        cols = slice(h * P, (h + 1) * P)
                        m = nc.vector.tensor_tensor_reduce(out=sq[0:n, cols], in0=o_sb[0:n, cols], in1=o_sb[0:n, cols],
                                                           scale=1.0, scalar=0.0, op0=ALU.mult, op1=ALU.add,
                                                           accum_out=ssh[0:n, h:h + 1])
                    m.then_inc(s_ssh, 1)
                elif piece == "scale_o":
                    dve.wait_ge(s_rmsh, t + 1)
                    chain("m", nc.vector.reciprocal(rsh[0:n, :], rmsh[0:n, :]))
                    linked(dve, "m")
                    for h in range(HA):
                        cols = slice(h * P, (h + 1) * P)
                        m = nc.vector.scalar_tensor_tensor(out=o_sb[0:n, cols], in0=o_sb[0:n, cols], scalar=rsh[0:n, h:h + 1],
                                                           in1=gain_sub[0:n, :], op0=ALU.mult, op1=ALU.mult)
                    m.then_inc(s_On, 1)
                elif piece == "mix":
                    dve.wait_ge(s_sig, t + 1)
                    dve.sem_inc(turn["dve"], 1)
                    dve.wait_ge(s_wu, t * NW + 8)
                    chain("m", nc.vector.tensor_tensor(mixed[0:n, :], both(2)[0:n, :], gates[0:n, 0:D], ALU.mult))
                    chain("m", nc.vector.tensor_tensor(gates[0:n, D:2 * D], both(4)[0:n, :], gates[0:n, D:2 * D], ALU.mult))
                    linked(dve, "m")
                    nc.vector.tensor_tensor(mixed[0:n, :], mixed[0:n, :], gates[0:n, D:2 * D], ALU.add).then_inc(s_m, 1)
                elif piece == "residual":
                    dve.wait_ge(s_wu, t * NW + 16)
                    dve.sem_inc(turn["dve"], 1)
                    dve.wait_ge(s_res, t)
                    dve.sem_inc(turn["dve"], 1)
                    dve.wait_ge(s_xin, t * 16 + 16)
                    nc.vector.tensor_tensor(h_sb[0:n, :], both(2)[0:n, :], x_sb[0:n, :], ALU.add).then_inc(s_h, 1)
                    dve.wait_ge(s_h, t + 1)
                    nc.vector.tensor_tensor_reduce(out=sq[0:n, :], in0=h_sb[0:n, :], in1=h_sb[0:n, :], scale=1.0, scalar=0.0,
                                                   op0=ALU.mult, op1=ALU.add, accum_out=ssx[0:n, :]).then_inc(s_ssx, 1)
                elif piece == "norm_x":
                    dve.wait_ge(s_rmsx, t + 1)
                    chain("r", nc.vector.reciprocal(rsx[0:n, :], rmsx[0:n, :]))
                    linked(dve, "r")
                    nc.vector.scalar_tensor_tensor(out=xn_sb[0:n, :], in0=h_sb[0:n, :], scalar=rsx[0:n, :],
                                                   in1=gain_ffn[0:n, :], op0=ALU.mult, op1=ALU.mult).then_inc(s_xn, 1)
                sc = [ps[0:n, 2 + i // 4, (i % 4) * P:(i % 4 + 1) * P] for i in range(2 * PH)]
                lf = [left[0:n, i * P:(i + 1) * P] for i in range(2 * PH)]
                cd = [cand[0:n, i * 2 * P:(i + 1) * 2 * P] for i in range(PH)]
                lc = [left[0:n, i * 2 * P:(i + 1) * 2 * P] for i in range(PH)]
                if piece == "key_1":
                    dve.wait_ge(s_sc, t + 1)
                    dve.sem_inc(turn["dve"], 1)
                    for i in range(2 * PH):
                        m = nc.vector.max(top[0:n, i, 0:8], sc[i])
                    chain("r", m)
                elif piece == "key_2":
                    linked(dve, "r")
                    for i in range(2 * PH):
                        m = nc.vector.match_replace(lf[i], top[0:n, i, 0:8], sc[i], LOWEST)
                    chain("r", m)
                elif piece == "key_3":
                    for i in range(2 * PH):
                        m = nc.vector.max_index(topi[0:n, i, 0:8], top[0:n, i, 0:8], sc[i])
                    m.then_inc(s_scr, 1)
                elif piece == "key_4":
                    linked(dve, "r")
                    for i in range(2 * PH):
                        m = nc.vector.max(top[0:n, i, 8:16], lf[i])
                    chain("r", m)
                elif piece == "key_5":
                    linked(dve, "r")
                    for i in range(2 * PH):
                        m = nc.vector.max_index(topi[0:n, i, 8:16], top[0:n, i, 8:16], lf[i])
                    chain("r", m)
                elif piece == "pair_1":
                    linked(dve, "r")
                    chain("r", nc.vector.tensor_copy(topf[0:n], topi[0:n]))
                    halves = top[0:n].rearrange("p (h c) a -> p h c a", c=2)
                    chain("r", nc.vector.tensor_tensor(cand[0:n, :].rearrange("p (h k a) -> p h k a", h=PH, k=TK),
                                                       halves[:, :, 0, :].unsqueeze(3).broadcast_to([n, PH, TK, TK]),
                                                       halves[:, :, 1, :].unsqueeze(2).broadcast_to([n, PH, TK, TK]), ALU.add))
                elif piece == "pair_2":
                    linked(dve, "r")
                    for i in range(PH):
                        m = nc.vector.max(best[0:n, i, 0:8], cd[i])
                    chain("r", m)
                elif piece == "pair_3":
                    linked(dve, "r")
                    for i in range(PH):
                        m = nc.vector.match_replace(lc[i], best[0:n, i, 0:8], cd[i], LOWEST)
                    chain("r", m)
                elif piece == "pair_4":
                    for i in range(PH):
                        nc.vector.max_index(bestj[0:n, i * TK:i * TK + 8], best[0:n, i, 0:8], cd[i])
                elif piece == "pair_5":
                    linked(dve, "r")
                    for i in range(PH):
                        m = nc.vector.max(best[0:n, i, 8:16], lc[i])
                    chain("r", m)
                elif piece == "pair_6":
                    linked(dve, "r")
                    for i in range(PH):
                        m = nc.vector.max_index(bestj[0:n, i * TK + 8:(i + 1) * TK], best[0:n, i, 8:16], lc[i])
                    chain("r", m)
                elif piece == "gate":
                    linked(dve, "r")
                    nc.vector.tensor_tensor(gexp[0:n], best[0:n], best[0:n, :, 0:1].broadcast_to([n, PH, TK]),
                                            ALU.subtract).then_inc(s_shift, 1)
                    nc.vector.tensor_scalar(ja[0:n, 0, :], bestj[0:n, :], 4, None, ALU.logical_shift_right)
                    chain("r", nc.vector.tensor_scalar(ja[0:n, 1, :], bestj[0:n, :], 15, None, ALU.bitwise_and))
                    linked(dve, "r")
                    chain("r", nc.vector.tensor_copy(jf[0:n], ja[0:n]))
                elif piece in ("pick_1", "pick_2"):
                    c = int(piece == "pick_2")
                    linked(dve, "r")
                    hot4 = pick[0:n, :].rearrange("p (h k a) -> p h k a", h=PH, k=TK)
                    hot3 = pick[0:n, :].rearrange("p (s a) -> p s a", a=TK)
                    ids = topf[0:n].rearrange("p (h c) a -> p h c a", c=2)[:, :, c, :].unsqueeze(2).broadcast_to([n, PH, TK, TK])
                    chain("r", nc.vector.tensor_tensor(hot3, jf[0:n, c, :].unsqueeze(2).broadcast_to([n, NSLOT, TK]),
                                                       iota16[0:n, :].unsqueeze(1).broadcast_to([n, NSLOT, TK]), ALU.is_equal))
                    linked(dve, "r")
                    chain("r", nc.vector.tensor_tensor(hot4, hot4, ids, ALU.mult))
                    linked(dve, "r")
                    chain("r", nc.vector.tensor_reduce(sel[0:n, c, :], hot3, AX, ALU.add))
                elif piece == "choose":
                    linked(dve, "r")
                    nc.vector.scalar_tensor_tensor(out=idx_u[0:n, :], in0=sel[0:n, 0, :], scalar=float(P), in1=sel[0:n, 1, :],
                                                   op0=ALU.mult, op1=ALU.add)
                    dve.wait_ge(s_gexp, t + 1)
                    chain("r", nc.vector.tensor_reduce(gsum[0:n, :], gexp[0:n], AX, ALU.add))
                    linked(dve, "r")
                    chain("r", nc.vector.reciprocal(grec[0:n, :], gsum[0:n, :]))
                    linked(dve, "r")
                    nc.vector.tensor_tensor(gate[0:n], gexp[0:n], grec[0:n, :].unsqueeze(2).broadcast_to([n, PH, TK]),
                                            ALU.mult).then_inc(s_route, 1)

            def dve_dots(dve, e, first, last):
                n = rows_of(e)
                for s in range(first, last):
                    dve.wait_ge(*arrived(e, 0, s))
                    nc.vector.tensor_tensor_reduce(out=ring[0:n, s % R, :], in0=ring[0:n, s % R, :], in1=xn_sb[0:n, :],
                                                   scale=1.0, scalar=0.0, op0=ALU.mult, op1=ALU.add,
                                                   accum_out=dots[0:n, s:s + 1]).then_inc(s_dot, 1)

            def dve_keep_idx(dve, e):
                dve.wait_ge(*summed(e, NSLOT - 1, -(NSLOT // R)))
                dve.wait_ge(*summed(e, NSLOT - 2, -(NSLOT // R)))
                nc.vector.tensor_copy(idx_v[0:rows_of(e), :], idx_u[0:rows_of(e), :]).then_inc(s_idxv, 1)

            def dve_weights(dve, e):
                n = rows_of(e)
                dve.wait_ge(s_gelu, e + 1)
                nc.vector.tensor_tensor(wgt[0:n, :], act_u[0:n, :], gate[0:n].rearrange("p h k -> p (h k)"), ALU.mult).then_inc(s_wgt, 1)

            def dve_experts(dve, e, k):
                n = rows_of(e)
                if k == 0:
                    dve.wait_ge(s_wgt, e + 1)
                    dve.wait_ge(s_yst, e * 16 + 16)
                for s in range(4 * k, 4 * k + 4):
                    if s % R in VSUM:
                        row, w = ring[0:n, s % R, :], wgt[0:n, s:s + 1]
                        dve.wait_ge(*arrived(e, 1, s))
                        if s == VSUM[0]:
                            m = nc.vector.tensor_scalar_mul(y_sb[0:n, :], row, w)
                        else:
                            before_this = s_vsum, summed(e, s)[1] - 1
                            dve.wait_ge(*before_this)
                            m = nc.vector.scalar_tensor_tensor(out=y_sb[0:n, :], in0=row, scalar=w, in1=y_sb[0:n, :],
                                                               op0=ALU.mult, op1=ALU.add)
                        m.then_inc(s_vsum, 1)

            def dve_finish(dve, e, part):
                n = rows_of(e)
                if part == 0:
                    lk["f"].begin(e)
                    dve.wait_ge(*summed(e, NSLOT - R + TSUM[-1]))
                    dve.sem_inc(turn["dve"], 1)
                    dve.wait_ge(*summed(e, NSLOT - R + VSUM[-1]))
                    nc.vector.tensor_tensor(y_sb[0:n, :], both(0)[0:n, :], y_sb[0:n, :], ALU.add).then_inc(s_yc, 1)
                    dve.wait_ge(s_yc, e + 2)
                    nc.vector.tensor_tensor_reduce(out=ysq[0:n, :], in0=y_sb[0:n, :], in1=y_sb[0:n, :], scale=1.0, scalar=0.0,
                                                   op0=ALU.mult, op1=ALU.add, accum_out=ssy[0:n, :]).then_inc(s_ssy, 1)
                else:
                    dve.wait_ge(s_rmsy, e + 1)
                    chain("f", nc.vector.reciprocal(rsy[0:n, :], rmsy[0:n, :]))
                    linked(dve, "f")
                    nc.vector.scalar_tensor_tensor(out=y_sb[0:n, :], in0=y_sb[0:n, :], scalar=rsy[0:n, :], in1=gain_fin[0:n, :],
                                                   op0=ALU.mult, op1=ALU.mult).then_inc(s_y_out, 1)


            def sync_sample(sp):
                sp.dma_start(pages[:], a["page_table"].rearrange("(o b) g -> o (b g)", o=1)).then_inc(d_pt, 16)
                sp.wait_ge(s_Oc, NPT * 2)
                for n, (c0, c1) in enumerate(((QA, QB), (KA, KB))):
                    sp.dma_start(qk[:, n, 0:CH], proj_d[SEQ:T, c0:c0 + CH]).then_inc(d_qk, 16)
                    sp.dma_start(qk[:, n, CH:D], proj_d[SEQ:T, c1:c1 + CH]).then_inc(d_qk, 16)
                sp.wait_ge(d_pt, 16)

                def load(b, which, done):
                    for g in range(PAGES):
                        page = sp.value_load(pages[0:1, b * PAGES + g:b * PAGES + g + 1], min_val=0, max_val=last_page)
                        for n in range(2):
                            dst = kpage[:, g, :] if which == 0 else vpage[:, b % 2, g, :]
                            sp.dma_start(dst[:, n * CH:(n + 1) * CH],
                                         pools[2 * which + n][ds(page, 1)].rearrange("o p c -> (o p) c")).then_inc(done, 16)

                def load_keys(b):
                    if b:
                        sp.wait_ge(d_kT, 4 * b)
                    load(b, 0, d_page)

                def load_values(b):
                    if b >= 2:
                        sp.wait_ge(d_O, b - 1)
                    load(b, 1, d_val[b % 2])
                    for n, col in enumerate((VA, VB)):
                        sp.dma_start(vnew[:, b % 2, n * CH:(n + 1) * CH],
                                     proj_d[SEQ + b * TD:SEQ + (b + 1) * TD, col:col + CH]).then_inc(d_val[b % 2], 16)

                load_keys(0)
                for m in range(2 * HA + HB):
                    row = min(m // 2, HA)
                    sp.dma_start(smask[m * TD:(m + 1) * TD, :],
                                 slab_d[row, 0:TD, SLABW - SEQ - PAST:SLABW - SEQ - PAST + KS]).then_inc(d_mask, 16)
                load_values(0)
                load_keys(1)
                load_values(1)
                for b in range(NB_DEC):
                    if b + 2 < NB_DEC:
                        load_keys(b + 2)
                    sp.wait_ge(d_Oc, 2 * b + 2)
                    rows = slice(b * TD, (b + 1) * TD)
                    for h in range(HA):
                        sp.dma_start(attn_d[rows, h * P:(h + 1) * P],
                                     oa[h * TD:(h + 1) * TD, h * P:(h + 1) * P]).then_inc(d_store, 16)
                    for h in range(HB):
                        sp.dma_start(attn_d[rows, CH + h * 64:CH + (h + 1) * 64],
                                     ob[h * TD:(h + 1) * TD, h * 64:(h + 1) * 64]).then_inc(d_store, 16)
                    if b + 2 < NB_DEC:
                        load_values(b + 2)
                sp.wait_ge(d_store, 16 * NB_DEC * (HA + HB))

            def pe_sample(pe):
                pe.wait_ge(s_yc, NPT)
                pe.wait_ge(s_scr, NPT)
                pe.wait_ge(s_Tc, NPT * NTB)
                pe.wait_ge(d_qk, 64)
                for n in range(2):
                    for u in range(KD):
                        m = nc.tensor.transpose(ps[:, n, u * NS:(u + 1) * NS], qk[:, n, u * P:(u + 1) * P], ident[0:NS, 0:NS])
                    m.then_inc(d_qT, 1)
                pe.wait_ge(d_qTc, 2)

                def transpose_keys(b):
                    pe.wait_ge(d_page, 64 * (b + 1))
                    for g in range(PAGES):
                        for j in range(2):
                            bank = 2 * g + j
                            if b:
                                pe.wait_ge(d_kTc, 5 * (b - 1) + bank + 1)
                            for k in range(4):
                                u = 4 * j + k
                                m = nc.tensor.transpose(ps[:, bank, k * P:(k + 1) * P],
                                                        kpage[:, g, u * P:(u + 1) * P], ident[:])
                            m.then_inc(d_kT, 1)

                def scores(b):
                    pe.wait_ge(d_kTc, 5 * (b + 1))
                    pe.wait_ge(d_blk, 2 * (b + 1))
                    if b:
                        pe.wait_ge(d_Sr, b)
                    for u in range(KD):
                        m = nc.tensor.matmul(ps[:, 4, 0:KS], qblk_flat[:, u * P:(u + 1) * P], kT[:, u, :],
                                             start=(u == 0), stop=(u == KD - 1))
                    m.then_inc(d_S, 1)

                transpose_keys(0)
                scores(0)
                transpose_keys(1)
                for b in range(NB_DEC):
                    pe.wait_ge(d_prob, 2 * (b + 1))
                    if b:
                        pe.wait_ge(d_Tc, b)
                    for c, kc in enumerate(KC):
                        m = nc.tensor.transpose(ps[0:kc, 5, c * P:(c + 1) * P], sw_[:, c * P:c * P + kc], ident[:])
                    m.then_inc(d_T, 1)
                    if b + 1 < NB_DEC:
                        scores(b + 1)
                    pe.wait_ge(d_pd, b + 1)
                    pe.wait_ge(d_val[b % 2], 96 * (b // 2 + 1))
                    if b:
                        pe.wait_ge(d_Oc, 2 * b)
                    for c, kc in enumerate(KC):
                        v = vpage[:, b % 2, c, :] if c < PAGES else vnew[:, b % 2, :]
                        nc.tensor.matmul(ps[0:HA * TD, 6, :], pd[0:kc, c, :], v[0:kc, 0:CH], start=(c == 0), stop=(c == 2))
                    for c, kc in enumerate(KC):
                        v = vpage[:, b % 2, c, :] if c < PAGES else vnew[:, b % 2, :]
                        m = nc.tensor.matmul(ps[0:HB * TD, 7, :], pT[0:kc, c, 64:P], v[0:kc, CH:D], start=(c == 0), stop=(c == 2))
                    m.then_inc(d_O, 1)
                    if b + 2 < NB_DEC:
                        transpose_keys(b + 2)
                pe.wait_ge(d_kTc, 5 * NB_DEC)

            def act_sample(act):
                act.wait_ge(d_qT, 1)
                nc.scalar.activation(qT[:], ps[:, 0, :].rearrange("p (u r) -> p u r", r=NS), ACT.Copy, scale=0.125).then_inc(d_qTc, 1)
                act.wait_ge(d_qT, 2)
                nc.scalar.copy(knT[:], ps[:, 1, :].rearrange("p (u r) -> p u r", r=NS)).then_inc(d_qTc, 1)
                act.wait_ge(d_qTc, 2)

                def take_keys(b):
                    if b:
                        act.wait_ge(d_S, b)
                    for g in range(PAGES):
                        for j in range(2):
                            act.wait_ge(d_kT, 4 * b + 2 * g + j + 1)
                            nc.scalar.copy(kT[:, 4 * j:4 * j + 4, g * P:(g + 1) * P],
                                           ps[:, 2 * g + j, :].rearrange("p (u r) -> p u r", r=P)).then_inc(d_kTc, 1)
                    nc.scalar.copy(kT[:, :, PAST:KS], knT[:, :, b * TD:(b + 1) * TD]).then_inc(d_kTc, 1)

                take_keys(0)
                for b in range(NB_DEC):
                    act.wait_ge(d_Sr, b + 1)
                    nc.scalar.activation(se_[B], ss_[B], ACT.Abs).then_inc(d_act, 1)
                    act.wait_ge(d_act, 4 * b + 1)
                    nc.scalar.activation(se_[B], se_[B], ACT.Exp, scale=-1.0).then_inc(d_act, 1)
                    act.wait_ge(d_dve, 7 * b + 2)
                    nc.scalar.activation(se_[A], ss_[A], ACT.Exp, bias=snm[A, :], accum_out=sl_[A, :]).then_inc(d_act, 1)
                    act.wait_ge(d_act, 4 * b + 3)
                    nc.scalar.activation(se_[B], se_[B], ACT.Ln, bias=one_t[B, :]).then_inc(d_act, 1)
                    if b + 1 < NB_DEC:
                        take_keys(b + 1)
                    act.wait_ge(d_dve, 7 * b + 7)
                    nc.scalar.activation(sw_[B], ss_[B], ACT.Exp).then_inc(d_prob, 1)
                    act.wait_ge(d_T, b + 1)
                    nc.scalar.copy(pT[:, 0:2, :], ps[:, 5, 0:2 * P].rearrange("p (c r) -> p c r", r=P)).then_inc(d_Tc, 1)

            def dve_sample(dve, stepno):
                def place_queries(b):
                    if b:
                        dve.wait_ge(d_S, b)
                    for half in range(2):
                        rows = slice(64 * half, 64 * half + 64)
                        nc.vector.tensor_copy(qblk[rows, :, half * TD:(half + 1) * TD],
                                              qT[rows, :, b * TD:(b + 1) * TD]).then_inc(d_blk, 1)

                def take_scores(b):
                    dve.wait_ge(d_S, b + 1)
                    if b:
                        dve.wait_ge(d_prob, 2 * b)
                    nc.vector.tensor_tensor(ss_, ps[:, 4, 0:KS], smask, ALU.add).then_inc(d_Sr, 1)
                    dve.wait_ge(d_Sr, b + 1)
                    nc.vector.reduce_max(smx[A, :], ss_[A], AX).then_inc(d_dve, 1)
                    dve.wait_ge(d_dve, 7 * b + 1)
                    nc.vector.tensor_scalar_mul(snm[A, :], smx[A, :], -1.0).then_inc(d_dve, 1)

                def make_probabilities(b):
                    dve.wait_ge(d_act, 4 * b + 4)
                    nc.vector.reciprocal(srl[A, :], sl_[A, :]).then_inc(d_dve, 1)
                    nc.vector.scalar_tensor_tensor(out=se_[B], in0=ss_[B], scalar=0.0, in1=se_[B], op0=ALU.max, op1=ALU.add).then_inc(d_dve, 1)
                    dve.wait_ge(d_dve, 7 * b + 4)
                    if b:
                        dve.wait_ge(d_T, b)
                    nc.vector.tensor_scalar_mul(sw_[A], se_[A], srl[A, :]).then_inc(d_prob, 1)
                    nc.vector.tensor_tensor_scan(out=sw_[B, ::-1], data0=se_[B, ::-1], data1=se_[B, ::-1], initial=0.0,
                                                 op0=ALU.add, op1=ALU.bypass).then_inc(d_dve, 1)
                    dve.wait_ge(d_dve, 7 * b + 5)
                    nc.vector.tensor_tensor(ss_[B], ss_[B], sw_[B], ALU.subtract).then_inc(d_dve, 2)

                def join_maps(b):
                    dve.wait_ge(d_Tc, b + 1)
                    nc.vector.tensor_copy(pT[0:TD, 2, :], ps[0:TD, 5, 2 * P:3 * P]).then_inc(d_new, 1)
                    dve.wait_ge(d_new, b + 1)
                    for c, kc in enumerate(KC):
                        two = pT[0:kc, c, 0:64].rearrange("p (h m q) -> p h m q", m=2, q=TD)
                        m = nc.vector.scalar_tensor_tensor(out=pd[0:kc, c, :].rearrange("p (h q) -> p h q", q=TD),
                                                           in0=two[:, :, 1, :], scalar=neg_lam[0:kc, :],
                                                           in1=two[:, :, 0, :], op0=ALU.mult, op1=ALU.add)
                    m.then_inc(d_pd, 1)

                def take_o(b):
                    dve.wait_ge(d_O, b + 1)
                    if b:
                        dve.wait_ge(d_store, 16 * b * (HA + HB))
                    nc.vector.tensor_copy(oa, ps[0:HA * TD, 6, :]).then_inc(d_Oc, 1)
                    nc.vector.tensor_copy(ob, ps[0:HB * TD, 7, :]).then_inc(d_Oc, 1)

                b, second = (stepno - 1) // 2, (stepno - 1) % 2
                if stepno == 0:
                    dve.wait_ge(s_Oc, NPT * 2)
                    nc.vector.memset(qblk_flat, 0.0).then_inc(d_zero, 1)
                    dve.wait_ge(d_qTc, 1)
                    dve.wait_ge(d_zero, 1)
                    place_queries(0)
                    dve.wait_ge(d_mask, 16 * (2 * HA + HB))
                elif second == 0:
                    if b >= 1:
                        join_maps(b - 1)
                    if b < NB_DEC:
                        take_scores(b)
                        if b + 1 < NB_DEC:
                            place_queries(b + 1)
                else:
                    if b >= 1:
                        take_o(b - 1)
                    if b < NB_DEC:
                        make_probabilities(b)

            PIECES = ("norm_o", "scale_o", "turn_o", "branch_a", "branch_b", "mix", "turn_m", "out_1", "out_2", "residual",
                      "norm_x", "turn_x", "query_1", "query_2", "turn_q", "score", "key_1", "key_2", "key_3", "key_4", "key_5",
                      "pair_1", "pair_2", "pair_3", "pair_4", "pair_5", "pair_6", "gate", "pick_1", "pick_2", "choose", "")

            def tiles_of(eng, step):
                step(0, CH)
                with eng.Fori(1, NPT // 2) as t:
                    step(t, CH)
                with eng.Fori(NPT // 2, NPT) as t:
                    step(t, SEQ)
                step(NPT, None)
                step(NPT + 1, None)

            def before(t):
                return None if isinstance(t, int) and t == 0 else t - 1

            def mixes(t):
                return not (isinstance(t, int) and t > NPT)

            with nc.Block() as block:
                @block.sync
                def _(sp):
                    def step(t, kw):
                        if kw:
                            sync_attend(sp, t, kw)
                        elif mixes(t):
                            sync_sample(sp)
                        if mixes(t):
                            sync_merge(sp, t)
                        if before(t) is not None:
                            sync_finish(sp, before(t))

                    sp.sem_inc(s_yst, 16)
                    tiles_of(sp, step)
                    sp.wait_ge(s_yst, 16 * (NPT + 2))

                @block.gpsimd
                def _(pool):
                    with pool.Fori(0, NPT) as e:
                        pool_experts(pool, e)
                    pool_experts(pool, NPT)

                @block.tensor
                def _(pe):
                    pe.sem_inc(s_sum, len(TSUM))
                    pe.sem_inc(s_vsum, len(VSUM))
                    pe.sem_inc(s_yc, 1)

                    def step(t, kw):
                        if kw:
                            pe_attend(pe, t, kw)
                        elif mixes(t):
                            pe_sample(pe)
                        for k, piece in enumerate(PIECES):
                            if mixes(t):
                                pe_merge(pe, t, piece)
                            if before(t) is not None:
                                pe_experts(pe, before(t), k)

                    tiles_of(pe, step)

                @block.scalar
                def _(act):
                    def step(t, kw):
                        if kw:
                            act_attend(act, t, kw)
                        elif mixes(t):
                            act_sample(act)
                        if before(t) is not None:
                            act_gelu(act, before(t))
                        for k, piece in enumerate(PIECES):
                            if before(t) is not None:
                                act_experts(act, before(t), k)
                            if mixes(t):
                                act_merge(act, t, piece)
                        if before(t) is not None:
                            act_finish(act, before(t))

                    tiles_of(act, step)

                @block.vector
                def _(dve):
                    def step(t, kw):
                        parts = 16 if kw else 2 * NB_DEC + 3
                        for g in range(parts):
                            if before(t) is not None:
                                dve_dots(dve, before(t), g * NSLOT // parts, (g + 1) * NSLOT // parts)
                                if g == parts // 2:
                                    dve_keep_idx(dve, before(t))
                            if kw:
                                dve_attend(dve, t, g // 2, g % 2, kw)
                            elif mixes(t):
                                dve_sample(dve, g)
                        if before(t) is not None:
                            dve_weights(dve, before(t))
                        for k, piece in enumerate(PIECES):
                            if mixes(t):
                                dve_merge(dve, t, piece)
                            if before(t) is not None:
                                dve_experts(dve, before(t), k)
                        if before(t) is not None:
                            dve_finish(dve, before(t), 0)
                            dve_finish(dve, before(t), 1)

                    tiles_of(dve, step)



OUTS = [(1, SEQ, D), (NB_DEC, TD, D),
        (1, 1, SEQ, HA, 128), (1, 1, SEQ, HA, 128), (1, 1, SEQ, HB, 64), (1, 1, SEQ, HB, 64),
        (1, NB_DEC, TD, HA, 128), (1, NB_DEC, TD, HA, 128), (1, NB_DEC, TD, HB, 64), (1, NB_DEC, TD, HB, 64)]


def kernel(**inputs):
    import concourse.bacc as bacc
    from concourse.bass_utils import run_bass_kernel_spmd

    nc = bacc.Bacc("TRN2", target_bir_lowering=False, num_devices=1)
    arrays, args = {}, {}
    given = {name: np.ascontiguousarray(v) for name, v in inputs.items()}
    given["distance_onehot"] = distance_onehot()
    given["mask_rows"] = mask_rows()
    for name, v in given.items():
        arrays[f"in_{name}"] = v
        args[name] = nc.dram_tensor(f"in_{name}", v.shape, mybir.dt.from_np(v.dtype), kind="ExternalInput").ap()
    outs = [nc.dram_tensor(f"out_{n}", shape, F32, kind="ExternalOutput").ap() for n, shape in enumerate(OUTS)]
    build(nc, args, outs)
    r = run_bass_kernel_spmd(nc, [arrays], core_ids=[0])
    return tuple(r.results[0][f"out_{n}"] for n in range(len(OUTS)))
```

```python
from contextlib import ExitStack

import numpy as np

import concourse.bass as bass
from concourse import mybir

F32 = mybir.dt.float32
U32 = mybir.dt.uint32
I32 = mybir.dt.int32
ALU = mybir.AluOpType
ACT = mybir.ActivationFunctionType
AX = mybir.AxisListType.X
ds = bass.ds

P = 128
D = 1024
KD = D // P
NPT = 8
NS = 64
SEQ = NPT * P
T = SEQ + NS
W_IN = 5120
CH = 512
NCH = W_IN // CH
HA = 4
HB = 8
NB_DEC = 8
TD = 8
SLABW = 2 * SEQ - P
PAGES = 2
PAST = PAGES * P
KS = PAST + TD
PH = 8
TK = 16
NSLOT = PH * TK
R = 8
ATT_PARTS = 18
ATT_LEAD = 1
DEC_PARTS = 2 * NB_DEC + 4
NDG = 4
VSUM = (1, 4, 6)
TSUM = tuple(r for r in range(R) if r not in VSUM)
BUCKETS = 32
MAXD = 128
EPS = 1e-6
QA, KA, VA, QB, KB, VB, GA, GB = 0, 512, 1024, 1536, 2048, 2560, 3072, 4096
NEG = -1e30
LOWEST = -3.0e38
LAM_INIT = 0.2
RELW = 2 * SEQ


def distance_onehot():
    rel = (SEQ - 1) - np.arange(RELW)
    n = np.maximum(rel, 0)
    exact = BUCKETS // 2
    ratio = np.log(np.maximum(n, 1).astype(np.float32) / np.float32(exact)) / np.float32(np.log(MAXD / exact))
    large = np.minimum(exact + (ratio * (BUCKETS - exact)).astype(np.int32), BUCKETS - 1)
    bucket = np.where(n < exact, n, large)
    hot = np.zeros((BUCKETS + 2, RELW), np.float32)
    hot[bucket, np.arange(RELW)] = 1.0
    hot[BUCKETS, rel < 0] = 1.0
    hot[BUCKETS + 1, rel == 0] = 1.0
    return hot


def mask_rows():
    rows = np.zeros((BUCKETS + 2, HA + 1), np.float32)
    rows[BUCKETS, :] = NEG
    rows[BUCKETS + 1, HA] = NEG
    return rows


def build(nc, a, o):
    ctx = ExitStack()
    nc.disable_value_cache = True

    def dram(name, shape):
        return nc.dram_tensor(name, shape, F32, kind="Internal").ap()

    def semaphore(name):
        return ctx.enter_context(nc.semaphore(name))

    proj_d = dram("proj_d", (T, W_IN))
    attn_d = dram("attn_d", (NS, D))
    dist_d = dram("dist_d", (HA + 1, RELW))
    slab_d = dram("slab_d", (HA + 1, P, SLABW))

    x_all = [a["x_prompt"].rearrange("b s d -> (b s) d"), a["x_sample"].rearrange("b s d -> (b s) d")]
    w_in = a["w_in"][0].rearrange("(k p) n -> p k n", p=P)
    y_out = [o[0].rearrange("b s d -> (b s) d"), o[1].rearrange("b s d -> (b s) d")]
    kv_out = [[o[n].rearrange("l b s h e -> (l b s) (h e)") for n in group] for group in ((2, 3, 4, 5), (6, 7, 8, 9))]

    with ctx:
        ps = ctx.enter_context(nc.psum_tensor("ps", [P, 8, CH], F32))

        def both(b):
            return ps[:, b:b + 2, :].rearrange("p b c -> p (b c)")

        def keep(name, shape, dt=F32):
            return ctx.enter_context(nc.sbuf_tensor(name, shape, dt))

        ident = keep("ident", [P, P])
        gain_mix = keep("gain_mix", [P, D])
        gain_sub = keep("gain_sub", [P, P])
        neg_lam = keep("neg_lam", [P, 1])
        eps_t = keep("eps_t", [P, 1])
        one_t = keep("one_t", [P, 1])
        subkT = keep("subkT", [P, PH, 2 * P])
        iota16 = keep("iota16", [P, TK])
        half_scale = keep("half_scale", [P, 2])

        with ExitStack() as stage:
            def sb(name, shape, dt=F32):
                return stage.enter_context(nc.sbuf_tensor(name, shape, dt))

            hot = sb("hot", [BUCKETS + 2, RELW])
            table = sb("table", [BUCKETS + 2, HA + 1])
            dist = sb("dist", [HA + 1, RELW])
            lams = sb("lams", [P, 4, 64])
            prod = sb("prod", [P, 2, 64])
            dots = sb("dots", [P, 2])
            expd = sb("expd", [P, 2])
            diff = sb("diff", [P, 1])
            subk = sb("subk", [P, PH, 2, 64])
            s_mask = semaphore("c_mask")
            s_gain = semaphore("c_gain")
            s_lam = semaphore("c_lam")
            s_subk = semaphore("c_subk")
            s_tab = semaphore("c_tab")
            s_ident = semaphore("c_ident")
            s_zero = semaphore("c_zero")
            s_dot = semaphore("c_dot")
            s_exp = semaphore("c_exp")
            s_link = semaphore("c_link")
            s_dist = semaphore("c_dist")
            s_dcopy = semaphore("c_dcopy")
            s_skT = semaphore("c_skT")
            s_skc = semaphore("c_skc")
            s_store = semaphore("c_store")

            with nc.Block() as block:
                @block.sync
                def _(sp):
                    sp.dma_start(table[:], a["mask_rows"]).then_inc(s_mask, 16)
                    sp.dma_start(hot[:], a["distance_onehot"]).then_inc(s_tab, 16)
                    sp.wait_ge(s_mask, 16)
                    sp.dma_start(table[0:BUCKETS, 0:HA], a["rel_bias"], allow_slow_non_contiguous=True).then_inc(s_tab, 16)
                    sp.dma_start(subk[:], a["peer_sub_keys"][0].rearrange("h c n e -> n h c e")).then_inc(s_subk, 16)
                    for n, name in enumerate(("lambda_q1", "lambda_k1", "lambda_q2", "lambda_k2")):
                        sp.dma_start(lams[:, n, :], a[name][0:1, :].broadcast_to([P, 64])).then_inc(s_lam, 16)
                    sp.dma_start(gain_mix[:], a["norm_mix"][0:1, :].broadcast_to([P, D])).then_inc(s_gain, 16)
                    sp.dma_start(gain_sub[:], a["subln_gain"][0:1, :].broadcast_to([P, P])).then_inc(s_gain, 16)
                    sp.wait_ge(s_dcopy, 4)
                    sp.dma_start(dist_d[:, :], dist[:]).then_inc(s_store, 16)
                    sp.wait_ge(s_store, 16)
                    sp.wait_ge(s_gain, 32)

                @block.gpsimd
                def _(pool):
                    pool.memset(ident[:], 0.0).then_inc(s_zero, 1)
                    pool.memset(subkT[:], 0.0).then_inc(s_zero, 1)
                    pool.memset(eps_t[:], EPS).then_inc(s_zero, 1)
                    pool.memset(one_t[:], 1.0).then_inc(s_zero, 1)
                    pool.iota(iota16[:], pattern=[[1, TK]], base=0, channel_multiplier=0,
                              allow_small_or_imprecise_dtypes=True).then_inc(s_zero, 1)
                    pool.wait_ge(s_zero, 1)
                    pool.affine_select(out=ident[:], in_=ident[:], compare_op=ALU.not_equal, fill=1.0,
                                       base=0, pattern=[[-1, P]], channel_multiplier=1).then_inc(s_ident, 1)

                @block.tensor
                def _(pe):
                    pe.wait_ge(s_tab, 32)
                    for c in range(4):
                        nc.tensor.matmul(ps[0:HA + 1, c, :], table[:], hot[:, c * CH:(c + 1) * CH],
                                         start=True, stop=True).then_inc(s_dist, 1)
                    pe.wait_ge(s_ident, 1)
                    pe.wait_ge(s_subk, 16)
                    for h in range(PH):
                        nc.tensor.transpose(ps[:, 4 + h // 4, (h % 4) * P:(h % 4 + 1) * P],
                                            subk[:, h].rearrange("n c e -> n (c e)"), ident[:]).then_inc(s_skT, 1)

                @block.vector
                def _(dve):
                    for m in range(2):
                        nc.vector.memset(half_scale[64 * m:64 * m + 64, m:m + 1], 0.125)
                        nc.vector.memset(half_scale[64 * m:64 * m + 64, 1 - m:2 - m], 0.0)
                    for c in range(4):
                        dve.wait_ge(s_dist, c + 1)
                        nc.vector.tensor_copy(dist[:, c * CH:(c + 1) * CH], ps[0:HA + 1, c, :]).then_inc(s_dcopy, 1)
                    dve.wait_ge(s_lam, 64)
                    for n in range(2):
                        nc.vector.tensor_tensor_reduce(out=prod[:, n, :], in0=lams[:, 2 * n, :], in1=lams[:, 2 * n + 1, :],
                                                       scale=1.0, scalar=0.0, op0=ALU.mult, op1=ALU.add,
                                                       accum_out=dots[:, n:n + 1]).then_inc(s_dot, 1)
                    dve.wait_ge(s_exp, 1)
                    nc.vector.tensor_tensor(diff[:], expd[:, 1:2], expd[:, 0:1], ALU.subtract).then_inc(s_link, 1)
                    dve.wait_ge(s_link, 1)
                    nc.vector.tensor_scalar_add(neg_lam[:], diff[:], -LAM_INIT).then_inc(s_link, 1)
                    dve.wait_ge(s_gain, 32)
                    nc.vector.tensor_scalar_mul(gain_sub[:], gain_sub[:], 1.0 - LAM_INIT).then_inc(s_link, 1)
                    dve.wait_ge(s_skT, PH)
                    dve.wait_ge(s_zero, 2)
                    for half in range(2):
                        rows = slice(64 * half, 64 * half + 64)
                        nc.vector.tensor_copy(subkT[rows, :, half * P:(half + 1) * P],
                                              both(4)[rows, :].rearrange("p (h n) -> p h n", n=P)).then_inc(s_skc, 1)

                @block.scalar
                def _(act):
                    act.wait_ge(s_dot, 2)
                    nc.scalar.activation(expd[:], dots[:], ACT.Exp).then_inc(s_exp, 1)

        keyT = keep("keyT", [P, KD, SEQ])
        with ExitStack() as stage:
            def sb(name, shape, dt=F32):
                return stage.enter_context(nc.sbuf_tensor(name, shape, dt))

            WB = KD // 4
            xhi = sb("xhi", [P, KD, T])
            xlo = sb("xlo", [P, KD, T])
            whi = sb("whi", [P, 2, KD, CH])
            wlo = sb("wlo", [P, 2, KD, CH])
            wraw = sb("wraw", [P, 2, WB, CH])
            kst = sb("kst", [P, 2, D])
            pout = sb("pout", [P, 3, CH])
            ssum = sb("ssum", [P, 2])
            rms = sb("rms", [P, 2])
            rstd = sb("rstd", [P, 2])
            HW = SLABW // 2
            room = keyT[:].rearrange("p u k -> p (u k)")
            bounds = np.cumsum([0, 2 * D, 2 * D, D, 2 * HW, HW, P])
            assert bounds[-1] <= KD * SEQ
            xin, xn, sq, climb, slab, flip = (room[:, int(b0):int(b1)] for b0, b1 in zip(bounds, bounds[1:]))
            xin = xin.rearrange("p (b c) -> p b c", b=2)
            xn = xn.rearrange("p (b c) -> p b c", b=2)
            climb = climb.rearrange("p (b c) -> p b c", b=2)
            s_x = [semaphore(f"p_x{n}") for n in range(2)]
            s_w = [semaphore(f"p_w{n}") for n in range(2)]
            s_sum = semaphore("p_sum")
            s_rms = semaphore("p_rms")
            s_rstd = semaphore("p_rstd")
            s_xn = semaphore("p_xn")
            s_xT = semaphore("p_xT")
            s_xhi = semaphore("p_xhi")
            s_xlo = semaphore("p_xlo")
            s_whi = semaphore("p_whi")
            s_wlo = semaphore("p_wlo")
            s_mm = semaphore("p_mm")
            s_ev = semaphore("p_ev")
            s_st = [semaphore(f"p_st{n}") for n in range(3)]
            s_turn_pool = semaphore("p_turn_pool")
            s_turn_act = semaphore("p_turn_act")
            s_turn_dve = semaphore("p_turn_dve")
            s_turn_sp = semaphore("p_turn_sp")
            s_turn_pe = semaphore("p_turn_pe")
            s_climb = [semaphore(f"k_climb{n}") for n in range(2)]
            s_flip = semaphore("k_flip")
            s_flipped = semaphore("k_flipped")
            s_slab = semaphore("k_slab")
            s_slab_out = semaphore("k_slab_out")
            s_k = [semaphore(f"k_k{n}") for n in range(2)]
            s_kT = semaphore("k_kT")
            s_kTc = semaphore("k_kTc")

            tiles = [(t, P) for t in range(NPT)] + [(NPT, NS)]
            NT = len(tiles)
            NSL = 2 * (HA + 1)
            LATE = 3
            KEY_AT = (2, 6, 10, 14)

            def key_tile(i, j):
                return (i - LATE) * 4 + j

            def as_f32r(ap):
                return ap.bitcast(mybir.dt.float32r)

            with nc.Block() as block:
                def load_x(sp, t):
                    src = x_all[0][t * P:(t + 1) * P, :] if t < NPT else x_all[1]
                    sp.dma_start(xin[0:tiles[t][1], t % 2, :], src).then_inc(s_x[t % 2], 16)

                W_AFTER_X = {2: ((0, 2), (0, 3)), 5: ((1, 0), (1, 1)), 6: ((1, 2), (1, 3))}

                def load_w(sp, i, n, q):
                    col = sp.snap(i * (2 * CH) + n * CH)
                    if not isinstance(i, int) or 4 * n + q >= 2:
                        sp.wait_ge(s_wlo, i * 8 + 4 * n + q - 1)
                        sp.sem_inc(s_turn_sp, 1)
                    sp.dma_start(wraw[:, q % 2], w_in[:, q * WB:(q + 1) * WB, ds(col, CH)]).then_inc(s_w[q % 2], 16)

                def load_climb(eng, n):
                    if n >= 2:
                        eng.wait_ge(s_flipped, 2 * (n - 1))
                    eng.dma_start(climb[:, n % 2, :], bass.AP(tensor=dist_d.tensor, offset=(n // 2) * RELW + (n % 2) * HW,
                                                              ap=[[1, P], [1, HW]])).then_inc(s_climb[n % 2], 16)

                def store_slab(eng, n):
                    eng.wait_ge(s_slab, 2 * n + 2)
                    eng.dma_start(slab_d[n // 2, :, (n % 2) * HW:(n % 2 + 1) * HW], slab).then_inc(s_slab_out, 16)

                @block.sync
                def _(sp):
                    load_x(sp, 0)
                    load_x(sp, 1)
                    load_w(sp, 0, 0, 0)
                    load_w(sp, 0, 0, 1)
                    for t in range(2, NT):
                        sp.wait_ge(s_xn, t - 1)
                        load_x(sp, t)
                        for n, q in W_AFTER_X.get(t, ()):
                            load_w(sp, 0, n, q)
                    with sp.Fori(1, LATE) as i:
                        for n in range(2):
                            for q in range(4):
                                load_w(sp, i, n, q)
                    with sp.Fori(LATE, NCH // 2) as i:
                        for n in range(2):
                            for q in range(4):
                                load_w(sp, i, n, q)
                        for n in range(3):
                            sp.wait_ge(s_st[n], 16 * 2 * LATE * NT // 3)
                        for j in range(4):
                            first = sp.snap(key_tile(i, j) * P)
                            sp.wait_ge(s_kT, key_tile(i, j) * 2 + 2)
                            sp.sem_inc(s_turn_sp, 1)
                            for n, col in enumerate((KA, KB)):
                                sp.dma_start(kst[:, j % 2, n * CH:(n + 1) * CH],
                                             proj_d[ds(first, P), col:col + CH]).then_inc(s_k[j % 2], 16)

                @block.gpsimd
                def _(pool):
                    pool.memset(flip, 0.0).then_inc(s_flip, 1)
                    pool.wait_ge(s_flip, 1)
                    pool.affine_select(out=flip, in_=flip, compare_op=ALU.not_equal, fill=1.0,
                                       base=1 - P, pattern=[[1, P]], channel_multiplier=1).then_inc(s_flip, 1)
                    with pool.Fori(0, NCH // 2) as i:
                        for c in range(2):
                            for t, rows in tiles:
                                k = c * NT + t
                                col = pool.snap(i * (2 * CH) + c * CH)
                                pool.wait_ge(s_ev, i * (2 * NT) + k + 1)
                                pool.sem_inc(s_turn_pool, 1)
                                pool.dma_start(proj_d[t * P:t * P + rows, ds(col, CH)],
                                               pout[0:rows, k % 3, :]).then_inc(s_st[k % 3], 16)
                    for n in range(3):
                        pool.wait_ge(s_st[n], 16 * NCH * NT // 3)

                @block.vector
                def _(dve):
                    def norm(t):
                        rows, b = tiles[t][1], t % 2
                        dve.wait_ge(s_x[b], 16 * (t // 2 + 1))
                        if t:
                            dve.wait_ge(s_sum, t)
                        nc.vector.tensor_tensor_reduce(out=sq[0:rows, :], in0=xin[0:rows, b, :], in1=xin[0:rows, b, :],
                                                       scale=1.0, scalar=0.0, op0=ALU.mult, op1=ALU.add,
                                                       accum_out=ssum[0:rows, b:b + 1]).then_inc(s_sum, 1)

                    def norm_end(t):
                        rows, b = tiles[t][1], t % 2
                        dve.wait_ge(s_rms, t + 1)
                        nc.vector.reciprocal(rstd[0:rows, b:b + 1], rms[0:rows, b:b + 1]).then_inc(s_rstd, 1)
                        dve.wait_ge(s_rstd, t + 1)
                        if t >= 2:
                            dve.wait_ge(s_xT, 2 * (t - 1))
                        nc.vector.scalar_tensor_tensor(out=xn[0:rows, b, :], in0=xin[0:rows, b, :],
                                                       scalar=rstd[0:rows, b:b + 1], in1=gain_mix[0:rows, :],
                                                       op0=ALU.mult, op1=ALU.mult).then_inc(s_xn, 1)

                    def split_x(t):
                        rows = tiles[t][1]
                        for g in range(2):
                            dst = slice(4 * g, 4 * g + 4), slice(t * P, t * P + rows)
                            dve.wait_ge(s_xhi, 2 * t + g + 1)
                            src = ps[:, g, :].rearrange("p (k r) -> p k r", r=P)[:, :, 0:rows]
                            nc.vector.tensor_tensor(as_f32r(xlo[:, dst[0], dst[1]]), src, xhi[:, dst[0], dst[1]],
                                                    ALU.subtract).then_inc(s_xlo, 1)

                    def split_w(i, n, q):
                        if not isinstance(i, int) or i:
                            dve.wait_ge(s_mm, i * (2 * NT) + (n - 1) * NT)
                            dve.sem_inc(s_turn_dve, 1)
                        blocks = slice(q * WB, (q + 1) * WB)
                        dve.wait_ge(s_w[q % 2], i * 64 + 32 * n + 16 * (q // 2 + 1))
                        dve.sem_inc(s_turn_dve, 1)
                        nc.vector.tensor_copy(as_f32r(whi[:, n, blocks, :]), wraw[:, q % 2]).then_inc(s_whi, 1)
                        dve.wait_ge(s_whi, i * 8 + 4 * n + q + 1)
                        dve.sem_inc(s_turn_dve, 1)
                        nc.vector.tensor_tensor(as_f32r(wlo[:, n, blocks, :]), wraw[:, q % 2], whi[:, n, blocks, :],
                                                ALU.subtract).then_inc(s_wlo, 1)

                    SPLIT_AFTER_X = {0: ((0, 0), (0, 1)), 1: ((0, 2), (0, 3)), 5: ((1, 0), (1, 1)), 6: ((1, 2), (1, 3))}
                    for t in range(NT + 1):
                        if t < NT:
                            norm(t)
                        if 1 <= t:
                            split_x(t - 1)
                        if t < NT:
                            norm_end(t)
                        for n, q in SPLIT_AFTER_X.get(t, ()):
                            split_w(0, n, q)
                    for n in range(NSL):
                        for c in range(2):
                            dve.wait_ge(s_flipped, 2 * n + c + 1)
                            if n and c == 0:
                                dve.wait_ge(s_slab_out, 16 * n)
                            nc.vector.tensor_copy(slab[:, c * (HW // 2):(c + 1) * (HW // 2)], ps[:, c, 0:HW // 2]).then_inc(s_slab, 1)
                        if n % 2 == 0 and n:
                            split_w(1, 0, n // 2 - 1)
                    for q in range(4):
                        split_w(1, 1, q)
                    with dve.Fori(2, NCH // 2) as i:
                        for n in range(2):
                            for q in range(4):
                                split_w(i, n, q)

                @block.scalar
                def _(act):
                    def root(t):
                        rows, b = tiles[t][1], t % 2
                        act.wait_ge(s_sum, t + 1)
                        nc.scalar.activation(rms[0:rows, b:b + 1], ssum[0:rows, b:b + 1], ACT.Sqrt,
                                             bias=eps_t[0:rows, :], scale=1.0 / D).then_inc(s_rms, 1)

                    def take_x(t):
                        rows = tiles[t][1]
                        for g in range(2):
                            act.wait_ge(s_xT, 2 * t + g + 1)
                            nc.scalar.copy(as_f32r(xhi[:, 4 * g:4 * g + 4, t * P:t * P + rows]),
                                           ps[:, g, :].rearrange("p (k r) -> p k r", r=P)[:, :, 0:rows]).then_inc(s_xhi, 1)

                    def take(k, i):
                        rows = tiles[k % NT][1]
                        act.wait_ge(s_mm, i * (2 * NT) + k + 1)
                        act.sem_inc(s_turn_act, 1)
                        if k >= 3 or not isinstance(i, int):
                            act.wait_ge(s_st[k % 3], i * (16 * 2 * NT // 3) + 16 * (k // 3))
                        nc.scalar.copy(pout[0:rows, k % 3, :], ps[0:rows, k % 6 + 2, :]).then_inc(s_ev, 1)

                    root(0)
                    for t, _rows in tiles:
                        take_x(t)
                        if t + 1 < NT:
                            root(t + 1)
                        if t:
                            take(t - 1, 0)
                    load_climb(act, 0)
                    load_climb(act, 1)
                    for k in range(NT - 1, 2 * NT):
                        take(k, 0)
                        if k > NT:
                            store_slab(act, k - NT - 1)
                            if k - NT + 1 < NSL:
                                load_climb(act, k - NT + 1)
                    store_slab(act, NSL - 2)
                    store_slab(act, NSL - 1)
                    with act.Fori(1, LATE) as i:
                        for k in range(2 * NT):
                            take(k, i)
                    act.wait_ge(s_slab_out, 16 * NSL)
                    with act.Fori(LATE, NCH // 2) as i:
                        for k in range(2 * NT):
                            take(k, i)
                            if k in KEY_AT:
                                kt = key_tile(i, KEY_AT.index(k))
                                first = act.snap(kt * P)
                                for g in range(2):
                                    act.wait_ge(s_kT, kt * 2 + g + 5)
                                    act.sem_inc(s_turn_act, 1)
                                    nc.scalar.copy(keyT[:, 4 * g:4 * g + 4, ds(first, P)],
                                                   ps[:, g, :].rearrange("p (u r) -> p u r", r=P)).then_inc(s_kTc, 1)

                @block.tensor
                def _(pe):
                    pe.sem_inc(s_kTc, 2)
                    pe.sem_inc(s_kT, 4)

                    def turn_x(t):
                        rows = tiles[t][1]
                        pe.wait_ge(s_xn, t + 1)
                        for g in range(2):
                            if t:
                                pe.wait_ge(s_xlo, 2 * (t - 1) + g + 1)
                            for k in range(4):
                                kt = 4 * g + k
                                m = nc.tensor.transpose(ps[:, g, k * P:k * P + rows],
                                                        xn[0:rows, t % 2, kt * P:(kt + 1) * P], ident[0:rows, 0:rows])
                            m.then_inc(s_xT, 1)

                    def product(k, i):
                        c, (t, rows) = k // NT, tiles[k % NT]
                        if t == 0:
                            pe.wait_ge(s_wlo, i * 8 + 4 * c + 4)
                        if not isinstance(i, int):
                            pe.wait_ge(s_ev, i * (2 * NT) + k - 5)
                        elif k >= 6:
                            pe.wait_ge(s_ev, k - 5)
                        n = 0
                        for xp, wp in ((xlo, whi), (xhi, wlo), (xhi, whi)):
                            for kt in range(KD):
                                m = nc.tensor.matmul(ps[0:rows, k % 6 + 2, :], as_f32r(xp[:, kt, t * P:t * P + rows]),
                                                     as_f32r(wp[:, c, kt, :]), start=(n == 0), stop=(n == 3 * KD - 1))
                                n += 1
                        m.then_inc(s_mm, 1)

                    def flip_rows(n):
                        if n == 0:
                            pe.wait_ge(s_xlo, 2 * NT)
                            pe.wait_ge(s_flip, 2)
                        pe.wait_ge(s_climb[n % 2], 16 * (n // 2 + 1))
                        for c in range(2):
                            if n:
                                pe.wait_ge(s_slab, 2 * (n - 1) + c + 1)
                            nc.tensor.matmul(ps[:, c, 0:HW // 2], flip, climb[:, n % 2, c * (HW // 2):(c + 1) * (HW // 2)],
                                             start=True, stop=True).then_inc(s_flipped, 1)

                    turn_x(0)
                    for t in range(NT):
                        if t + 1 < NT:
                            turn_x(t + 1)
                        pe.wait_ge(s_xlo, 2 * t + 2)
                        product(t, 0)
                    for k in range(NT, 2 * NT):
                        product(k, 0)
                        flip_rows(k - NT)
                    flip_rows(NSL - 1)
                    with pe.Fori(1, LATE) as i:
                        for k in range(2 * NT):
                            product(k, i)
                    pe.wait_ge(s_slab, 2 * NSL)
                    with pe.Fori(LATE, NCH // 2) as i:
                        for k in range(2 * NT):
                            product(k, i)
                            if k in KEY_AT:
                                j = KEY_AT.index(k)
                                pe.wait_ge(s_k[j % 2], (i - LATE) * 64 + 32 * (j // 2 + 1))
                                for g in range(2):
                                    pe.wait_ge(s_kTc, key_tile(i, j) * 2 + g + 1)
                                    pe.sem_inc(s_turn_pe, 1)
                                    for q in range(4):
                                        u = 4 * g + q
                                        m = nc.tensor.transpose(ps[:, g, q * P:(q + 1) * P],
                                                                kst[:, j % 2, u * P:(u + 1) * P], ident[:])
                                    m.then_inc(s_kT, 1)

        val = keep("val", [P, NPT, D])
        gain_ffn = keep("gain_ffn", [P, D])
        gain_fin = keep("gain_fin", [P, D])
        with ExitStack() as stage:
            def sb(name, shape, dt=F32):
                return stage.enter_context(nc.sbuf_tensor(name, shape, dt))

            ring = sb("t_ring", [P, R, D])
            big = sb("t_big", [P, 11, D])
            pTr = sb("t_pTr", [P, KD, P])
            o_sb = sb("t_o_sb", [P, D])
            h_sb = sb("t_h_sb", [P, D])
            xn_sb = sb("t_xn_sb", [P, D])
            y_sb = sb("t_y_sb", [P, D])

            def slots(n, m):
                return big[:, n:m, :].rearrange("p a c -> p (a c)")

            bias = big[:, 0:2, :]
            bmask = big[:, 2, :]
            z = big[:, 3:5, :]
            soft = big[:, 5:7, :]
            prob = big[:, 7:9, :]
            qz = slots(9, 11).rearrange("p (u m r) -> p u m r", m=2, r=P)
            x_sb = big[:, 0, :]
            sq = big[:, 1, :]
            wring = big[:, 3:7, :]
            mixed = big[:, 7, :]
            gates = slots(9, 11)
            q_sb = big[:, 8, :]
            left = slots(9, 11)
            cand = slots(7, 9)
            pick = slots(0, 2)
            ysq = big[:, 8, :]
            mx = sb("t_mx", [P, 2])
            nm = sb("t_nm", [P, 2])
            l = sb("t_l", [P, 2])
            rl = sb("t_rl", [P, HA, 2])
            rl2 = sb("t_rl2", [P, 1])
            ssh, rmsh, rsh = (sb("t_" + n, [P, HA]) for n in ("ssh", "rmsh", "rsh"))
            ssx, rmsx, rsx = (sb("t_" + n, [P, 1]) for n in ("ssx", "rmsx", "rsx"))
            ssy, rmsy, rsy = (sb("t_" + n, [P, 1]) for n in ("ssy", "rmsy", "rsy"))
            top = sb("t_top", [P, 2 * PH, TK])
            topi = sb("t_topi", [P, 2 * PH, TK], U32)
            topf = sb("t_topf", [P, 2 * PH, TK])
            best = sb("t_best", [P, PH, TK])
            bestj = sb("t_bestj", [P, NSLOT], U32)
            ja = sb("t_ja", [P, 2, NSLOT], U32)
            jf = sb("t_jf", [P, 2, NSLOT])
            sel = sb("t_sel", [P, 2, NSLOT])
            idx_u = sb("t_idx_u", [P, NSLOT], U32)
            idx_v = sb("t_idx_v", [P, NSLOT], U32)
            gexp = sb("t_gexp", [P, PH, TK])
            gsum = sb("t_gsum", [P, PH])
            grec = sb("t_grec", [P, PH])
            gate = sb("t_gate", [P, PH, TK])
            gate_flat = gate[:].rearrange("p h k -> p (h k)")
            fold = sb("t_fold", [P, NS])
            dots = sb("t_dots", [P, NSLOT])
            act_u = sb("t_act_u", [P, NSLOT])
            wgt = sb("t_wgt", [P, NSLOT])
            diag = sb("t_diag", [P, NDG, P])

            s_qin = semaphore("a_qin")
            s_v = semaphore("a_v")
            s_fold = semaphore("e_fold")
            s_folded = semaphore("e_folded")
            s_out = semaphore("kv_out")
            s_gain = semaphore("t_gain")
            s_bias = [semaphore(f"a_bias{n}") for n in range(2)]
            s_bmask = semaphore("a_bmask")
            s_S = [semaphore(f"a_S{n}") for n in range(2)]
            s_Sr = [semaphore(f"a_Sr{n}") for n in range(2)]
            s_nm = semaphore("a_nm")
            s_exp = semaphore("a_exp")
            s_softc = semaphore("a_softc")
            s_soft = semaphore("a_soft")
            s_w = semaphore("a_w")
            s_pA = semaphore("a_pA")
            s_pB = semaphore("a_pB")
            s_T = semaphore("t_full")
            s_Tc = semaphore("t_taken")
            s_PV = semaphore("a_PV")
            s_Oc = semaphore("a_Oc")
            s_oin = semaphore("m_oin")
            s_adve = semaphore("a_dve")
            s_gin = semaphore("m_gin")
            s_xin = semaphore("m_xin")
            s_wr = [semaphore(f"m_wr{n}") for n in range(4)]
            s_wu = semaphore("m_wu")
            s_sig = semaphore("m_sig")
            s_ssh = semaphore("m_ssh")
            s_rmsh = semaphore("m_rmsh")
            s_mdve = semaphore("m_dve")
            s_On = semaphore("m_On")
            s_m = semaphore("m_m")
            s_h = semaphore("m_h")
            s_ssx = semaphore("r_ssx")
            s_rmsx = semaphore("r_rmsx")
            s_rdve = semaphore("r_dve")
            s_xn = semaphore("r_xn")
            s_qc = semaphore("r_qc")
            s_sc = semaphore("r_sc")
            s_scr = semaphore("r_scr")
            s_route = semaphore("r_route")
            s_shift = semaphore("r_shift")
            s_gexp = semaphore("r_gexp")
            s_ring = [semaphore(f"e_ring{n}") for n in range(R)]
            s_dot = semaphore("e_dot")
            s_sum = semaphore("e_sum")
            s_vsum = semaphore("e_vsum")
            s_idxv = semaphore("e_idxv")
            s_gelu = semaphore("e_gelu")
            s_wgt = semaphore("e_wgt")
            s_diag = semaphore("e_diag")
            s_res = semaphore("e_res")
            s_yc = semaphore("f_yc")
            s_ssy = semaphore("f_ssy")
            s_rmsy = semaphore("f_rmsy")
            s_fdve = semaphore("f_dve")
            s_y_out = semaphore("f_y")
            s_yst = semaphore("f_yst")
            turn = {n: semaphore(f"turn_{n}") for n in ("sync", "pool", "act", "dve")}

            room_k = keyT[:].rearrange("p u k -> p (u k)")
            room_v = val[:].rearrange("p t c -> p (t c)")
            taken_cols = {}

            def part(room, name, shape):
                cols = int(np.prod(shape[1:]))
                first = taken_cols.get(name, 0)
                taken_cols[name] = first + cols
                assert taken_cols[name] <= KD * SEQ
                flat = room[0:shape[0], first:first + cols]
                if len(shape) == 3:
                    return flat.rearrange("p (a b) -> p a b", b=shape[2])
                if len(shape) == 4:
                    return flat.rearrange("p (a b c) -> p a b c", b=shape[2], c=shape[3])
                return flat

            kpage = part(room_k, "k", (P, PAGES, D))
            vpage = part(room_k, "k", (P, 2, PAGES, D))
            qk = part(room_k, "k", (NS, 2, D))
            oa, ob = qk[0:HA * TD, 0, 0:CH], qk[0:HB * TD, 0, CH:D]
            vnew = part(room_v, "v", (TD, 2, D))
            kT = part(room_v, "v", (P, KD, KS))
            qblk = part(room_v, "v", (P, KD, P + TK))
            qblk_flat = qblk.rearrange("p u c -> p (u c)")
            qT = part(room_v, "v", (P, KD, NS))
            knT = part(room_v, "v", (P, KD, NS))
            dec_mask = part(room_v, "v", (P, KS))
            dec_scores = part(room_v, "v", (P, KS))
            dec_exp = part(room_v, "v", (P, KS))
            dec_prob = part(room_v, "v", (P, KS))
            pT = part(room_v, "v", (P, 3, P))
            pd = part(room_v, "v", (P, 3, HA * TD))
            dec_mx, dec_nm, dec_l, dec_rl = mx[:, 0:1], nm[:, 0:1], l[:, 0:1], rl[:, 0, 0:1]
            pages = sb("t_pages", [1, NB_DEC * PAGES], I32)
            d_qk = semaphore("d_qk")
            d_pt = semaphore("d_pt")
            d_mask = semaphore("d_mask")
            d_page = semaphore("d_page")
            d_val = [semaphore(f"d_val{n}") for n in range(2)]
            d_zero = semaphore("d_zero")
            d_qT = semaphore("d_qT")
            d_qTc = semaphore("d_qTc")
            d_blk = semaphore("d_blk")
            d_kT = semaphore("d_kT")
            d_kTc = semaphore("d_kTc")
            d_S = semaphore("d_S")
            d_Sr = semaphore("d_Sr")
            d_act = semaphore("d_act")
            d_dve = semaphore("d_dve")
            d_prob = semaphore("d_prob")
            d_T = semaphore("d_T")
            d_Tc = semaphore("d_Tc")
            d_new = semaphore("d_new")
            d_pd = semaphore("d_pd")
            d_O = semaphore("d_O")
            d_Oc = semaphore("d_Oc")
            d_store = semaphore("d_store")
            A, B = slice(0, HA * 2 * TD), slice(HA * 2 * TD, P)
            KC = (P, P, TD)
            pools = [a[n][0].rearrange("n p h e -> n p (h e)") for n in
                     ("cache_k_diff", "cache_k_sb", "cache_v_diff", "cache_v_sb")]
            last_page = pools[0].shape[0] - 1


            NTB = 34
            NW = 24

            class Steps:

                def __init__(self, sem, per):
                    self.sem, self.per, self.k, self.t = sem, per, 0, 0

                def begin(self, t):
                    self.t, self.k = t, 0

                def raised_by(self, instruction):
                    instruction.then_inc(self.sem, 1)
                    self.k += 1

                @property
                def value(self):
                    return self.t * self.per + self.k

            def tile(t):
                return slice(t * P, t * P + P) if isinstance(t, int) else ds(t * P, P)

            def is_sample(t):
                return isinstance(t, int) and t == NPT

            def rows_of(t):
                return P

            def out_rows(t):
                return NS if is_sample(t) else P

            def slots_of(t):
                return NSLOT // 2 if is_sample(t) else NSLOT

            HALVES = ((0, slice(0, NS)), (1, slice(NS, P)))

            def window(row, t, kw):
                first = SLABW - SEQ - t * P
                return slab_d[row, :, first:first + kw] if isinstance(t, int) else slab_d[row, :, ds(first, kw)]

            def sync_attend(sp, t, kw):
                rows = tile(t)
                if not (isinstance(t, int) and t == 0):
                    sp.wait_ge(s_T, (t - 1) * NTB + (28))
                    sp.sem_inc(turn["sync"], 1)
                for n, col in enumerate((QA, QB)):
                    sp.dma_start(o_sb[:, n * CH:(n + 1) * CH], proj_d[rows, col:col + CH]).then_inc(s_qin, 16)
                wins = [window(u, t, kw) for u in range(HA + 1)]
                sp.wait_ge(s_route, t)
                sp.sem_inc(turn["sync"], 1)
                for u in range(HA):
                    if u >= 2:
                        sp.wait_ge(s_Sr[1], t * 8 + u - 1)
                        sp.sem_inc(turn["sync"], 1)
                    sp.dma_start(bias[:, u % 2, 0:kw], wins[u]).then_inc(s_bias[u % 2], 16)
                    if u == 1:
                        sp.dma_start(bmask[:, 0:kw], wins[HA]).then_inc(s_bmask, 16)
                        if isinstance(t, int) and t == 0:
                            for n, col in enumerate((VA, VB)):
                                sp.dma_start(val[:, :, n * CH:(n + 1) * CH],
                                             proj_d[0:SEQ, col:col + CH].rearrange("(t p) c -> p t c", p=P)).then_inc(s_v, 16)
                            sp.dma_start(gain_ffn[:], a["norm_ffn"][0:1, :].broadcast_to([P, D])).then_inc(s_gain, 16)
                            sp.dma_start(gain_fin[:], a["norm_final"].rearrange("(o d) -> o d", o=1).broadcast_to([P, D])).then_inc(s_gain, 16)

            def sync_merge(sp, t):
                if not is_sample(t):
                    x_src, g_src = x_all[0][tile(t), :], proj_d[tile(t), GA:W_IN]
                    sp.wait_ge(s_S[1], t * 8 + 8)
                    sp.sem_inc(turn["sync"], 1)
                    sp.dma_start(gates[:], g_src).then_inc(s_gin, 16)
                    sp.wait_ge(s_Sr[1], t * 8 + 3)
                    sp.sem_inc(turn["sync"], 1)
                    sp.dma_start(x_sb, x_src).then_inc(s_xin, 16)
                    sp.wait_ge(s_pB, t * 8 + 8)
                    sp.sem_inc(turn["sync"], 1)
                else:
                    sp.wait_ge(s_T, (t - 1) * NTB + 28)
                    sp.sem_inc(turn["sync"], 1)
                    for _half, to in HALVES:
                        sp.dma_start(o_sb[to, :], attn_d[:, :]).then_inc(s_oin, 16)
                    sp.wait_ge(s_route, t)
                    sp.sem_inc(turn["sync"], 1)
                    for _half, to in HALVES:
                        sp.dma_start(gates[to, :], proj_d[SEQ:T, GA:W_IN]).then_inc(s_gin, 16)
                        sp.dma_start(x_sb[to, :], x_all[1]).then_inc(s_xin, 16)
                for n in range(NW):
                    for name, first, last in (("w_proj_diff", 0, 4), ("w_proj_sb", 4, 8), ("w_out", 8, 16),
                                              ("peer_w_query", 16, 24)):
                        if first <= n < last:
                            src = a[name][0][(n - first) * P:(n - first + 1) * P, :]
                    if n >= 4:
                        sp.wait_ge(s_wu, t * NW + n - 3)
                        sp.sem_inc(turn["sync"], 1)
                    sp.dma_start(wring[:, n % 4, :], src).then_inc(s_wr[n % 4], 16)

            def sync_finish(sp, e):
                dst = y_out[1] if is_sample(e) else y_out[0][tile(e), :]
                sp.wait_ge(s_y_out, e + 1)
                sp.sem_inc(turn["sync"], 1)
                sp.dma_start(dst, y_sb[0:out_rows(e), :]).then_inc(s_yst, 16)

            def gather(pool, e, table, idx, phase):
                n = rows_of(e)
                for s in range(slots_of(e)):
                    if phase == 0:
                        free = summed(e, s, -1) if s < R else (s_dot, e * NSLOT + s - R + 1)
                    else:
                        free = (s_dot, e * NSLOT + slots_of(e) - R + s + 1) if s < R else summed(e, s, -1)
                    pool.wait_ge(*free)
                    pool.sem_inc(turn["pool"], 1)
                    pool.indirect_dma_start(ring[0:n, s % R, :], None, table,
                                            bass.IndirectOffsetOnAxis(ap=idx[0:n, s:s + 1], axis=0)).then_inc(s_ring[s % R], 16)

            def summed(e, s, rounds=0):
                mine, sem = (VSUM, s_vsum) if s % R in VSUM else (TSUM, s_sum)
                return sem, (e * (NSLOT // R) + s // R + 1 + rounds) * len(mine) + mine.index(s % R) + 1

            def arrived(e, phase, s):
                return s_ring[s % R], (e * (2 * NSLOT // R) + phase * (slots_of(e) // R) + s // R + 1) * 16

            def pool_experts(pool, e):
                pool.wait_ge(s_route, e + 1)
                pool.sem_inc(turn["pool"], 1)
                gather(pool, e, a["peer_u"][0], idx_u, 0)
                pool.wait_ge(s_idxv, e + 1)
                pool.sem_inc(turn["pool"], 1)
                gather(pool, e, a["peer_v"][0], idx_v, 1)

            pe_T = Steps(s_T, NTB)

            def pe_transposes(pe, blocks, n):
                pe.wait_ge(s_Tc, pe_T.value)
                for k, blk in enumerate(blocks):
                    m = nc.tensor.transpose(ps[:, 6, k * P:k * P + n], blk, ident[0:n, 0:n])
                pe_T.raised_by(m)

            def pe_scores(pe, t, u, kw):
                for hf in range(2):
                    pe.wait_ge(s_Sr[hf], t * 8 + u)
                    for c in range(0, kw, CH):
                        wide = min(CH, kw - c)
                        m = nc.tensor.matmul(ps[:, 2 + 2 * hf + c // CH, 0:wide], qz[:, u, hf, :], keyT[:, u, c:c + wide],
                                             start=True, stop=True)
                    m.then_inc(s_S[hf], 1)

            def pe_attend(pe, t, kw):
                nb = kw // P // 2
                pe_T.begin(t)
                pe.wait_ge(s_qin, t * 32 + 32)
                for g in range(2):
                    pe_transposes(pe, [o_sb[:, u * P:(u + 1) * P] for u in range(4 * g, 4 * g + 4)], P)
                pe.wait_ge(s_Tc, pe_T.value)
                pe.wait_ge(s_scr, t)
                pe_scores(pe, t, 0, kw)
                for u in range(8):
                    if u < 7:
                        pe_scores(pe, t, u + 1, kw)
                    if u % 4 == 0:
                        pe.wait_ge(s_Oc, t * 2 + u // 4)
                    for hf in range(1 if u < HA else 2):
                        n = u if u < HA else 4 + 2 * (u - HA) + hf
                        pe.wait_ge(*((s_pA, t * 4 + u + 1) if u < HA else (s_pB, t * 8 + n - 3)))
                        for j in range(2):
                            pe_transposes(pe, [prob[:, n % 2, (j * nb + k) * P:(j * nb + k + 1) * P] for k in range(nb)], P)
                        pe.wait_ge(s_Tc, pe_T.value)
                        if isinstance(t, int) and t == 0:
                            pe.wait_ge(s_v, 32)
                        wide = P if u < HA else 64
                        col = (u % 4) * P + hf * 64
                        for kb in range(2 * nb):
                            m = nc.tensor.matmul(ps[:, 7, col:col + wide], pTr[:, kb, :],
                                                 val[:, kb, u * P + hf * 64:u * P + hf * 64 + wide],
                                                 start=(kb == 0), stop=(kb == 2 * nb - 1))
                        m.then_inc(s_PV, 1)

            def pe_product(pe, t, n, bank, first, blocks, k0, k1):
                for k in range(k0, k1):
                    w = first + k - blocks[0]
                    pe.wait_ge(s_wr[w % 4], t * (16 * NW // 4) + 16 * (w // 4) + 16)
                    for c in range(2):
                        m = nc.tensor.matmul(ps[0:n, bank + c, :], pTr[:, k, 0:n], wring[:, w % 4, c * CH:(c + 1) * CH],
                                             start=(k == blocks[0]), stop=(k == blocks[1] - 1))
                    m.then_inc(s_wu, 1)

            def pe_merge(pe, t, piece):
                n = rows_of(t)

                def turn_rows(src):
                    for g in range(2):
                        pe_transposes(pe, [src[0:n, k * P:(k + 1) * P] for k in range(4 * g, 4 * g + 4)], n)

                if piece == "turn_o":
                    if is_sample(t):
                        pe_T.begin(t)
                    pe.wait_ge(s_On, t + 1)
                    turn_rows(o_sb)
                elif piece == "branch_a":
                    pe.wait_ge(s_Tc, pe_T.value)
                    pe_product(pe, t, n, 2, 0, (0, 4), 0, 4)
                elif piece == "branch_b":
                    pe_product(pe, t, n, 4, 4, (4, 8), 4, 8)
                elif piece == "turn_m":
                    pe.wait_ge(s_m, t + 1)
                    turn_rows(mixed)
                elif piece == "out_1":
                    pe.wait_ge(s_Tc, pe_T.value)
                    pe_product(pe, t, n, 2, 8, (0, 8), 0, 4)
                elif piece == "out_2":
                    pe_product(pe, t, n, 2, 8, (0, 8), 4, 8)
                elif piece == "turn_x":
                    pe.wait_ge(s_xn, t + 1)
                    turn_rows(xn_sb)
                elif piece == "query_1":
                    pe.wait_ge(s_Tc, pe_T.value)
                    pe_product(pe, t, n, 4, 16, (0, 8), 0, 4)
                elif piece == "query_2":
                    pe_product(pe, t, n, 4, 16, (0, 8), 4, 8)
                elif piece == "turn_q":
                    pe.wait_ge(s_qc, t + 1)
                    turn_rows(q_sb)
                elif piece == "score":
                    pe.wait_ge(s_Tc, pe_T.value)
                    for h in range(PH):
                        m = nc.tensor.matmul(ps[0:n, 2 + h // 2, (h % 2) * 2 * P:(h % 2 + 1) * 2 * P], pTr[:, h, 0:n],
                                             subkT[:, h, :], start=True, stop=True)
                    m.then_inc(s_sc, 1)

            def turn_of(e, s):
                return e * (NSLOT // R * len(TSUM)) + s // R * len(TSUM) + TSUM.index(s % R)

            def pe_experts(pe, e, k):
                n = out_rows(e)
                if k == 0:
                    pe.wait_ge(s_yc, e + 1)
                    pe.wait_ge(s_h, e + 1)
                    for c in range(2):
                        m = nc.tensor.matmul(ps[0:n, c, :], ident[:, 0:n], h_sb[:, c * CH:(c + 1) * CH], start=True, stop=False)
                    m.then_inc(s_res, 1)
                for s in range(4 * k, min(4 * k + 4, slots_of(e))):
                    if s % R in TSUM:
                        pe.wait_ge(*arrived(e, 1, s))
                        pe.wait_ge(s_diag, turn_of(e, s) + 1)
                        for c in range(2):
                            m = nc.tensor.matmul(ps[0:n, c, :], diag[:, turn_of(0, s) % NDG, 0:n], ring[:, s % R, c * CH:(c + 1) * CH],
                                                 start=False, stop=(s == NSLOT - R + TSUM[-1]))
                        m.then_inc(s_sum, 1)
                if is_sample(e) and 4 * k + 4 == slots_of(e):
                    pe.wait_ge(*summed(e, slots_of(e) - R + VSUM[-1]))
                    for c in range(2):
                        m = nc.tensor.matmul(ps[0:n, c, :], fold[:], y_sb[:, c * CH:(c + 1) * CH], start=False, stop=True)
                    m.then_inc(s_folded, 1)

            act_T = Steps(s_Tc, NTB)

            def act_take(act, dst, n):
                act.wait_ge(s_T, act_T.value + 1)
                src = ps[:, 6, 0:dst.shape[1] * P].rearrange("p (k r) -> p k r", r=P)[:, :, 0:n]
                act_T.raised_by(nc.scalar.copy(dst[:, :, 0:n], src))

            def act_attend(act, t, kw):
                nb = kw // P // 2
                act_T.begin(t)
                act.wait_ge(s_route, t)
                act.sem_inc(turn["act"], 1)
                for g in range(2):
                    act.wait_ge(s_T, act_T.value + 1)
                    src = ps[:, 6, :].rearrange("p (u r) -> p u r", r=P)
                    nc.scalar.activation(qz[:, 4 * g:4 * g + 4, 0, :], src, ACT.Copy, scale=half_scale[:, 0:1])
                    act_T.raised_by(nc.scalar.activation(qz[:, 4 * g:4 * g + 4, 1, :], src, ACT.Copy, scale=half_scale[:, 1:2]))
                for u in range(8):
                    if u < HA:
                        for hf in range(2):
                            act.wait_ge(s_nm, t * 8 + 2 * u + hf + 1)
                            nc.scalar.activation(z[:, hf, 0:kw], z[:, hf, 0:kw], ACT.Exp, bias=nm[:, hf:hf + 1],
                                                 accum_out=l[:, hf:hf + 1]).then_inc(s_exp, 1)
                        for j in range(2):
                            act_take(act, pTr[:, j * nb:(j + 1) * nb, :], P)
                    else:
                        v = 4 * (u - HA)
                        for hf in range(2):
                            act.wait_ge(s_Sr[hf], t * 8 + u + 1)
                            nc.scalar.activation(soft[:, hf, 0:kw], z[:, hf, 0:kw], ACT.Abs).then_inc(s_softc, 1)
                        for hf in range(2):
                            act.wait_ge(s_softc, t * 16 + v + hf + 1)
                            nc.scalar.activation(soft[:, hf, 0:kw], soft[:, hf, 0:kw], ACT.Exp, scale=-1.0).then_inc(s_softc, 1)
                        for hf in range(2):
                            act.wait_ge(s_softc, t * 16 + v + hf + 3)
                            nc.scalar.activation(soft[:, hf, 0:kw], soft[:, hf, 0:kw], ACT.Ln, bias=one_t[:]).then_inc(s_soft, 1)
                        for hf in range(2):
                            act.wait_ge(s_w, t * 8 + 2 * (u - HA) + hf + 1)
                            nc.scalar.activation(prob[:, hf, 0:kw], z[:, hf, 0:kw], ACT.Exp).then_inc(s_pB, 1)
                        for j in range(4):
                            act_take(act, pTr[:, (j % 2) * nb:(j % 2 + 1) * nb, :], P)
                    if u % 4 == 3:
                        act.wait_ge(s_PV, t * 12 + (4 if u == 3 else 12))
                        if u < HA:
                            for h in range(HA):
                                m = nc.scalar.activation(o_sb[:, h * P:(h + 1) * P], ps[:, 7, h * P:(h + 1) * P], ACT.Copy,
                                                         scale=rl[:, h, 0:1])
                        else:
                            m = nc.scalar.copy(o_sb[:, CH:D], ps[:, 7, :])
                        m.then_inc(s_Oc, 1)

            def act_merge(act, t, piece):
                n = rows_of(t)

                def take_two():
                    for g in range(2):
                        act_take(act, pTr[:, 4 * g:4 * g + 4, :], n)

                if piece == "norm_o":
                    if is_sample(t):
                        act_T.begin(t)
                    act.wait_ge(s_gin, t * 16 + (32 if is_sample(t) else 16))
                    nc.scalar.activation(gates[0:n, :], gates[0:n, :], ACT.Sigmoid).then_inc(s_sig, 1)
                    act.wait_ge(s_ssh, t + 1)
                    nc.scalar.activation(rmsh[0:n, :], ssh[0:n, :], ACT.Sqrt, bias=eps_t[0:n, :], scale=1.0 / P).then_inc(s_rmsh, 1)
                elif piece in ("turn_o", "turn_m", "turn_x", "turn_q"):
                    take_two()
                elif piece == "residual":
                    act.wait_ge(s_ssx, t + 1)
                    nc.scalar.activation(rmsx[0:n, :], ssx[0:n, :], ACT.Sqrt, bias=eps_t[0:n, :], scale=1.0 / D).then_inc(s_rmsx, 1)
                elif piece == "query_2":
                    act.wait_ge(s_wu, t * NW + 24)
                    nc.scalar.copy(q_sb[0:n, :], both(4)[0:n, :]).then_inc(s_qc, 1)
                elif piece == "gate":
                    act.wait_ge(s_shift, t + 1)
                    nc.scalar.activation(gexp[0:n], gexp[0:n], ACT.Exp).then_inc(s_gexp, 1)

            def act_gelu(act, e):
                cols = slice(0, slots_of(e))
                act.wait_ge(s_dot, e * NSLOT + slots_of(e))
                nc.scalar.activation(act_u[:, cols], dots[:, cols], ACT.Gelu).then_inc(s_gelu, 1)

            def act_experts(act, e, k):
                if k == 0:
                    act.wait_ge(s_wgt, e + 1)
                    act.sem_inc(turn["act"], 1)
                    if is_sample(e):
                        act.wait_ge(s_fold, 1)
                unit = fold if is_sample(e) else ident
                for s in range(4 * k, min(4 * k + 4, slots_of(e))):
                    if s % R in TSUM:
                        act.wait_ge(s_sum, turn_of(e, s) + 1 - NDG + len(TSUM))
                        nc.scalar.activation(diag[:, turn_of(0, s) % NDG, 0:out_rows(e)], unit[:], ACT.Copy,
                                             scale=wgt[:, s:s + 1]).then_inc(s_diag, 1)

            def act_finish(act, e):
                n = out_rows(e)
                act.wait_ge(s_ssy, e + 1)
                nc.scalar.activation(rmsy[0:n, :], ssy[0:n, :], ACT.Sqrt, bias=eps_t[0:n, :], scale=1.0 / D).then_inc(s_rmsy, 1)

            lk = {"a": Steps(s_adve, 4 * 2 + 4 * 4), "m": Steps(s_mdve, 3), "r": Steps(s_rdve, 21), "f": Steps(s_fdve, 1)}

            def chain(name, instruction):
                lk[name].raised_by(instruction)

            def linked(dve, name):
                dve.wait_ge(lk[name].sem, lk[name].value)
                dve.sem_inc(turn["dve"], 1)

            def dve_attend(dve, t, u, part, kw):
                if u == 0 and part == 0:
                    lk["a"].begin(t)
                    dve.wait_ge(s_wu, t * NW)
                if part == 0:
                    if u < HA:
                        dve.wait_ge(s_bias[u % 2], t * 32 + 16 * (u // 2) + 16)
                    elif u == HA:
                        dve.wait_ge(s_bmask, t * 16 + 16)
                    if u <= HA:
                        dve.wait_ge(s_pA, t * 4 + u)
                        dve.sem_inc(turn["dve"], 1)
                    for hf in range(2):
                        if u == 0 or u > HA:
                            dve.wait_ge(s_pB, t * 8 + (0 if u == 0 else 2 * (u - HA) - 1 + hf))
                            dve.sem_inc(turn["dve"], 1)
                        dve.wait_ge(s_S[hf], t * 8 + u + 1)
                        dve.sem_inc(turn["dve"], 1)
                        src = both(2 + 2 * hf)[:, 0:kw]
                        if u < HA:
                            nc.vector.tensor_tensor_reduce(out=z[:, hf, 0:kw], in0=src, in1=bias[:, u % 2, 0:kw], scale=1.0,
                                                           scalar=LOWEST, op0=ALU.add, op1=ALU.max,
                                                           accum_out=mx[:, hf:hf + 1]).then_inc(s_Sr[hf], 1)
                        else:
                            nc.vector.tensor_tensor(z[:, hf, 0:kw], src, bmask[:, 0:kw], ALU.add).then_inc(s_Sr[hf], 1)
                    if u < HA:
                        for hf in range(2):
                            dve.wait_ge(s_Sr[hf], t * 8 + u + 1)
                            nc.vector.tensor_scalar_mul(nm[:, hf:hf + 1], mx[:, hf:hf + 1], -1.0).then_inc(s_nm, 1)
                elif u < HA:
                    dve.wait_ge(s_exp, t * 8 + 2 * u + 2)
                    chain("a", nc.vector.reciprocal(rl[:, u, :], l[:]))
                    linked(dve, "a")
                    chain("a", nc.vector.scalar_tensor_tensor(out=rl2[:], in0=rl[:, u, 1:2], scalar=neg_lam[:], in1=l[:, 0:1],
                                                              op0=ALU.mult, op1=ALU.mult))
                    dve.wait_ge(s_T, t * NTB + 2 * u)
                    dve.sem_inc(turn["dve"], 1)
                    linked(dve, "a")
                    nc.vector.scalar_tensor_tensor(out=prob[:, u % 2, 0:kw], in0=z[:, 1, 0:kw], scalar=rl2[:],
                                                   in1=z[:, 0, 0:kw], op0=ALU.mult, op1=ALU.add).then_inc(s_pA, 1)
                else:
                    for hf in range(2):
                        dve.wait_ge(s_soft, t * 8 + 2 * (u - HA) + hf + 1)
                        chain("a", nc.vector.scalar_tensor_tensor(out=soft[:, hf, 0:kw], in0=z[:, hf, 0:kw], scalar=0.0,
                                                                  in1=soft[:, hf, 0:kw], op0=ALU.max, op1=ALU.add))
                    for hf in range(2):
                        dve.wait_ge(s_T, t * NTB + 2 * (4 + 2 * (u - HA) + hf))
                        dve.sem_inc(turn["dve"], 1)
                        dve.wait_ge(s_adve, lk["a"].value - 1)
                        m = nc.vector.tensor_tensor_scan(out=prob[:, hf, kw - 1::-1],
                                                         data0=soft[:, hf, kw - 1::-1], data1=soft[:, hf, kw - 1::-1],
                                                         initial=0.0, op0=ALU.add, op1=ALU.bypass)
                        chain("a", m)
                    for hf in range(2):
                        dve.wait_ge(s_adve, lk["a"].value - 1 + hf)
                        nc.vector.tensor_tensor(z[:, hf, 0:kw], z[:, hf, 0:kw], prob[:, hf, 0:kw], ALU.subtract).then_inc(s_w, 1)

            def dve_merge(dve, t, piece):
                n = rows_of(t)
                if piece == "norm_o":
                    lk["m"].begin(t)
                    lk["r"].begin(t)
                    if is_sample(t):
                        dve.wait_ge(s_oin, 32)
                    else:
                        dve.wait_ge(s_Oc, t * 2 + 2)
                    for h in range(HA):
                        cols = slice(h * P, (h + 1) * P)
                        m = nc.vector.tensor_tensor_reduce(out=sq[0:n, cols], in0=o_sb[0:n, cols], in1=o_sb[0:n, cols],
                                                           scale=1.0, scalar=0.0, op0=ALU.mult, op1=ALU.add,
                                                           accum_out=ssh[0:n, h:h + 1])
                    m.then_inc(s_ssh, 1)
                elif piece == "scale_o":
                    dve.wait_ge(s_rmsh, t + 1)
                    chain("m", nc.vector.reciprocal(rsh[0:n, :], rmsh[0:n, :]))
                    linked(dve, "m")
                    for h in range(HA):
                        cols = slice(h * P, (h + 1) * P)
                        m = nc.vector.scalar_tensor_tensor(out=o_sb[0:n, cols], in0=o_sb[0:n, cols], scalar=rsh[0:n, h:h + 1],
                                                           in1=gain_sub[0:n, :], op0=ALU.mult, op1=ALU.mult)
                    m.then_inc(s_On, 1)
                elif piece == "mix":
                    dve.wait_ge(s_sig, t + 1)
                    dve.sem_inc(turn["dve"], 1)
                    dve.wait_ge(s_wu, t * NW + 8)
                    chain("m", nc.vector.tensor_tensor(mixed[0:n, :], both(2)[0:n, :], gates[0:n, 0:D], ALU.mult))
                    chain("m", nc.vector.tensor_tensor(gates[0:n, D:2 * D], both(4)[0:n, :], gates[0:n, D:2 * D], ALU.mult))
                    linked(dve, "m")
                    nc.vector.tensor_tensor(mixed[0:n, :], mixed[0:n, :], gates[0:n, D:2 * D], ALU.add).then_inc(s_m, 1)
                elif piece == "residual":
                    dve.wait_ge(s_wu, t * NW + 16)
                    dve.sem_inc(turn["dve"], 1)
                    dve.wait_ge(s_res, t)
                    dve.sem_inc(turn["dve"], 1)
                    dve.wait_ge(s_xin, t * 16 + (32 if is_sample(t) else 16))
                    nc.vector.tensor_tensor(h_sb[0:n, :], both(2)[0:n, :], x_sb[0:n, :], ALU.add).then_inc(s_h, 1)
                    dve.wait_ge(s_h, t + 1)
                    nc.vector.tensor_tensor_reduce(out=sq[0:n, :], in0=h_sb[0:n, :], in1=h_sb[0:n, :], scale=1.0, scalar=0.0,
                                                   op0=ALU.mult, op1=ALU.add, accum_out=ssx[0:n, :]).then_inc(s_ssx, 1)
                elif piece == "norm_x":
                    dve.wait_ge(s_rmsx, t + 1)
                    chain("r", nc.vector.reciprocal(rsx[0:n, :], rmsx[0:n, :]))
                    linked(dve, "r")
                    if isinstance(t, int) and t == 0:
                        dve.wait_ge(s_gain, 32)
                    nc.vector.scalar_tensor_tensor(out=xn_sb[0:n, :], in0=h_sb[0:n, :], scalar=rsx[0:n, :],
                                                   in1=gain_ffn[0:n, :], op0=ALU.mult, op1=ALU.mult).then_inc(s_xn, 1)
                sc = [ps[0:n, 2 + i // 4, (i % 4) * P:(i % 4 + 1) * P] for i in range(2 * PH)]
                lf = [left[0:n, i * P:(i + 1) * P] for i in range(2 * PH)]
                cd = [cand[0:n, i * 2 * P:(i + 1) * 2 * P] for i in range(PH)]
                lc = [left[0:n, i * 2 * P:(i + 1) * 2 * P] for i in range(PH)]
                if piece == "key_1":
                    dve.wait_ge(s_sc, t + 1)
                    dve.sem_inc(turn["dve"], 1)
                    for i in range(2 * PH):
                        m = nc.vector.max(top[0:n, i, 0:8], sc[i])
                    chain("r", m)
                elif piece == "key_2":
                    linked(dve, "r")
                    for i in range(2 * PH):
                        m = nc.vector.match_replace(lf[i], top[0:n, i, 0:8], sc[i], LOWEST)
                    chain("r", m)
                elif piece == "key_3":
                    for i in range(2 * PH):
                        m = nc.vector.max_index(topi[0:n, i, 0:8], top[0:n, i, 0:8], sc[i])
                    m.then_inc(s_scr, 1)
                elif piece == "key_4":
                    linked(dve, "r")
                    for i in range(2 * PH):
                        m = nc.vector.max(top[0:n, i, 8:16], lf[i])
                    chain("r", m)
                elif piece == "key_5":
                    linked(dve, "r")
                    for i in range(2 * PH):
                        m = nc.vector.max_index(topi[0:n, i, 8:16], top[0:n, i, 8:16], lf[i])
                    chain("r", m)
                elif piece == "pair_1":
                    linked(dve, "r")
                    chain("r", nc.vector.tensor_copy(topf[0:n], topi[0:n]))
                    halves = top[0:n].rearrange("p (h c) a -> p h c a", c=2)
                    chain("r", nc.vector.tensor_tensor(cand[0:n, :].rearrange("p (h k a) -> p h k a", h=PH, k=TK),
                                                       halves[:, :, 0, :].unsqueeze(3).broadcast_to([n, PH, TK, TK]),
                                                       halves[:, :, 1, :].unsqueeze(2).broadcast_to([n, PH, TK, TK]), ALU.add))
                elif piece == "pair_2":
                    linked(dve, "r")
                    for i in range(PH):
                        m = nc.vector.max(best[0:n, i, 0:8], cd[i])
                    chain("r", m)
                elif piece == "pair_3":
                    linked(dve, "r")
                    for i in range(PH):
                        m = nc.vector.match_replace(lc[i], best[0:n, i, 0:8], cd[i], LOWEST)
                    chain("r", m)
                elif piece == "pair_4":
                    for i in range(PH):
                        nc.vector.max_index(bestj[0:n, i * TK:i * TK + 8], best[0:n, i, 0:8], cd[i])
                elif piece == "pair_5":
                    linked(dve, "r")
                    for i in range(PH):
                        m = nc.vector.max(best[0:n, i, 8:16], lc[i])
                    chain("r", m)
                elif piece == "pair_6":
                    linked(dve, "r")
                    for i in range(PH):
                        m = nc.vector.max_index(bestj[0:n, i * TK + 8:(i + 1) * TK], best[0:n, i, 8:16], lc[i])
                    chain("r", m)
                elif piece == "gate":
                    linked(dve, "r")
                    nc.vector.tensor_tensor(gexp[0:n], best[0:n], best[0:n, :, 0:1].broadcast_to([n, PH, TK]),
                                            ALU.subtract).then_inc(s_shift, 1)
                    nc.vector.tensor_scalar(ja[0:n, 0, :], bestj[0:n, :], 4, None, ALU.logical_shift_right)
                    chain("r", nc.vector.tensor_scalar(ja[0:n, 1, :], bestj[0:n, :], 15, None, ALU.bitwise_and))
                    linked(dve, "r")
                    chain("r", nc.vector.tensor_copy(jf[0:n], ja[0:n]))
                elif piece in ("pick_1", "pick_2"):
                    c = int(piece == "pick_2")
                    linked(dve, "r")
                    hot4 = pick[0:n, :].rearrange("p (h k a) -> p h k a", h=PH, k=TK)
                    hot3 = pick[0:n, :].rearrange("p (s a) -> p s a", a=TK)
                    ids = topf[0:n].rearrange("p (h c) a -> p h c a", c=2)[:, :, c, :].unsqueeze(2).broadcast_to([n, PH, TK, TK])
                    chain("r", nc.vector.tensor_tensor(hot3, jf[0:n, c, :].unsqueeze(2).broadcast_to([n, NSLOT, TK]),
                                                       iota16[0:n, :].unsqueeze(1).broadcast_to([n, NSLOT, TK]), ALU.is_equal))
                    linked(dve, "r")
                    chain("r", nc.vector.tensor_tensor(hot4, hot4, ids, ALU.mult))
                    linked(dve, "r")
                    chain("r", nc.vector.tensor_reduce(sel[0:n, c, :], hot3, AX, ALU.add))
                elif piece == "choose":
                    linked(dve, "r")
                    if is_sample(t):
                        for half, rows in HALVES:
                            nc.vector.scalar_tensor_tensor(out=idx_u[rows, 0:NSLOT // 2], in0=sel[rows, 0, half::2], scalar=float(P),
                                                           in1=sel[rows, 1, half::2], op0=ALU.mult, op1=ALU.add)
                    else:
                        nc.vector.scalar_tensor_tensor(out=idx_u[:], in0=sel[:, 0, :], scalar=float(P), in1=sel[:, 1, :],
                                                       op0=ALU.mult, op1=ALU.add)
                    dve.wait_ge(s_gexp, t + 1)
                    chain("r", nc.vector.tensor_reduce(gsum[0:n, :], gexp[0:n], AX, ALU.add))
                    linked(dve, "r")
                    chain("r", nc.vector.reciprocal(grec[0:n, :], gsum[0:n, :]))
                    linked(dve, "r")
                    if is_sample(t):
                        for half, rows in HALVES:
                            m = nc.vector.tensor_tensor(gate_flat[rows, 0:NSLOT // 2].rearrange("p (h k) -> p h k", h=PH),
                                                        gexp[rows, :, half::2],
                                                        grec[rows, :].unsqueeze(2).broadcast_to([NS, PH, TK // 2]), ALU.mult)
                    else:
                        m = nc.vector.tensor_tensor(gate[:], gexp[:], grec[:].unsqueeze(2).broadcast_to([P, PH, TK]), ALU.mult)
                    m.then_inc(s_route, 1)

            def dve_dots(dve, e, first, last):
                n = rows_of(e)
                for s in range(first, last):
                    dve.wait_ge(*arrived(e, 0, s))
                    nc.vector.tensor_tensor_reduce(out=ring[0:n, s % R, :], in0=ring[0:n, s % R, :], in1=xn_sb[0:n, :],
                                                   scale=1.0, scalar=0.0, op0=ALU.mult, op1=ALU.add,
                                                   accum_out=dots[0:n, s:s + 1]).then_inc(s_dot, 1)

            def dve_keep_idx(dve, e):
                dve.wait_ge(*summed(e, NSLOT - 1, -(NSLOT // R)))
                dve.wait_ge(*summed(e, NSLOT - 2, -(NSLOT // R)))
                cols = slice(0, slots_of(e))
                nc.vector.tensor_copy(idx_v[:, cols], idx_u[:, cols]).then_inc(s_idxv, 1)

            def dve_weights(dve, e):
                cols = slice(0, slots_of(e))
                dve.wait_ge(s_gelu, e + 1)
                nc.vector.tensor_tensor(wgt[:, cols], act_u[:, cols], gate_flat[:, cols], ALU.mult).then_inc(s_wgt, 1)

            def dve_experts(dve, e, k):
                n = rows_of(e)
                if k == 0:
                    dve.wait_ge(s_wgt, e + 1)
                    dve.wait_ge(s_yst, e * 16 + 16)
                for s in range(4 * k, min(4 * k + 4, slots_of(e))):
                    if s % R in VSUM:
                        row, w = ring[0:n, s % R, :], wgt[0:n, s:s + 1]
                        dve.wait_ge(*arrived(e, 1, s))
                        if s == VSUM[0]:
                            m = nc.vector.tensor_scalar_mul(y_sb[0:n, :], row, w)
                        else:
                            before_this = s_vsum, summed(e, s)[1] - 1
                            dve.wait_ge(*before_this)
                            m = nc.vector.scalar_tensor_tensor(out=y_sb[0:n, :], in0=row, scalar=w, in1=y_sb[0:n, :],
                                                               op0=ALU.mult, op1=ALU.add)
                        m.then_inc(s_vsum, 1)

            def dve_finish(dve, e, part):
                n = out_rows(e)
                if part == 0:
                    lk["f"].begin(e)
                    if is_sample(e):
                        dve.wait_ge(s_folded, 1)
                        nc.vector.tensor_copy(y_sb[0:n, :], both(0)[0:n, :]).then_inc(s_yc, 1)
                    else:
                        dve.wait_ge(*summed(e, NSLOT - R + TSUM[-1]))
                        dve.sem_inc(turn["dve"], 1)
                        dve.wait_ge(*summed(e, NSLOT - R + VSUM[-1]))
                        nc.vector.tensor_tensor(y_sb[0:n, :], both(0)[0:n, :], y_sb[0:n, :], ALU.add).then_inc(s_yc, 1)
                    dve.wait_ge(s_yc, e + 2)
                    nc.vector.tensor_tensor_reduce(out=ysq[0:n, :], in0=y_sb[0:n, :], in1=y_sb[0:n, :], scale=1.0, scalar=0.0,
                                                   op0=ALU.mult, op1=ALU.add, accum_out=ssy[0:n, :]).then_inc(s_ssy, 1)
                else:
                    dve.wait_ge(s_rmsy, e + 1)
                    chain("f", nc.vector.reciprocal(rsy[0:n, :], rmsy[0:n, :]))
                    linked(dve, "f")
                    nc.vector.scalar_tensor_tensor(out=y_sb[0:n, :], in0=y_sb[0:n, :], scalar=rsy[0:n, :], in1=gain_fin[0:n, :],
                                                   op0=ALU.mult, op1=ALU.mult).then_inc(s_y_out, 1)


            def sync_sample(sp):
                sp.dma_start(pages[:], a["page_table"].rearrange("(o b) g -> o (b g)", o=1)).then_inc(d_pt, 16)
                sp.wait_ge(s_Oc, NPT * 2)
                for n, (c0, c1) in enumerate(((QA, QB), (KA, KB))):
                    sp.dma_start(qk[:, n, 0:CH], proj_d[SEQ:T, c0:c0 + CH]).then_inc(d_qk, 16)
                    sp.dma_start(qk[:, n, CH:D], proj_d[SEQ:T, c1:c1 + CH]).then_inc(d_qk, 16)
                sp.wait_ge(d_pt, 16)

                def load(b, which, done):
                    for g in range(PAGES):
                        page = sp.value_load(pages[0:1, b * PAGES + g:b * PAGES + g + 1], min_val=0, max_val=last_page)
                        for n in range(2):
                            dst = kpage[:, g, :] if which == 0 else vpage[:, b % 2, g, :]
                            sp.dma_start(dst[:, n * CH:(n + 1) * CH],
                                         pools[2 * which + n][ds(page, 1)].rearrange("o p c -> (o p) c")).then_inc(done, 16)

                def load_keys(b):
                    if b:
                        sp.wait_ge(d_kT, 4 * b)
                    load(b, 0, d_page)

                def load_values(b):
                    if b >= 2:
                        sp.wait_ge(d_O, b - 1)
                    load(b, 1, d_val[b % 2])
                    for n, col in enumerate((VA, VB)):
                        sp.dma_start(vnew[:, b % 2, n * CH:(n + 1) * CH],
                                     proj_d[SEQ + b * TD:SEQ + (b + 1) * TD, col:col + CH]).then_inc(d_val[b % 2], 16)

                load_keys(0)
                for m in range(2 * HA + HB):
                    row = min(m // 2, HA)
                    sp.dma_start(dec_mask[m * TD:(m + 1) * TD, :],
                                 slab_d[row, 0:TD, SLABW - SEQ - PAST:SLABW - SEQ - PAST + KS]).then_inc(d_mask, 16)
                load_values(0)
                load_keys(1)
                load_values(1)
                for b in range(NB_DEC):
                    if b + 2 < NB_DEC:
                        load_keys(b + 2)
                    sp.wait_ge(d_Oc, 2 * b + 2)
                    rows = slice(b * TD, (b + 1) * TD)
                    for h in range(HA):
                        sp.dma_start(attn_d[rows, h * P:(h + 1) * P],
                                     oa[h * TD:(h + 1) * TD, h * P:(h + 1) * P]).then_inc(d_store, 16)
                    for h in range(HB):
                        sp.dma_start(attn_d[rows, CH + h * 64:CH + (h + 1) * 64],
                                     ob[h * TD:(h + 1) * TD, h * 64:(h + 1) * 64]).then_inc(d_store, 16)
                    if b + 2 < NB_DEC:
                        load_values(b + 2)
                sp.wait_ge(d_store, 16 * NB_DEC * (HA + HB))

            def pe_sample(pe):
                pe.wait_ge(s_yc, NPT)
                pe.wait_ge(s_scr, NPT)
                pe.wait_ge(s_Tc, NPT * NTB)
                pe.wait_ge(d_qk, 64)
                for n in range(2):
                    for u in range(KD):
                        m = nc.tensor.transpose(ps[:, n, u * NS:(u + 1) * NS], qk[:, n, u * P:(u + 1) * P], ident[0:NS, 0:NS])
                    m.then_inc(d_qT, 1)
                pe.wait_ge(d_qTc, 2)

                def transpose_keys(b):
                    pe.wait_ge(d_page, 64 * (b + 1))
                    for g in range(PAGES):
                        for j in range(2):
                            bank = 2 * g + j
                            if b:
                                pe.wait_ge(d_kTc, 5 * (b - 1) + bank + 1)
                            for k in range(4):
                                u = 4 * j + k
                                m = nc.tensor.transpose(ps[:, bank, k * P:(k + 1) * P],
                                                        kpage[:, g, u * P:(u + 1) * P], ident[:])
                            m.then_inc(d_kT, 1)

                def scores(b):
                    pe.wait_ge(d_kTc, 5 * (b + 1))
                    pe.wait_ge(d_blk, 2 * (b + 1))
                    if b:
                        pe.wait_ge(d_Sr, b)
                    for u in range(KD):
                        m = nc.tensor.matmul(ps[:, 4, 0:KS], qblk_flat[:, u * P:(u + 1) * P], kT[:, u, :],
                                             start=(u == 0), stop=(u == KD - 1))
                    m.then_inc(d_S, 1)

                transpose_keys(0)
                scores(0)
                transpose_keys(1)
                for b in range(NB_DEC):
                    pe.wait_ge(d_prob, 2 * (b + 1))
                    if b:
                        pe.wait_ge(d_Tc, b)
                    for c, kc in enumerate(KC):
                        m = nc.tensor.transpose(ps[0:kc, 5, c * P:(c + 1) * P], dec_prob[:, c * P:c * P + kc], ident[:])
                    m.then_inc(d_T, 1)
                    if b + 1 < NB_DEC:
                        scores(b + 1)
                    pe.wait_ge(d_pd, b + 1)
                    pe.wait_ge(d_val[b % 2], 96 * (b // 2 + 1))
                    if b:
                        pe.wait_ge(d_Oc, 2 * b)
                    for c, kc in enumerate(KC):
                        v = vpage[:, b % 2, c, :] if c < PAGES else vnew[:, b % 2, :]
                        nc.tensor.matmul(ps[0:HA * TD, 6, :], pd[0:kc, c, :], v[0:kc, 0:CH], start=(c == 0), stop=(c == 2))
                    for c, kc in enumerate(KC):
                        v = vpage[:, b % 2, c, :] if c < PAGES else vnew[:, b % 2, :]
                        m = nc.tensor.matmul(ps[0:HB * TD, 7, :], pT[0:kc, c, 64:P], v[0:kc, CH:D], start=(c == 0), stop=(c == 2))
                    m.then_inc(d_O, 1)
                    if b + 2 < NB_DEC:
                        transpose_keys(b + 2)
                pe.wait_ge(d_kTc, 5 * NB_DEC)

            def act_sample(act):
                act.wait_ge(d_qT, 1)
                nc.scalar.activation(qT[:], ps[:, 0, :].rearrange("p (u r) -> p u r", r=NS), ACT.Copy, scale=0.125).then_inc(d_qTc, 1)
                act.wait_ge(d_qT, 2)
                nc.scalar.copy(knT[:], ps[:, 1, :].rearrange("p (u r) -> p u r", r=NS)).then_inc(d_qTc, 1)
                act.wait_ge(d_qTc, 2)

                def take_keys(b):
                    if b:
                        act.wait_ge(d_S, b)
                    for g in range(PAGES):
                        for j in range(2):
                            act.wait_ge(d_kT, 4 * b + 2 * g + j + 1)
                            nc.scalar.copy(kT[:, 4 * j:4 * j + 4, g * P:(g + 1) * P],
                                           ps[:, 2 * g + j, :].rearrange("p (u r) -> p u r", r=P)).then_inc(d_kTc, 1)
                    nc.scalar.copy(kT[:, :, PAST:KS], knT[:, :, b * TD:(b + 1) * TD]).then_inc(d_kTc, 1)

                take_keys(0)
                for b in range(NB_DEC):
                    act.wait_ge(d_Sr, b + 1)
                    nc.scalar.activation(dec_exp[B], dec_scores[B], ACT.Abs).then_inc(d_act, 1)
                    act.wait_ge(d_act, 4 * b + 1)
                    nc.scalar.activation(dec_exp[B], dec_exp[B], ACT.Exp, scale=-1.0).then_inc(d_act, 1)
                    act.wait_ge(d_dve, 7 * b + 2)
                    nc.scalar.activation(dec_exp[A], dec_scores[A], ACT.Exp, bias=dec_nm[A, :], accum_out=dec_l[A, :]).then_inc(d_act, 1)
                    act.wait_ge(d_act, 4 * b + 3)
                    nc.scalar.activation(dec_exp[B], dec_exp[B], ACT.Ln, bias=one_t[B, :]).then_inc(d_act, 1)
                    if b + 1 < NB_DEC:
                        take_keys(b + 1)
                    act.wait_ge(d_dve, 7 * b + 7)
                    nc.scalar.activation(dec_prob[B], dec_scores[B], ACT.Exp).then_inc(d_prob, 1)
                    act.wait_ge(d_T, b + 1)
                    nc.scalar.copy(pT[:, 0:2, :], ps[:, 5, 0:2 * P].rearrange("p (c r) -> p c r", r=P)).then_inc(d_Tc, 1)

            def dve_sample(dve, stepno):
                def place_queries(b):
                    if b:
                        dve.wait_ge(d_S, b)
                    for half in range(2):
                        rows = slice(64 * half, 64 * half + 64)
                        nc.vector.tensor_copy(qblk[rows, :, half * TD:(half + 1) * TD],
                                              qT[rows, :, b * TD:(b + 1) * TD]).then_inc(d_blk, 1)

                def take_scores(b):
                    dve.wait_ge(d_S, b + 1)
                    if b:
                        dve.wait_ge(d_prob, 2 * b)
                    nc.vector.tensor_tensor(dec_scores, ps[:, 4, 0:KS], dec_mask, ALU.add).then_inc(d_Sr, 1)
                    dve.wait_ge(d_Sr, b + 1)
                    nc.vector.reduce_max(dec_mx[A, :], dec_scores[A], AX).then_inc(d_dve, 1)
                    dve.wait_ge(d_dve, 7 * b + 1)
                    nc.vector.tensor_scalar_mul(dec_nm[A, :], dec_mx[A, :], -1.0).then_inc(d_dve, 1)

                def make_probabilities(b):
                    dve.wait_ge(d_act, 4 * b + 4)
                    nc.vector.reciprocal(dec_rl[A, :], dec_l[A, :]).then_inc(d_dve, 1)
                    nc.vector.scalar_tensor_tensor(out=dec_exp[B], in0=dec_scores[B], scalar=0.0, in1=dec_exp[B], op0=ALU.max, op1=ALU.add).then_inc(d_dve, 1)
                    dve.wait_ge(d_dve, 7 * b + 4)
                    if b:
                        dve.wait_ge(d_T, b)
                    nc.vector.tensor_scalar_mul(dec_prob[A], dec_exp[A], dec_rl[A, :]).then_inc(d_prob, 1)
                    nc.vector.tensor_tensor_scan(out=dec_prob[B, ::-1], data0=dec_exp[B, ::-1], data1=dec_exp[B, ::-1], initial=0.0,
                                                 op0=ALU.add, op1=ALU.bypass).then_inc(d_dve, 1)
                    dve.wait_ge(d_dve, 7 * b + 5)
                    nc.vector.tensor_tensor(dec_scores[B], dec_scores[B], dec_prob[B], ALU.subtract).then_inc(d_dve, 2)

                def join_maps(b):
                    dve.wait_ge(d_Tc, b + 1)
                    nc.vector.tensor_copy(pT[0:TD, 2, :], ps[0:TD, 5, 2 * P:3 * P]).then_inc(d_new, 1)
                    dve.wait_ge(d_new, b + 1)
                    for c, kc in enumerate(KC):
                        two = pT[0:kc, c, 0:64].rearrange("p (h m q) -> p h m q", m=2, q=TD)
                        m = nc.vector.scalar_tensor_tensor(out=pd[0:kc, c, :].rearrange("p (h q) -> p h q", q=TD),
                                                           in0=two[:, :, 1, :], scalar=neg_lam[0:kc, :],
                                                           in1=two[:, :, 0, :], op0=ALU.mult, op1=ALU.add)
                    m.then_inc(d_pd, 1)

                def take_o(b):
                    dve.wait_ge(d_O, b + 1)
                    if b:
                        dve.wait_ge(d_store, 16 * b * (HA + HB))
                    nc.vector.tensor_copy(oa, ps[0:HA * TD, 6, :]).then_inc(d_Oc, 1)
                    nc.vector.tensor_copy(ob, ps[0:HB * TD, 7, :]).then_inc(d_Oc, 1)

                b, second = (stepno - 1) // 2, (stepno - 1) % 2
                if stepno == 0:
                    dve.wait_ge(s_Oc, NPT * 2)
                    nc.vector.memset(qblk_flat, 0.0).then_inc(d_zero, 1)
                    dve.wait_ge(d_qTc, 1)
                    dve.wait_ge(d_zero, 1)
                    place_queries(0)
                    dve.wait_ge(d_mask, 16 * (2 * HA + HB))
                elif second == 0:
                    if b >= 1:
                        join_maps(b - 1)
                    if b < NB_DEC:
                        take_scores(b)
                        if b + 1 < NB_DEC:
                            place_queries(b + 1)
                else:
                    if b >= 1:
                        take_o(b - 1)
                    if b < NB_DEC:
                        make_probabilities(b)

            PIECES = ("norm_o", "scale_o", "turn_o", "branch_a", "branch_b", "mix", "turn_m", "out_1", "out_2", "residual",
                      "norm_x", "turn_x", "query_1", "query_2", "turn_q", "score", "key_1", "key_2", "key_3", "key_4", "key_5",
                      "pair_1", "pair_2", "pair_3", "pair_4", "pair_5", "pair_6", "gate", "pick_1", "pick_2", "choose", "")

            def tiles_of(eng, step):
                step(0, 2 * P)
                for first, last in ((1, 4), (4, 6), (6, 8)):
                    with eng.Fori(first, last) as t:
                        step(t, last * P)
                step(NPT, None)
                step(NPT + 1, None)

            def before(t):
                return None if isinstance(t, int) and t == 0 else t - 1

            def mixes(t):
                return not (isinstance(t, int) and t > NPT)

            with nc.Block() as block:
                @block.sync
                def _(sp):
                    def step(t, kw):
                        if kw:
                            sync_attend(sp, t, kw)
                        elif mixes(t):
                            sync_sample(sp)
                        if mixes(t):
                            sync_merge(sp, t)
                        if isinstance(t, int) and t == 0:
                            for group, (r0, r1) in zip(kv_out, ((0, SEQ), (SEQ, T))):
                                for dst, c0 in zip(group, (KA, VA, KB, VB)):
                                    sp.dma_start(dst, proj_d[r0:r1, c0:c0 + CH]).then_inc(s_out, 16)
                        if before(t) is not None:
                            sync_finish(sp, before(t))

                    sp.sem_inc(s_yst, 16)
                    tiles_of(sp, step)
                    sp.wait_ge(s_yst, 16 * (NPT + 2))
                    sp.wait_ge(s_out, 16 * 8)

                @block.gpsimd
                def _(pool):
                    with pool.Fori(0, NPT) as e:
                        pool_experts(pool, e)
                    pool_experts(pool, NPT)

                @block.tensor
                def _(pe):
                    pe.sem_inc(s_sum, len(TSUM))
                    pe.sem_inc(s_vsum, len(VSUM))
                    pe.sem_inc(s_yc, 1)

                    def step(t, kw):
                        if kw:
                            pe_attend(pe, t, kw)
                        elif mixes(t):
                            pe_sample(pe)
                        for k, piece in enumerate(PIECES):
                            if mixes(t):
                                pe_merge(pe, t, piece)
                            if before(t) is not None:
                                pe_experts(pe, before(t), k)

                    tiles_of(pe, step)

                @block.scalar
                def _(act):
                    def step(t, kw):
                        if kw:
                            act_attend(act, t, kw)
                        elif mixes(t):
                            act_sample(act)
                        if before(t) is not None:
                            act_gelu(act, before(t))
                        for k, piece in enumerate(PIECES):
                            if before(t) is not None:
                                act_experts(act, before(t), k)
                            if mixes(t):
                                act_merge(act, t, piece)
                        if before(t) is not None:
                            act_finish(act, before(t))

                    tiles_of(act, step)

                @block.vector
                def _(dve):
                    def step(t, kw):
                        parts = ATT_PARTS if kw else DEC_PARTS
                        for g in range(parts):
                            if before(t) is not None:
                                n_slots = slots_of(before(t))
                                dve_dots(dve, before(t), g * n_slots // parts, (g + 1) * n_slots // parts)
                                if g == parts // 2:
                                    dve_keep_idx(dve, before(t))
                            if kw and ATT_LEAD <= g < ATT_LEAD + 16:
                                dve_attend(dve, t, (g - ATT_LEAD) // 2, (g - ATT_LEAD) % 2, kw)
                            elif not kw and mixes(t) and g < 2 * NB_DEC + 3:
                                dve_sample(dve, g)
                        if before(t) is not None:
                            dve_weights(dve, before(t))
                        for k, piece in enumerate(PIECES):
                            if mixes(t):
                                dve_merge(dve, t, piece)
                            if before(t) is not None:
                                dve_experts(dve, before(t), k)
                        if before(t) is not None:
                            dve_finish(dve, before(t), 0)
                            dve_finish(dve, before(t), 1)

                    nc.vector.tensor_tensor(fold[:], ident[:, 0:NS], ident[:, NS:P], ALU.add).then_inc(s_fold, 1)
                    tiles_of(dve, step)



OUTS = [(1, SEQ, D), (NB_DEC, TD, D),
        (1, 1, SEQ, HA, 128), (1, 1, SEQ, HA, 128), (1, 1, SEQ, HB, 64), (1, 1, SEQ, HB, 64),
        (1, NB_DEC, TD, HA, 128), (1, NB_DEC, TD, HA, 128), (1, NB_DEC, TD, HB, 64), (1, NB_DEC, TD, HB, 64)]


def kernel(**inputs):
    import concourse.bacc as bacc
    from concourse.bass_utils import run_bass_kernel_spmd

    nc = bacc.Bacc("TRN2", target_bir_lowering=False, num_devices=1)
    arrays, args = {}, {}
    given = {name: np.ascontiguousarray(v) for name, v in inputs.items()}
    given["distance_onehot"] = distance_onehot()
    given["mask_rows"] = mask_rows()
    for name, v in given.items():
        arrays[f"in_{name}"] = v
        args[name] = nc.dram_tensor(f"in_{name}", v.shape, mybir.dt.from_np(v.dtype), kind="ExternalInput").ap()
    outs = [nc.dram_tensor(f"out_{n}", shape, F32, kind="ExternalOutput").ap() for n, shape in enumerate(OUTS)]
    build(nc, args, outs)
    r = run_bass_kernel_spmd(nc, [arrays], core_ids=[0])
    return tuple(r.results[0][f"out_{n}"] for n in range(len(OUTS)))
```
